# Optimizing a Trainium2 kernel written in Bass

```python
import jax, jax.numpy as jnp
from jax import lax
import numpy as np

D_MODEL = 1024
BATCH = 1
SEQ = 128
DEPTH = 2
DEC_BATCH = 1
DEC_SEQ = 1024
PAST_LEN = 128

GRID_W = 64
N_EVEN = (DEPTH + 1) // 2
N_ODD = DEPTH // 2
HD = 64
A_HEADS = 8
A_KV = 2
A_W = A_HEADS * HD
B_HEADS = 4
B_DK = 64
B_DV = 128
B_RANK = 16
B_W = B_HEADS * B_DV
GLA_NORMALIZER = 16.0
C_HEADS = 8
C_KV = 2
C_W = C_HEADS * HD
WINDOW = 128
D_HEADS = 4
D_DK = 128
D_DV = 128
D_W = D_HEADS * D_DV
CONV_K = 5
CONV_CH = 2 * D_HEADS * D_DK + D_W
MIX_W = A_W + B_W
Q_BLOCK = 128
CHUNK = 64
ROPE_THETA = 10000.0
ROT_AXIS = HD // 2
EPS = 1e-6
EVEN_SIZES = (A_W, A_KV * HD, A_KV * HD, A_W, B_HEADS * B_DK, B_HEADS * B_DK, B_W, 2 * B_RANK, B_W)
ODD_SIZES = (C_W, C_KV * HD, C_KV * HD, C_W, D_HEADS * D_DK, D_HEADS * D_DK, D_W, 2 * D_HEADS, 2 * D_HEADS, D_W)
PROJ_EVEN = 2 * A_W + 2 * A_KV * HD + 2 * B_HEADS * B_DK + 2 * B_W + 2 * B_RANK
PROJ_ODD = 2 * C_W + 2 * C_KV * HD + 2 * D_HEADS * D_DK + 2 * D_W + 4 * D_HEADS

kernel_name = 'hybrid_flow_backbone_step'

F32 = jnp.float32

def split_cols(z, sizes):
    idx = [int(i) for i in np.cumsum(sizes)[:-1]]
    return jnp.split(z, idx, axis=-1)

def rms_norm(x, w):
    xf = x.astype(F32)
    y = xf * lax.rsqrt(jnp.mean(xf * xf, axis=-1, keepdims=True) + EPS)
    return (y * w.astype(F32)).astype(x.dtype)

def l2_norm(x):
    xf = x.astype(F32)
    return (xf * lax.rsqrt(jnp.sum(xf * xf, axis=-1, keepdims=True) + EPS)).astype(x.dtype)

def flip(x):
    return x[:, ::-1]

def adaln_in(x, cond, w, b, g):
    m = jax.nn.silu(cond) @ w + b
    shift, scale, gate = jnp.split(m[:, None, :], 3, axis=-1)
    return rms_norm(x, g) * (1 + scale) + shift, gate

def rope_tables(T):
    n_rows = T // GRID_W
    rows = jnp.repeat(jnp.arange(n_rows, dtype=F32), GRID_W)
    cols = jnp.tile(jnp.arange(GRID_W, dtype=F32), n_rows)
    inv = jnp.power(ROPE_THETA, jnp.arange(ROT_AXIS // 2, dtype=F32) * (-2.0 / ROT_AXIS))
    ang_r = rows[:, None] * inv[None, :]
    ang_c = cols[:, None] * inv[None, :]
    return (jnp.cos(ang_r), jnp.sin(ang_r), jnp.cos(ang_c), jnp.sin(ang_c))

def rope_1d(x, cos, sin):
    half = x.shape[-1] // 2
    xf = x.astype(F32)
    x1, x2 = xf[..., :half], xf[..., half:]
    cc, ss = cos[None, :, None, :], sin[None, :, None, :]
    return jnp.concatenate([x1 * cc - x2 * ss, x2 * cc + x1 * ss], axis=-1)

def axial_rope(x, tables):
    cr, sr, cc, sc = tables
    out = jnp.concatenate([rope_1d(x[..., :ROT_AXIS], cr, sr), rope_1d(x[..., ROT_AXIS:], cc, sc)], axis=-1)
    return out.astype(x.dtype)

def block_attention(q, k, v, sink=None):
    B, Tq, H, hd = q.shape
    KV = k.shape[2]
    G = H // KV
    nb = Tq // Q_BLOCK
    qb = q.reshape(B, nb, Q_BLOCK, KV, G, hd).swapaxes(0, 1)
    scale = hd ** -0.5

    def one(qblk):
        s = jnp.einsum('bqkgd,bskd->bkgqs', qblk, k).astype(F32) * scale
        if sink is not None:
            sk = jnp.broadcast_to(sink.astype(F32).reshape(KV, G)[None, :, :, None, None], s.shape[:-1] + (1,))
            p = jax.nn.softmax(jnp.concatenate([s, sk], axis=-1), axis=-1)[..., :-1]
        else:
            p = jax.nn.softmax(s, axis=-1)
        return jnp.einsum('bkgqs,bskd->bqkgd', p.astype(v.dtype), v)

    o = lax.map(one, qb)
    return o.swapaxes(0, 1).reshape(B, Tq, H, hd)

def banded_attention(q, k, v, k_ctx, v_ctx, sink):
    B, T, H, hd = q.shape
    KV = k.shape[2]
    G = H // KV
    nb = T // Q_BLOCK
    nl = 3 * Q_BLOCK
    nc = k_ctx.shape[1]
    pad = ((0, 0), (Q_BLOCK, Q_BLOCK), (0, 0), (0, 0))
    k_pad = jnp.pad(k, pad)
    v_pad = jnp.pad(v, pad)
    qb = q.reshape(B, nb, Q_BLOCK, KV, G, hd).swapaxes(0, 1)
    a_idx = jnp.arange(Q_BLOCK)[:, None]
    b_idx = jnp.arange(nl)[None, :]
    dist = Q_BLOCK + a_idx - b_idx
    sink_col = sink.astype(F32).reshape(KV, G)[None, :, :, None, None]
    scale = hd ** -0.5

    def one(args):
        qblk, n = args
        kb = lax.dynamic_slice_in_dim(k_pad, n * Q_BLOCK, nl, axis=1)
        vb = lax.dynamic_slice_in_dim(v_pad, n * Q_BLOCK, nl, axis=1)
        j = n * Q_BLOCK - Q_BLOCK + b_idx
        valid = (jnp.abs(dist) <= WINDOW) & (j >= 0) & (j < T)
        s_loc = jnp.einsum('bqkgd,bskd->bkgqs', qblk, kb).astype(F32) * scale
        s_loc = jnp.where(valid, s_loc, -jnp.inf)
        s_ctx = jnp.einsum('bqkgd,bskd->bkgqs', qblk, k_ctx).astype(F32) * scale
        s = jnp.concatenate([s_loc, s_ctx, jnp.broadcast_to(sink_col, s_loc.shape[:-1] + (1,))], axis=-1)
        p = jax.nn.softmax(s, axis=-1).astype(v.dtype)
        return (jnp.einsum('bkgqs,bskd->bqkgd', p[..., :nl], vb)
                + jnp.einsum('bkgqs,bskd->bqkgd', p[..., nl:nl + nc], v_ctx))

    o = lax.map(one, (qb, jnp.arange(nb)))
    return o.swapaxes(0, 1).reshape(B, T, H, hd)

def gla_chunked(q, k, v, g, s0):
    B, T, H, dk = q.shape
    dv = v.shape[-1]
    N = T // CHUNK
    qc = q.astype(F32).reshape(B, N, CHUNK, H, dk)
    kc = k.astype(F32).reshape(B, N, CHUNK, H, dk)
    vc = v.astype(F32).reshape(B, N, CHUNK, H, dv)
    b = jnp.cumsum(g.astype(F32).reshape(B, N, CHUNK, H, dk), axis=2)
    b_last = b[:, :, -1]
    q_t = qc * jnp.exp(b)
    k_t = kc * jnp.exp(-b)
    k_end = kc * jnp.exp(b_last[:, :, None] - b)
    incl = jnp.tril(jnp.ones((CHUNK, CHUNK), dtype=bool))
    att = jnp.where(incl, jnp.einsum('bnihd,bnjhd->bnhij', q_t, k_t), 0.0)
    o_intra = jnp.einsum('bnhij,bnjhv->bnihv', att, vc)
    u = jnp.einsum('bnjhd,bnjhv->bnhdv', k_end, vc)

    def step(s, inp):
        dec, un = inp
        return dec[..., None] * s + un, s

    s_fin, s_prev = lax.scan(step, s0.astype(F32), (jnp.exp(b_last).swapaxes(0, 1), u.swapaxes(0, 1)))
    o_inter = jnp.einsum('bnihd,bnhdv->bnihv', q_t, s_prev.swapaxes(0, 1))
    o = (o_intra + o_inter).reshape(B, T, H, dv)
    return o.astype(v.dtype), s_fin.astype(v.dtype)

def delta_chunked(q, k, v, g, beta, s0):
    B, T, H, dk = q.shape
    dv = v.shape[-1]
    N = T // CHUNK

    def chunk(x):
        return x.astype(F32).reshape((B, N, CHUNK) + x.shape[2:]).swapaxes(2, 3)

    qc, kc, vc, bc = chunk(q), chunk(k), chunk(v), chunk(beta)
    gc = jnp.cumsum(chunk(g), axis=-1)
    idx = jnp.arange(CHUNK)
    incl = idx[:, None] >= idx[None, :]
    strict = idx[:, None] > idx[None, :]
    decay = jnp.exp(jnp.where(incl, gc[..., :, None] - gc[..., None, :], -jnp.inf))
    kb = kc * bc[..., None]
    t_mat = jnp.where(strict, jnp.einsum('bnhid,bnhjd->bnhij', kb, kc) * decay, 0.0)
    rhs = jnp.concatenate([vc * bc[..., None], kb * jnp.exp(gc)[..., None]], axis=-1)
    sol = lax.linalg.triangular_solve(jnp.eye(CHUNK, dtype=F32) + t_mat, rhs, left_side=True, lower=True)
    u, w = sol[..., :dv], sol[..., dv:]
    att = jnp.einsum('bnhid,bnhjd->bnhij', qc, kc) * decay
    q_dec = qc * jnp.exp(gc)[..., None]
    g_last = gc[..., -1]
    k_dec = kc * jnp.exp(g_last[..., None] - gc)[..., None]

    def step(s, inp):
        u_n, w_n, att_n, qd_n, kd_n, gl_n = inp
        v_new = u_n - jnp.einsum('bhcd,bhdv->bhcv', w_n, s)
        o_n = jnp.einsum('bhcd,bhdv->bhcv', qd_n, s) + jnp.einsum('bhij,bhjv->bhiv', att_n, v_new)
        s = s * jnp.exp(gl_n)[..., None, None] + jnp.einsum('bhcd,bhcv->bhdv', kd_n, v_new)
        return s, o_n

    xs = (u.swapaxes(0, 1), w.swapaxes(0, 1), att.swapaxes(0, 1), q_dec.swapaxes(0, 1),
          k_dec.swapaxes(0, 1), g_last.swapaxes(0, 1))
    s_fin, o = lax.scan(step, s0.astype(F32), xs)
    o = o.transpose(1, 0, 3, 2, 4).reshape(B, T, H, dv)
    return o.astype(v.dtype), s_fin.astype(v.dtype)

def gla_log_gate(r, up, bias):
    B, T = r.shape[:2]
    gk = r @ up + bias
    return jax.nn.log_sigmoid(gk.astype(F32)).reshape(B, T, B_HEADS, B_DK) / GLA_NORMALIZER

def delta_log_decay(a, a_log, dt_bias):
    return -jnp.exp(a_log.astype(F32)) * jax.nn.softplus(a.astype(F32) + dt_bias.astype(F32))

def short_conv(x, w):
    y = lax.conv_general_dilated(x, w[:, None, :].astype(x.dtype), window_strides=(1,),
                                 padding=[(CONV_K // 2, CONV_K // 2)],
                                 dimension_numbers=('NWC', 'WIO', 'NWC'), feature_group_count=x.shape[-1])
    return jax.nn.silu(y)

def even_mixer(h, w_in, w_out, qn, kn, gk_up, gk_bias, onorm, rope=None, ctx=None):
    B, T, _ = h.shape
    a_q, a_k, a_v, a_g, b_q, b_k, b_v, b_r, b_g = split_cols(h @ w_in, EVEN_SIZES)
    q = rms_norm(a_q.reshape(B, T, A_HEADS, HD), qn)
    k = rms_norm(a_k.reshape(B, T, A_KV, HD), kn)
    v = a_v.reshape(B, T, A_KV, HD)
    if ctx is None:
        o_a = block_attention(q, k, v)
    else:
        k_ctx, v_ctx, s_ctx = ctx
        o_a = block_attention(axial_rope(q, rope),
                              jnp.concatenate([axial_rope(k, rope), k_ctx], axis=1),
                              jnp.concatenate([v, v_ctx], axis=1))
    y_a = o_a.reshape(B, T, A_W) * jax.nn.silu(a_g)
    qg = b_q.reshape(B, T, B_HEADS, B_DK) * (B_DK ** -0.5)
    kg = b_k.reshape(B, T, B_HEADS, B_DK)
    vg = b_v.reshape(B, T, B_HEADS, B_DV)
    r_f, r_b = jnp.split(b_r, 2, axis=-1)
    g_f = gla_log_gate(r_f, gk_up[0], gk_bias[0])
    g_b = gla_log_gate(r_b, gk_up[1], gk_bias[1])
    if ctx is None:
        s0_f = s0_b = jnp.zeros((B, B_HEADS, B_DK, B_DV), h.dtype)
    else:
        s0_f, s0_b = s_ctx[:, 0], s_ctx[:, 1]
    o_f, s_f = gla_chunked(qg, kg, vg, g_f, s0_f)
    o_b, s_b = gla_chunked(flip(qg), flip(kg), flip(vg), flip(g_b), s0_b)
    y_b = rms_norm(o_f + flip(o_b), onorm).reshape(B, T, B_W) * jax.nn.silu(b_g)
    out = jnp.concatenate([y_a, y_b], axis=-1) @ w_out
    if ctx is None:
        return out, (k, v, jnp.stack([s_f, s_b], axis=1))
    return out

def odd_mixer(h, w_in, w_out, sink, conv_w, a_log, dt_bias, onorm, rope=None, ctx=None):
    B, T, _ = h.shape
    c_q, c_k, c_v, c_g, d_q, d_k, d_v, d_a, d_b, d_g = split_cols(h @ w_in, ODD_SIZES)
    q = c_q.reshape(B, T, C_HEADS, HD)
    k = c_k.reshape(B, T, C_KV, HD)
    v = c_v.reshape(B, T, C_KV, HD)
    if ctx is None:
        o_c = block_attention(q, k, v, sink)
    else:
        k_ctx, v_ctx, s_ctx = ctx
        o_c = banded_attention(axial_rope(q, rope), axial_rope(k, rope), v, k_ctx, v_ctx, sink)
    y_c = o_c.reshape(B, T, C_W) * jax.nn.silu(c_g)
    qkv = short_conv(jnp.concatenate([d_q, d_k, d_v], axis=-1), conv_w)
    qd, kd, vd = split_cols(qkv, (D_HEADS * D_DK, D_HEADS * D_DK, D_W))
    qd = l2_norm(qd.reshape(B, T, D_HEADS, D_DK)) * (D_DK ** -0.5)
    kd = l2_norm(kd.reshape(B, T, D_HEADS, D_DK))
    vd = vd.reshape(B, T, D_HEADS, D_DV)
    a_f, a_b = jnp.split(d_a, 2, axis=-1)
    b_f, b_b = jnp.split(d_b, 2, axis=-1)
    g_f = delta_log_decay(a_f, a_log[0], dt_bias[0])
    g_b = delta_log_decay(a_b, a_log[1], dt_bias[1])
    beta_f = jax.nn.sigmoid(b_f.astype(F32))
    beta_b = jax.nn.sigmoid(b_b.astype(F32))
    if ctx is None:
        s0_f = s0_b = jnp.zeros((B, D_HEADS, D_DK, D_DV), h.dtype)
    else:
        s0_f, s0_b = s_ctx[:, 0], s_ctx[:, 1]
    o_f, s_f = delta_chunked(qd, kd, vd, g_f, beta_f, s0_f)
    o_b, s_b = delta_chunked(flip(qd), flip(kd), flip(vd), flip(g_b), flip(beta_b), s0_b)
    y_d = rms_norm(o_f + flip(o_b), onorm).reshape(B, T, D_W) * jax.nn.silu(d_g)
    out = jnp.concatenate([y_c, y_d], axis=-1) @ w_out
    if ctx is None:
        return out, (k, v, jnp.stack([s_f, s_b], axis=1))
    return out

def setup_inputs(seed: int = 0) -> dict:
    key = jax.random.key(seed)
    ks = jax.random.split(key, 32)

    def nrm(k, shape, scale):
        return jax.random.normal(k, shape, F32) * scale

    u_a = jax.random.uniform(ks[27], (N_ODD, 2, D_HEADS), F32, 1.0, 16.0)
    dt = jnp.exp(jax.random.uniform(ks[28], (N_ODD, 2, D_HEADS), F32, np.log(1e-3), np.log(1e-1)))
    return {
        'x_prompt': nrm(ks[0], (BATCH, SEQ, D_MODEL), 1.0),
        'x_sample': nrm(ks[1], (DEC_BATCH, DEC_SEQ, D_MODEL), 1.0),
        'c': nrm(ks[2], (DEC_BATCH, D_MODEL), 1.0),
        'cache_attn_k': nrm(ks[3], (DEC_BATCH, N_EVEN, PAST_LEN, A_KV, HD), 1.0),
        'cache_attn_v': nrm(ks[4], (DEC_BATCH, N_EVEN, PAST_LEN, A_KV, HD), 1.0),
        'state_gla': nrm(ks[5], (DEC_BATCH, N_EVEN, 2, B_HEADS, B_DK, B_DV), 0.3),
        'cache_swa_k': nrm(ks[6], (DEC_BATCH, N_ODD, PAST_LEN, C_KV, HD), 1.0),
        'cache_swa_v': nrm(ks[7], (DEC_BATCH, N_ODD, PAST_LEN, C_KV, HD), 1.0),
        'state_delta': nrm(ks[8], (DEC_BATCH, N_ODD, 2, D_HEADS, D_DK, D_DV), 0.3),
        'c_ctx': nrm(ks[9], (D_MODEL,), 1.0),
        'w_mod': nrm(ks[10], (DEPTH, D_MODEL, 3 * D_MODEL), 0.5 * D_MODEL ** -0.5),
        'b_mod': nrm(ks[11], (DEPTH, 3 * D_MODEL), 0.02),
        'g_pre': 1.0 + nrm(ks[12], (DEPTH, D_MODEL), 0.02),
        'g_post': 1.0 + nrm(ks[13], (DEPTH, D_MODEL), 0.02),
        'w_in_even': nrm(ks[14], (N_EVEN, D_MODEL, PROJ_EVEN), D_MODEL ** -0.5),
        'w_out_even': nrm(ks[15], (N_EVEN, MIX_W, D_MODEL), MIX_W ** -0.5),
        'qnorm_a': 1.0 + nrm(ks[16], (N_EVEN, HD), 0.02),
        'knorm_a': 1.0 + nrm(ks[17], (N_EVEN, HD), 0.02),
        'gla_gk_up': nrm(ks[18], (N_EVEN, 2, B_RANK, B_HEADS * B_DK), B_RANK ** -0.5),
        'gla_gk_bias': nrm(ks[19], (N_EVEN, 2, B_HEADS * B_DK), 0.1),
        'gla_onorm': 1.0 + nrm(ks[20], (N_EVEN, B_DV), 0.02),
        'w_in_odd': nrm(ks[21], (N_ODD, D_MODEL, PROJ_ODD), D_MODEL ** -0.5),
        'w_out_odd': nrm(ks[22], (N_ODD, MIX_W, D_MODEL), MIX_W ** -0.5),
        'sink_c': nrm(ks[23], (N_ODD, C_HEADS), 0.5),
        'conv_d': nrm(ks[24], (N_ODD, CONV_K, CONV_CH), CONV_K ** -0.5),
        'a_log_d': jnp.log(u_a),
        'dt_bias_d': dt + jnp.log(-jnp.expm1(-dt)),
        'delta_onorm': 1.0 + nrm(ks[25], (N_ODD, D_DV), 0.02),
    }

def reference(x_prompt, x_sample, c, cache_attn_k, cache_attn_v, state_gla, cache_swa_k, cache_swa_v,
              state_delta, c_ctx, w_mod, b_mod, g_pre, g_post, w_in_even, w_out_even, qnorm_a, knorm_a,
              gla_gk_up, gla_gk_bias, gla_onorm, w_in_odd, w_out_odd, sink_c, conv_d, a_log_d, dt_bias_d,
              delta_onorm):
    rope = rope_tables(x_sample.shape[1])
    y_p, y_s = x_prompt, x_sample
    attn_k, attn_v, gla_s, swa_k, swa_v, delta_s = [], [], [], [], [], []
    for l in range(DEPTH):
        i = l // 2
        h_p, gate_p = adaln_in(y_p, c_ctx[None, :], w_mod[l], b_mod[l], g_pre[l])
        h_s, gate_s = adaln_in(y_s, c, w_mod[l], b_mod[l], g_pre[l])
        if l % 2 == 0:
            prm = (w_in_even[i], w_out_even[i], qnorm_a[i], knorm_a[i], gla_gk_up[i], gla_gk_bias[i], gla_onorm[i])
            out_p, (k_c, v_c, s_c) = even_mixer(h_p, *prm)
            out_s = even_mixer(h_s, *prm, rope=rope,
                               ctx=(cache_attn_k[:, i], cache_attn_v[:, i], state_gla[:, i]))
            attn_k.append(k_c)
            attn_v.append(v_c)
            gla_s.append(s_c)
        else:
            prm = (w_in_odd[i], w_out_odd[i], sink_c[i], conv_d[i], a_log_d[i], dt_bias_d[i], delta_onorm[i])
            out_p, (k_c, v_c, s_c) = odd_mixer(h_p, *prm)
            out_s = odd_mixer(h_s, *prm, rope=rope,
                              ctx=(cache_swa_k[:, i], cache_swa_v[:, i], state_delta[:, i]))
            swa_k.append(k_c)
            swa_v.append(v_c)
            delta_s.append(s_c)
        y_p = y_p + gate_p * rms_norm(out_p, g_post[l])
        y_s = y_s + gate_s * rms_norm(out_s, g_post[l])
    new_attn_k = jnp.stack(attn_k, axis=1)
    new_attn_v = jnp.stack(attn_v, axis=1)
    new_gla_state = jnp.stack(gla_s, axis=1)
    new_swa_k = jnp.stack(swa_k, axis=1)
    new_swa_v = jnp.stack(swa_v, axis=1)
    new_delta_state = jnp.stack(delta_s, axis=1)
    return (y_p, y_s, new_attn_k, new_attn_v, new_gla_state, new_swa_k, new_swa_v, new_delta_state)


_drawn_inputs = setup_inputs


def setup_inputs(seed=0):
    import zlib

    import numpy as np

    out = dict(_drawn_inputs(seed))
    spreads = {}
    factors = {'cache_attn_k': 8.0,
     'cache_attn_v': 8.0,
     'state_gla': 8.0,
     'cache_swa_k': 4.059,
     'cache_swa_v': 3.539,
     'g_post': 6.094,
     'qnorm_a': 8.0,
     'knorm_a': 8.196,
     'gla_onorm': 7.135,
     'sink_c': 33.698,
     'delta_onorm': 33.926}
    for name, (base, spread) in spreads.items():
        noise = np.random.default_rng([zlib.crc32(name.encode()), seed]).standard_normal(out[name].shape)
        drawn = base * np.exp(spread * noise) if base else spread * noise
        out[name] = __import__('jax').numpy.asarray(drawn.astype(out[name].dtype))
    for name, factor in factors.items():
        out[name] = (out[name] * factor).astype(out[name].dtype)
    return out
```

```python
from contextlib import ExitStack

import numpy as np

import concourse.bass as bass
from concourse import mybir

F32 = mybir.dt.float32
ALU = mybir.AluOpType
ACT = mybir.ActivationFunctionType
AX = mybir.AxisListType

P = 128
D = 1024
KD = D // P
T_S = 1024
T_P = 128
NS = T_S // P
NT = NS + 1
T = T_S + T_P
HD = 64
CH = 64
QW = 512
EPS = 1e-6
BIG = 1e30
DV = 128
NLEV = 6
CTX = NS
PROMPT_KEYS = NS + 1
SLOT = 544
RING = 2

E_Q, E_K, E_V, E_G, E_BQ, E_BV, E_BG = 0, 512, 640, 768, 1280, 1792, 2336
O_Q, O_K, O_V, O_G, O_DQ, O_DK, O_DV, O_AB, O_DG = 0, 512, 640, 768, 1280, 1792, 2304, 2816, 2832


def constant_tables():
    a = np.arange(P)
    row, col = a[:, None], a[None, :]
    same = row // CH == col // CH
    parts, at = [], {}

    def put(name, m):
        at[name] = (sum(x.shape[1] for x in parts), m.shape[1])
        parts.append(m.astype(np.float32))

    put("ident", row == col)
    put("ones", np.ones((P, P)))
    put("upto", np.concatenate([(row <= col) & same, (row >= col) & same], 1))
    put("beyond", np.concatenate([(row > col) & same, (row < col) & same], 1))
    put("inchunk", np.concatenate([(row // CH == c) & (col >= 0) for c in range(2)], 1))
    put("strict", np.concatenate([np.where((row > col) & same, 0, BIG), np.where((row < col) & same, 0, BIG)], 1))
    put("incl", np.concatenate([np.where((row <= col) & same, 0, -BIG), np.where((row >= col) & same, 0, -BIG)], 1))
    for k in range(NLEV):
        s = 2 ** k
        pair = row // (2 * s) == col // (2 * s)
        low = (row // s % 2 == 0) & (col // s % 2 == 1) & pair
        put(f"level{k}", np.concatenate([low, low.T], 1))
    prev, nxt = np.where(col >= row, 0, -BIG), np.where(col <= row, 0, -BIG)
    zero = np.zeros((P, P))
    put("window", np.concatenate([prev, zero, zero, nxt], 1))
    put("chunkcol", np.stack([a // CH == c for c in range(2)], 1))
    sel = np.zeros((P, 2 * P))
    sel[0, :P] = 1
    sel[1, P:] = 1
    put("sel", sel)
    tok = np.arange(T_S)
    inv = np.power(np.float32(10000.0), np.arange(16, dtype=np.float32) * np.float32(-2.0 / 32)).astype(np.float32)
    cos, sin = [], []
    for pos in (tok // 64, tok % 64):
        ang = pos.astype(np.float32)[:, None] * inv[None, :]
        cos += [np.cos(ang), np.cos(ang)]
        sin += [-np.sin(ang), np.sin(ang)]
    for name, m in (("cos", cos), ("sin", sin)):
        m = np.concatenate(m, 1).reshape(NS, P, HD).transpose(1, 0, 2).reshape(P, NS * HD)
        put(name, m)
    return np.concatenate(parts, 1), at


CONSTS, CONST_AT = constant_tables()
NCONST = CONSTS.shape[1]


def backbone(nc, x_prompt, x_sample, c, cache_attn_k, cache_attn_v, state_gla, cache_swa_k, cache_swa_v,
             state_delta, c_ctx, w_mod, b_mod, g_pre, g_post, w_in_even, w_out_even, qnorm_a, knorm_a,
             gla_gk_up, gla_gk_bias, gla_onorm, w_in_odd, w_out_odd, sink_c, conv_d, a_log_d, dt_bias_d,
             delta_onorm, consts, y_prompt, y_sample, new_attn_k, new_attn_v, new_gla_state, new_swa_k,
             new_swa_v, new_delta_state):
    ctx = ExitStack()
    with ctx:
        def sb(name, *shape):
            return ctx.enter_context(nc.sbuf_tensor(name, [P, *shape], F32))

        def sem(name):
            return ctx.enter_context(nc.semaphore(name))

        con = sb("con", NCONST)
        hT = sb("hT", KD, T)
        wring = sb("wring", RING, KD * SLOT)
        gg = sb("gg", 2, D)
        mods = sb("mods", 3, KD, 2)
        vecs = sb("vecs", 128)
        vecsT = sb("vecsT", 128)
        sc = sb("sc", 16)
        small = sb("small", 8)
        WORK = (nc.sbuf_bytes_remaining - 1024) // 4
        work = sb("work", WORK)
        ps = ctx.enter_context(nc.psum_tensor("ps", [P, 8, 512], F32))
        y_dram = nc.dram_tensor("y_mixed", (T, D), F32, kind="Internal").ap()

        class Region:
            def __init__(self, at=0):
                self.at = at

            def take(self, n):
                a = self.at
                self.at += n
                assert self.at <= WORK, (self.at, WORK)
                return work[:, a:self.at]

        def cst(name, i=0, n=None):
            o, w = CONST_AT[name]
            n = w if n is None else n
            return con[:, o + i * n:o + (i + 1) * n]

        ident, ones = cst("ident"), cst("ones")

        def wslot(i, n):
            return wring[:, i % RING, 0:KD * n].rearrange("p (k n) -> p k n", n=n)

        S = {}

        def sm(name):
            if name not in S:
                S[name] = sem(name)
            return S[name]

        phase_no = {}

        def phase_end(eng):
            n = phase_no.get(id(eng), 0) + 1
            phase_no[id(eng)] = n
            eng.drain().then_inc(sm("phase"), 1)
            eng.wait_ge(sm("phase"), 3 * n)

        def phase_seen(sp, n):
            if n:
                sp.wait_ge(sm("phase"), 3 * n)

        chunks = []
        for l, (w_in, w_out) in enumerate(((w_in_even, w_out_even), (w_in_odd, w_out_odd))):
            def cols(w, a, b):
                return [w[:, a:b].rearrange("(k p) n -> p k n", p=P)]
            chunks += [(f"mod{l}.{j}", cols(w_mod[l], 512 * j, 512 * j + 512), 512) for j in range(6)]
            w = w_in[0]
            if l == 0:
                chunks += [("q0", cols(w, E_Q, E_K), 512), ("kv0", cols(w, E_K, E_G), 256),
                           ("ga0", cols(w, E_G, E_BQ), 512), ("bqk", cols(w, E_BQ, E_BV), 512),
                           ("bvr", cols(w, E_BV, E_BG), 544), ("gb0", cols(w, E_BG, E_BG + 512), 512)]
            else:
                chunks += [("q1", cols(w, O_Q, O_K), 512), ("kv1", cols(w, O_K, O_G), 256),
                           ("ga1", cols(w, O_G, O_DQ), 512), ("ab", cols(w, O_AB, O_DG), 16)]
                for h in range(4):
                    chunks.append((f"dh{h}", cols(w, O_DQ + 128 * h, O_DQ + 128 * h + 128)
                                   + cols(w, O_DK + 128 * h, O_DK + 128 * h + 128)
                                   + cols(w, O_DV + 128 * h, O_DV + 128 * h + 128), 384))
                chunks += [("gb1", cols(w, O_DG, O_DG + 512), 512)]
            chunks += [(f"out{l}.{j}", cols(w_out[0], 512 * j, 512 * j + 512), 512) for j in range(2)]
        chunk_no = {name: i for i, (name, _, _) in enumerate(chunks)}
        chunk_parts = [len(p) for _, p, _ in chunks]

        def weights(pe, name):
            i = chunk_no[name]
            n = sum(chunk_parts[j] for j in range(i % RING, i + 1, RING))
            pe.wait_ge(sm(f"w_loaded{i % RING}"), 16 * n)
            return wslot(i, chunks[i][2])

        gpost_b = Region().take(D)
        gb2 = Region(D).take(D)
        grow = Region(2 * D).take(D)

        def mod_sp(sp, l, n):
            phase_seen(sp, n)
            d = sm("vec_loaded")
            sp.dma_start(vecs[0:24, :], b_mod[l].rearrange("(r p) -> r p", p=P)).then_inc(d, 16)
            sp.dma_start(vecs[24:32, :], g_pre[l].rearrange("(r p) -> r p", p=P)).then_inc(d, 16)
            sp.dma_start(vecs[32:40, :], c[0].rearrange("(r p) -> r p", p=P)).then_inc(d, 16)
            sp.dma_start(vecs[40:48, :], c_ctx.rearrange("(r p) -> r p", p=P)).then_inc(d, 16)
            sp.dma_start(gpost_b, g_post[l].partition_broadcast(P)).then_inc(d, 16)
            sp.dma_start(gb2[0:2, :], b_mod[l, 2 * D:].partition_broadcast(2)).then_inc(d, 16)

        def mod_pe(pe, l):
            pe.wait_ge(sm("vec_loaded"), 96 * (l + 1))
            pe.transpose(ps[:, 0, 0:48], vecs[0:48, :], ident[0:48, 0:48]).then_inc(sm("vecT_ps"), 1)
            pe.wait_ge(sm("cond_silu"), l + 1)
            scv = sc[:, :].rearrange("p (c k) -> p k c", c=2)
            for j in range(4):
                w = weights(pe, f"mod{l}.{j}")
                for b in range(4):
                    o = (4 * j + b) * 2
                    for k in range(KD):
                        mm = pe.matmul(ps[:, 1, o:o + 2], w[:, k, b * P:(b + 1) * P], scv[:, k, :],
                                       start=(k == 0), stop=(k == KD - 1))
                mm.then_inc(sm("w_used"), 1)
            for j in range(2):
                w = weights(pe, f"mod{l}.{4 + j}")
                for k in range(KD):
                    mm = pe.matmul(ps[0:2, 2 + j, :], scv[:, k, :], w[:, k, :], start=(k == 0), stop=(k == KD - 1))
                mm.then_inc(sm("w_used"), 1)
            pe.drain().then_inc(sm("mod_ps"), 1)
            pe.wait_ge(sm("gate_rows"), l + 1)
            for cnd in range(2):
                for j in range(2):
                    mm = pe.matmul(ps[:, 4 + 2 * cnd + j, :], cst("sel", cnd, P)[0:2, :],
                                   grow[0:2, j * 512:(j + 1) * 512], start=True, stop=True)
            mm.then_inc(sm("gate_ps"), 1)
            phase_end(pe)

        def mod_act(act, l):
            act.wait_ge(sm("vecT_ps"), l + 1)
            act.activation(vecsT[:, 0:48], ps[:, 0, 0:48], ACT.Copy)
            act.activation(sc[:, :], ps[:, 0, 32:48], ACT.Silu).then_inc(sm("cond_silu"), 1)
            phase_end(act)

        def mod_dve(v, l):
            v.wait_ge(sm("mod_ps"), l + 1)
            v.wait_ge(sm("cond_silu"), l + 1)
            m = ps[:, 1, 0:32].rearrange("p (m k c) -> p m k c", m=2, c=2)
            for i in range(2):
                bias = vecsT[:, 8 * i:8 * i + 8].unsqueeze(2).to_broadcast([P, 8, 2])
                v.tensor_tensor(mods[:, i, :, :], m[:, i], bias, ALU.add)
            v.drain()
            v.tensor_scalar(mods[:, 2, :, :], mods[:, 1, :, :], 1.0, None, ALU.add)
            v.tensor_tensor(grow[0:2, :].rearrange("p (a n) -> p a n", a=2), ps[0:2, 2:4, :],
                            gb2[0:2, :].rearrange("p (a n) -> p a n", a=2), ALU.add).then_inc(sm("gate_rows"), 1)
            v.drain()
            v.tensor_tensor(mods[:, 1, :, :], mods[:, 2, :, :],
                            vecsT[:, 24:32].unsqueeze(2).to_broadcast([P, 8, 2]), ALU.mult)
            v.wait_ge(sm("gate_ps"), l + 1)
            for cnd in range(2):
                v.tensor_tensor(gg[:, cnd, :].rearrange("p (a n) -> p a n", a=2), ps[:, 4 + 2 * cnd:6 + 2 * cnd, :],
                                gpost_b.rearrange("p (a n) -> p a n", a=2), ALU.mult)
            phase_end(v)

        ar = Region()
        a_x = [ar.take(D) for _ in range(2)]
        a_xh = [ar.take(D) for _ in range(2)]
        a_junk = ar.take(D)
        a_st = ar.take(8)

        def x_rows(l, t):
            if l == 0:
                return x_prompt[0] if t == NS else x_sample[0, t * P:(t + 1) * P, :]
            return y_prompt[0] if t == NS else y_sample[0, t * P:(t + 1) * P, :]

        def ada_sp(sp, l, n):
            phase_seen(sp, n)
            if l:
                sp.wait_ge(sm("y_stored"), 16 * NT)
            for t in range(NT):
                if t >= 2:
                    sp.wait_ge(sm("xh_done"), NT * l + t - 1)
                sp.dma_start(a_x[t % 2], x_rows(l, t)).then_inc(sm(f"x_loaded{t % 2}"), 16)

        def x_load_count(l, t):
            per = [(NT + 1) // 2, NT // 2][t % 2]
            return 16 * (per * l + t // 2 + 1)

        def ada_act(act, l):
            for t in range(NT):
                act.wait_ge(sm(f"x_loaded{t % 2}"), x_load_count(l, t))
                if t >= 1:
                    act.wait_ge(sm("xh_done"), NT * l + t)
                act.activation(a_junk, a_x[t % 2], ACT.Square, accum_out=a_st[:, 0:1])
                act.drain()
                act.activation(a_st[:, 1:2], a_st[:, 0:1], ACT.Ln, scale=1.0 / D, bias=eps_col)
                act.drain()
                act.activation(a_st[:, 2:3], a_st[:, 1:2], ACT.Exp, scale=-0.5).then_inc(sm("x_rs"), 1)
                if t >= 1:
                    ada_evac_act(act, l, t - 1)
            ada_evac_act(act, l, NT - 1)
            phase_end(act)

        def ada_evac_act(act, l, t):
            act.wait_ge(sm("xT_ps"), NT * l + t + 1)
            cnd = int(t == NS)
            for k in range(4, KD):
                mm = act.activation(hT[:, k, t * P:(t + 1) * P], ps[:, 2 * (t % 2) + 1, (k - 4) * P:(k - 3) * P],
                                    ACT.Identity, scale=mods[:, 1, k, cnd:cnd + 1], bias=mods[:, 0, k, cnd:cnd + 1])
            mm.then_inc(sm("hT_act"), 1)

        def ada_dve(v, l):
            for t in range(NT):
                v.wait_ge(sm("x_rs"), NT * l + t + 1)
                if t >= 2:
                    v.wait_ge(sm("xT_ps"), NT * l + t - 1)
                v.tensor_scalar(a_xh[t % 2], a_x[t % 2], a_st[:, 2:3], None, ALU.mult).then_inc(sm("xh_done"), 1)
                if t >= 1:
                    ada_evac_dve(v, l, t - 1)
            ada_evac_dve(v, l, NT - 1)
            phase_end(v)

        def ada_evac_dve(v, l, t):
            v.wait_ge(sm("xT_ps"), NT * l + t + 1)
            cnd = int(t == NS)
            for k in range(4):
                mm = v.tensor_scalar(hT[:, k, t * P:(t + 1) * P], ps[:, 2 * (t % 2) + k // 4, (k % 4) * P:(k % 4 + 1) * P],
                                     mods[:, 1, k, cnd:cnd + 1], mods[:, 0, k, cnd:cnd + 1], ALU.mult, ALU.add)
            mm.then_inc(sm("hT_dve"), 1)

        def ada_pe(pe, l):
            for t in range(NT):
                pe.wait_ge(sm("xh_done"), NT * l + t + 1)
                if t >= 2:
                    pe.wait_ge(sm("hT_act"), NT * l + t - 1)
                    pe.wait_ge(sm("hT_dve"), NT * l + t - 1)
                for k in range(KD):
                    mm = pe.transpose(ps[:, 2 * (t % 2) + k // 4, (k % 4) * P:(k % 4 + 1) * P],
                                      a_xh[t % 2][:, k * P:(k + 1) * P], ident)
                mm.then_inc(sm("xT_ps"), 1)
            phase_end(pe)

        qr = Region()
        qT = qr.take(4 * T).rearrange("p (j t) -> p j t", j=4)
        kT = qr.take(10 * P)
        vt = qr.take(10 * P).rearrange("p (t n) -> p t n", n=P)
        oa = qr.take(NT * QW).rearrange("p (t n) -> p t n", n=QW)
        at_qkv = qr.at
        q_sq = qr.take(640)
        q_n = [qr.take(640) for _ in range(2)]
        q_t1 = qr.take(640)
        q_t2 = qr.take(640)
        q_r = [qr.take(640) for _ in range(2)]
        q_st = qr.take(32)
        ck = qr.take(P)
        wqk = qr.take(128)
        ar2 = Region(at_qkv)
        pbuf = [ar2.take(9 * P) for _ in range(2)]
        ptbuf = [ar2.take(9 * P) for _ in range(2)]
        a_nm = [ar2.take(8) for _ in range(2)]
        a_rs = [ar2.take(8) for _ in range(2)]
        a_se = [ar2.take(8) for _ in range(2)]
        a_mx = ar2.take(8)
        a_ri = ar2.take(8)
        ssb = [ar2.take(512) for _ in range(2)]
        sinks = ar2.take(16)

        def heads(ap, g=2):
            return ap.rearrange("p (g j d) -> p g j d", g=g, d=HD)

        def qkv_sp(sp, l, n):
            phase_seen(sp, n)
            d = sm("qkv_in")
            kc, vc = ((cache_attn_k, cache_attn_v), (cache_swa_k, cache_swa_v))[l]
            sp.dma_start(ck, kc[0, 0].rearrange("t g d -> t (g d)")).then_inc(d, 16)
            sp.dma_start(vt[:, CTX, :], vc[0, 0].rearrange("t g d -> t (g d)")).then_inc(d, 16)
            if l == 0:
                sp.dma_start(wqk[:, 0:HD], qnorm_a[0].partition_broadcast(P)).then_inc(d, 16)
                sp.dma_start(wqk[:, HD:2 * HD], knorm_a[0].partition_broadcast(P)).then_inc(d, 16)
            ko, vo = ((new_attn_k, new_attn_v), (new_swa_k, new_swa_v))[l]
            sp.wait_ge(sm("qkr_done"), NT * (l + 1))
            kk = q_r[NS % 2][:, 512:640]
            sp.dma_start(ko[0, 0].rearrange("t g d -> t (g d)"), kk).then_inc(sm("kv_stored"), 16)
            sp.wait_ge(sm("v_done"), NT * (l + 1))
            sp.dma_start(vo[0, 0].rearrange("t g d -> t (g d)"), vt[:, PROMPT_KEYS, :]).then_inc(sm("kv_stored"), 16)
            sp.wait_ge(sm("kv_stored"), 32 * (l + 1))
            sp.sem_inc(sm("phase_sp"), 1)

        def qkv_in_count(l):
            return (64, 96)[l]

        def qkv_pe(pe, l):
            wq, wkv = weights(pe, f"q{l}"), weights(pe, f"kv{l}")
            pe.wait_ge(sm("qkv_in"), qkv_in_count(l))
            for t in range(NT + 1):
                if t < NT:
                    if t >= 2:
                        pe.wait_ge(sm("qk_free"), NT * l + t - 1)
                        pe.wait_ge(sm("v_done"), NT * l + t - 1)
                    for w, b, n in ((wq, 0, 512), (wkv, 1, 256)):
                        for k in range(KD):
                            mm = pe.matmul(ps[:, 2 * (t % 2) + b, 0:n], hT[:, k, t * P:(t + 1) * P], w[:, k, :],
                                           start=(k == 0), stop=(k == KD - 1))
                    mm.then_inc(sm("qkv_ps"), 1)
                    if t == NT - 1:
                        pe.drain().then_inc(sm("w_used"), 2)
                if t == 0:
                    pe.transpose(ps[:, 7, 128:256], ck, ident).then_inc(sm("ckT_ps"), 1)
                if t >= 1:
                    u = t - 1
                    pe.wait_ge(sm("qkr_done"), NT * l + u + 1)
                    if u >= 2:
                        pe.wait_ge(sm("qkT_done"), NT * l + u - 1)
                    if u == 1:
                        pe.wait_ge(sm("ckT_done"), l + 1)
                    r = q_r[u % 2]
                    for j in range(5):
                        mm = pe.transpose(ps[:, 4 + 2 * (u % 2) + j // 4, (j % 4) * P:(j % 4 + 1) * P],
                                          r[:, j * P:(j + 1) * P], ident)
                    mm.then_inc(sm("qkT_ps"), 1)
            phase_end(pe)

        def qkv_act(act, l):
            act.wait_ge(sm("ckT_ps"), l + 1)
            act.activation(kT[:, CTX * P:(CTX + 1) * P], ps[:, 7, 128:256], ACT.Copy).then_inc(sm("ckT_done"), 1)
            for t in range(NT + 1):
                if t < NT:
                    a, b = ps[:, 2 * (t % 2), :], ps[:, 2 * (t % 2) + 1, :]
                    act.wait_ge(sm("qkv_ps"), NT * l + t + 1)
                    if l == 0:
                        if t >= 1:
                            act.wait_ge(sm("qk_ss"), t)
                        act.activation(q_sq[:, 0:512], a, ACT.Square)
                        act.activation(q_sq[:, 512:640], b[:, 0:128], ACT.Square).then_inc(sm("qk_sq"), 1)
                    if l == 1:
                        act.wait_ge(sm("qk_free"), NT * l + t + 1)
                    vdst = PROMPT_KEYS if t == NS else t
                    act.activation(vt[:, vdst, :], b[:, 128:256], ACT.Copy).then_inc(sm("v_done"), 1)
                    if l == 0:
                        act.wait_ge(sm("qk_ss"), t + 1)
                        if t >= 1:
                            act.wait_ge(sm("qk_free"), t)
                        act.activation(q_st[:, 10:20], q_st[:, 0:10], ACT.Ln, scale=1.0 / HD, bias=eps_col)
                        act.drain()
                        act.activation(q_st[:, 20:30], q_st[:, 10:20], ACT.Exp, scale=-0.5).then_inc(sm("qk_rs"), 1)
                if t >= 1:
                    u = t - 1
                    act.wait_ge(sm("qkT_ps"), NT * l + u + 1)
                    kdst = PROMPT_KEYS if u == NS else u
                    bk = 4 + 2 * (u % 2)
                    act.activation(qT[:, :, u * P:(u + 1) * P], ps[:, bk, :].rearrange("p (j t) -> p j t", j=4), ACT.Copy)
                    act.activation(kT[:, kdst * P:(kdst + 1) * P], ps[:, bk + 1, 0:P], ACT.Copy).then_inc(sm("qkT_done"), 1)
            phase_end(act)

        def qkv_dve(v, l):
            v.wait_ge(sm("qkv_in"), qkv_in_count(l))
            for t in range(NT):
                a, b = ps[:, 2 * (t % 2), :], ps[:, 2 * (t % 2) + 1, 0:128]
                n, r = q_n[t % 2], q_r[t % 2]
                if l == 0:
                    v.wait_ge(sm("qk_sq"), t + 1)
                    if t >= 1:
                        v.wait_ge(sm("qk_rs"), t)
                    v.tensor_reduce(q_st[:, 0:10], q_sq.rearrange("p (h d) -> p h d", d=HD), AX.X, ALU.add).then_inc(sm("qk_ss"), 1)
                    v.wait_ge(sm("qk_rs"), t + 1)
                    rsb = q_st[:, 20:30].unsqueeze(2).to_broadcast([P, 10, HD])
                    v.tensor_tensor(q_t1[:, 0:512].rearrange("p (h d) -> p h d", d=HD), a.rearrange("p (h d) -> p h d", d=HD), rsb[:, 0:8, :], ALU.mult)
                    v.tensor_tensor(q_t1[:, 512:640].rearrange("p (h d) -> p h d", d=HD), b.rearrange("p (h d) -> p h d", d=HD), rsb[:, 8:10, :], ALU.mult).then_inc(sm("qk_free"), 1)
                    v.drain()
                    for o, m, w in ((0, 8, wqk[:, 0:HD]), (512, 2, wqk[:, HD:2 * HD])):
                        v.tensor_tensor(n[:, o:o + m * HD].rearrange("p (h d) -> p h d", d=HD),
                                        q_t1[:, o:o + m * HD].rearrange("p (h d) -> p h d", d=HD),
                                        w.unsqueeze(1).to_broadcast([P, m, HD]), ALU.mult)
                    v.drain()
                else:
                    v.wait_ge(sm("qkv_ps"), NT * l + t + 1)
                    v.tensor_copy(n[:, 0:512], a)
                    v.tensor_copy(n[:, 512:640], b).then_inc(sm("qk_free"), 1)
                    v.drain()
                if t >= 2:
                    v.wait_ge(sm("qkT_ps"), NT * l + t - 1)
                rq = r[:, 0:512].rearrange("p (j g d) -> p g j d", g=2, d=HD)
                if t == NS:
                    for g in range(2):
                        v.tensor_copy(rq[:, g], heads(n[:, 0:512])[:, g])
                    v.tensor_copy(r[:, 512:640], n[:, 512:640]).then_inc(sm("qkr_done"), 1)
                else:
                    cosb = cst("cos", t, HD).unsqueeze(1).to_broadcast([P, 10, HD])
                    sinb = cst("sin", t, HD)
                    v.tensor_tensor(q_t1.rearrange("p (h d) -> p h d", d=HD), n.rearrange("p (h d) -> p h d", d=HD), cosb, ALU.mult)
                    nh = n.rearrange("p (h a s f) -> p h a s f", a=2, s=2, f=16)
                    th = q_t2.rearrange("p (h a s f) -> p h a s f", a=2, s=2, f=16)
                    sh = sinb.rearrange("p (a s f) -> p a s f", a=2, s=2)
                    for s in range(2):
                        v.tensor_tensor(th[:, :, :, s, :], nh[:, :, :, 1 - s, :],
                                        sh[:, :, s, :].unsqueeze(1).to_broadcast([P, 10, 2, 16]), ALU.mult)
                    v.drain()
                    for g in range(2):
                        v.tensor_tensor(rq[:, g], heads(q_t1[:, 0:512])[:, g], heads(q_t2[:, 0:512])[:, g], ALU.add)
                    v.tensor_tensor(r[:, 512:640], q_t1[:, 512:640], q_t2[:, 512:640], ALU.add).then_inc(sm("qkr_done"), 1)
            phase_end(v)

        def key_tiles(l, b):
            if b == NS:
                return [PROMPT_KEYS]
            if l == 0:
                return list(range(NS + 1))
            return ([b - 1] if b > 0 else []) + [b, CTX] + ([b + 1] if b < NS - 1 else [])

        UNITS = [(b, j, g) for b in range(NT) for j in range(4) for g in range(2)]
        NU = len(UNITS)

        def att_sp(sp, l, n):
            if l == 1:
                phase_seen(sp, n)
                sp.dma_start(sinks[:, 0:8], sink_c[0].partition_broadcast(P)).then_inc(sm("sink_in"), 16)

        def att_pe(pe, l):
            B0 = NU * l

            def scores(u):
                b, j, g = UNITS[u]
                tiles = key_tiles(l, b)
                if u >= 2:
                    pe.wait_ge(sm("pT_dve"), B0 + u - 1)
                    pe.wait_ge(sm("pT_act"), B0 + u - 1)
                q = qT[g * HD:(g + 1) * HD, j, b * P:(b + 1) * P]
                i = 0
                while i < len(tiles):
                    n = 1
                    while i + n < len(tiles) and tiles[i + n] == tiles[i] + n and (i % 4) + n < 4:
                        n += 1
                    mm = pe.matmul(ps[:, 3 * (u % 2) + i // 4, (i % 4) * P:(i % 4 + n) * P], q,
                                   kT[g * HD:(g + 1) * HD, tiles[i] * P:(tiles[i] + n) * P], start=True, stop=True)
                    i += n
                mm.then_inc(sm("s_ps"), 1)

            def transposes(u):
                b, j, g = UNITS[u]
                pe.wait_ge(sm("p_done"), B0 + u + 1)
                for i in range(len(key_tiles(l, b))):
                    mm = pe.transpose(ps[:, 3 * (u % 2) + i // 4, (i % 4) * P:(i % 4 + 1) * P],
                                      pbuf[u % 2][:, i * P:(i + 1) * P], ident)
                mm.then_inc(sm("pT_ps"), 1)

            def values(u):
                b, j, g = UNITS[u]
                tiles = key_tiles(l, b)
                h = g * 4 + j
                pe.wait_ge(sm("pT_dve"), B0 + u + 1)
                pe.wait_ge(sm("pT_act"), B0 + u + 1)
                if u % 8 == 0 and b >= 2:
                    pe.wait_ge(sm("o_done"), NT * l + b - 1)
                for i, kt in enumerate(tiles):
                    mm = pe.matmul(ps[:, 6 + b % 2, h * HD:(h + 1) * HD], ptbuf[u % 2][:, i * P:(i + 1) * P],
                                   vt[:, kt, g * HD:(g + 1) * HD], start=(i == 0), stop=(i == len(tiles) - 1))
                mm.then_inc(sm("pv_ps"), 1)

            for u in range(NU + 2):
                if u >= 2:
                    values(u - 2)
                if u < NU:
                    scores(u)
                if 1 <= u <= NU:
                    transposes(u - 1)
            phase_end(pe)

        def att_dve(v, l):
            B0 = NU * l
            if l == 1:
                v.wait_ge(sm("sink_in"), 16)
                v.tensor_scalar(sinks[:, 8:16], sinks[:, 0:8], -1.0, None, ALU.mult)
                v.drain()

            def evac(u):
                b, j, g = UNITS[u]
                n = min(len(key_tiles(l, b)), 4) * P
                v.wait_ge(sm("pT_ps"), B0 + u + 1)
                if u >= 2:
                    v.wait_ge(sm("pv_ps"), B0 + u - 1)
                v.tensor_copy(ptbuf[u % 2][:, 0:n], ps[:, 3 * (u % 2), 0:n]).then_inc(sm("pT_dve"), 1)

            def block_out(b):
                v.wait_ge(sm("pv_ps"), B0 + 8 * b + 8)
                if l == 1:
                    v.tensor_tensor(a_rs[b % 2], a_rs[b % 2], a_se[b % 2], ALU.add)
                    v.drain()
                v.reciprocal(a_ri, a_rs[b % 2])
                v.drain()
                v.tensor_tensor(oa[:, b, :].rearrange("p (h d) -> p h d", d=HD),
                                ps[:, 6 + b % 2, :].rearrange("p (h d) -> p h d", d=HD),
                                a_ri.unsqueeze(2).to_broadcast([P, 8, HD]), ALU.mult).then_inc(sm("o_done"), 1)

            for u in range(NU + 3):
                if u < NU:
                    b, j, g = UNITS[u]
                    h = g * 4 + j
                    nt = len(key_tiles(l, b))
                    n = nt * P
                    v.wait_ge(sm("s_ps"), B0 + u + 1)
                    if u % 8 == 0 and b >= 2:
                        v.wait_ge(sm("p_done"), B0 + 8 * (b - 1))
                    src = ps[:, 3 * (u % 2):3 * (u % 2) + 3, :].rearrange("p a n -> p (a n)")[:, 0:n]
                    if l == 1:
                        if u >= 2:
                            v.wait_ge(sm("p_done"), B0 + u - 1)
                        o = 0 if (b > 0 or b == NS) else 1
                        dst = ssb[u % 2][:, 0:n]
                        if b == NS:
                            v.tensor_copy(dst, src)
                        else:
                            v.tensor_tensor(dst, src, cst("window")[:, o * P:o * P + n], ALU.add)
                        v.drain()
                        src = dst
                    v.tensor_reduce(a_mx[:, u % 8:u % 8 + 1], src, AX.X, ALU.max)
                    v.drain()
                    if l == 0:
                        v.tensor_scalar(a_nm[b % 2][:, h:h + 1], a_mx[:, u % 8:u % 8 + 1], -0.125, None, ALU.mult).then_inc(sm("nm_done"), 1)
                    else:
                        v.tensor_scalar(a_nm[b % 2][:, h:h + 1], a_mx[:, u % 8:u % 8 + 1], -0.125, sinks[:, 8 + h:9 + h],
                                        ALU.mult, ALU.min).then_inc(sm("nm_done"), 1)
                if 1 <= u <= NU:
                    evac(u - 1)
                if u >= 3 and (u - 3) % 8 == 7:
                    block_out((u - 3) // 8)
            phase_end(v)

        def att_act(act, l):
            B0 = NU * l

            def evac(u):
                b, j, g = UNITS[u]
                n = len(key_tiles(l, b))
                act.wait_ge(sm("pT_ps"), B0 + u + 1)
                if u >= 2:
                    act.wait_ge(sm("pv_ps"), B0 + u - 1)
                if n > 4:
                    act.activation(ptbuf[u % 2][:, 512:n * P],
                                   ps[:, 3 * (u % 2) + 1:3 * (u % 2) + 3, :].rearrange("p a n -> p (a n)")[:, 0:(n - 4) * P],
                                   ACT.Copy).then_inc(sm("pT_act"), 1)
                else:
                    act.drain().then_inc(sm("pT_act"), 1)

            for u in range(NU + 1):
                if u < NU:
                    b, j, g = UNITS[u]
                    h = g * 4 + j
                    n = len(key_tiles(l, b)) * P
                    act.wait_ge(sm("nm_done"), B0 + u + 1)
                    if u % 8 == 0 and b >= 2:
                        act.wait_ge(sm("o_done"), NT * l + b - 1)
                    if u >= 2:
                        act.wait_ge(sm("pT_ps"), B0 + u - 1)
                    nm = a_nm[b % 2][:, h:h + 1]
                    if l == 1:
                        act.activation(a_se[b % 2][:, h:h + 1], sinks[:, h:h + 1], ACT.Exp, bias=nm)
                        src = ssb[u % 2][:, 0:n]
                    else:
                        src = ps[:, 3 * (u % 2):3 * (u % 2) + 3, :].rearrange("p a n -> p (a n)")[:, 0:n]
                    act.activation(pbuf[u % 2][:, 0:n], src, ACT.Exp, bias=nm, scale=0.125,
                                   accum_out=a_rs[b % 2][:, h:h + 1]).then_inc(sm("p_done"), 1)
                if u >= 1:
                    evac(u - 1)
            phase_end(act)

        gr_ = Region(WORK - 2200)
        g_sl = [gr_.take(QW) for _ in range(2)]
        g_y = [gr_.take(QW) for _ in range(2)]

        def gate_pe(pe, r, name):
            w = weights(pe, name)
            for t in range(NT):
                if t >= 2:
                    pe.wait_ge(sm("gate_silu"), NT * r + t - 1)
                for k in range(KD):
                    mm = pe.matmul(ps[:, t % 2, :], hT[:, k, t * P:(t + 1) * P], w[:, k, :], start=(k == 0), stop=(k == KD - 1))
                mm.then_inc(sm("gate_mm"), 1)
            pe.drain().then_inc(sm("w_used"), 1)
            phase_end(pe)

        def gate_act(act, r):
            for t in range(NT):
                act.wait_ge(sm("gate_mm"), NT * r + t + 1)
                if t >= 2:
                    act.wait_ge(sm("gated"), NT * r + t - 1)
                act.activation(g_sl[t % 2], ps[:, t % 2, :], ACT.Silu).then_inc(sm("gate_silu"), 1)
            phase_end(act)

        def gate_dve(v, r, o):
            for t in range(NT):
                v.wait_ge(sm("gate_silu"), NT * r + t + 1)
                if t >= 2:
                    v.wait_ge(sm(f"ym_stored{t % 2}"), ym_count(r, t - 2))
                v.tensor_tensor(g_y[t % 2], g_sl[t % 2], o[:, t, :], ALU.mult).then_inc(sm("gated"), 1)
            phase_end(v)

        def ym_count(r, t):
            per = [(NT + 1) // 2, NT // 2][t % 2]
            return 16 * (per * r + t // 2 + 1)

        def gate_sp(sp, r):
            for t in range(NT):
                sp.wait_ge(sm("gated"), NT * r + t + 1)
                half = r % 2
                sp.dma_start(y_dram[t * P:(t + 1) * P, half * QW:(half + 1) * QW], g_y[t % 2]).then_inc(sm(f"ym_stored{t % 2}"), 16)
            sp.wait_ge(sm("ym_stored0"), ym_count(r, NT - 1))
            sp.wait_ge(sm("ym_stored1"), ym_count(r, NT - 2))
            sp.sem_inc(sm("phase_sp"), 1)

        fr = Region()
        f_y = [fr.take(D) for _ in range(2)]
        f_x = [fr.take(D) for _ in range(2)]
        f_yT = [fr.take(D) for _ in range(2)]
        f_z = [fr.take(D) for _ in range(2)]
        f_o = [fr.take(D) for _ in range(2)]
        f_junk = fr.take(D)
        f_st = fr.take(8)

        def fin_sp(sp, l, n):
            phase_seen(sp, n)
            for t in range(NT + 1):
                if t < NT:
                    if t >= 2:
                        sp.wait_ge(sm("yT_ps"), NT * l + t - 1)
                        sp.wait_ge(sm("res_done"), NT * l + t - 1)
                    sp.dma_start(f_y[t % 2], y_dram[t * P:(t + 1) * P, :]).then_inc(sm(f"f_loaded{t % 2}"), 16)
                    sp.dma_start(f_x[t % 2], x_rows(l, t)).then_inc(sm(f"f_loaded{t % 2}"), 16)
                if t >= 1:
                    u = t - 1
                    sp.wait_ge(sm("res_done"), NT * l + u + 1)
                    sp.dma_start(x_rows(1, u), f_o[u % 2]).then_inc(sm("y_stored"), 16)
            sp.wait_ge(sm("y_stored"), 16 * NT * (l + 1))

        def f_count(l, t):
            per = [(NT + 1) // 2, NT // 2][t % 2]
            return 32 * (per * l + t // 2 + 1)

        def fin_pe(pe, l):
            w = [weights(pe, f"out{l}.{j}") for j in range(2)]
            for t in range(NT + 1):
                if t < NT:
                    pe.wait_ge(sm(f"f_loaded{t % 2}"), f_count(l, t))
                    if t >= 2:
                        pe.wait_ge(sm("yT_done"), NT * l + t - 1)
                    for k in range(KD):
                        mm = pe.transpose(ps[:, 2 * (t % 2) + k // 4, (k % 4) * P:(k % 4 + 1) * P],
                                          f_y[t % 2][:, k * P:(k + 1) * P], ident)
                    mm.then_inc(sm("yT_ps"), 1)
                if t >= 1:
                    u = t - 1
                    pe.wait_ge(sm("yT_done"), NT * l + u + 1)
                    if u >= 2:
                        pe.wait_ge(sm("z_free"), NT * l + u - 1)
                    for j in range(2):
                        for k in range(KD):
                            mm = pe.matmul(ps[:, 4 + 2 * (u % 2) + j, :], f_yT[u % 2][:, k * P:(k + 1) * P], w[j][:, k, :],
                                           start=(k == 0), stop=(k == KD - 1))
                    mm.then_inc(sm("z_ps"), 1)
            pe.drain().then_inc(sm("w_used"), 2)
            phase_end(pe)

        def fin_act(act, l):
            for t in range(NT + 1):
                if t < NT:
                    act.wait_ge(sm("yT_ps"), NT * l + t + 1)
                    if t >= 2:
                        act.wait_ge(sm("z_ps"), NT * l + t - 1)
                    act.activation(f_yT[t % 2].rearrange("p (a n) -> p a n", a=2), ps[:, 2 * (t % 2):2 * (t % 2) + 2, :], ACT.Copy).then_inc(sm("yT_done"), 1)
                if t >= 1:
                    u = t - 1
                    act.wait_ge(sm("z_ps"), NT * l + u + 1)
                    if u >= 1:
                        act.wait_ge(sm("z_free"), NT * l + u)
                    act.drain()
                    act.activation(f_junk.rearrange("p (a n) -> p a n", a=2), ps[:, 4 + 2 * (u % 2):6 + 2 * (u % 2), :], ACT.Square, accum_out=f_st[:, 0:1])
                    act.drain()
                    act.activation(f_st[:, 1:2], f_st[:, 0:1], ACT.Ln, scale=1.0 / D, bias=eps_col)
                    act.drain()
                    act.activation(f_st[:, 2:3], f_st[:, 1:2], ACT.Exp, scale=-0.5).then_inc(sm("z_rs"), 1)
            phase_end(act)

        def fin_dve(v, l):
            for t in range(NT):
                cnd = int(t == NS)
                v.wait_ge(sm("z_rs"), NT * l + t + 1)
                v.wait_ge(sm(f"f_loaded{t % 2}"), f_count(l, t))
                v.scalar_tensor_tensor(f_z[t % 2].rearrange("p (a n) -> p a n", a=2), ps[:, 4 + 2 * (t % 2):6 + 2 * (t % 2), :], f_st[:, 2:3],
                                       gg[:, cnd, :].rearrange("p (a n) -> p a n", a=2), ALU.mult, ALU.mult).then_inc(sm("z_free"), 1)
                v.drain()
                if t >= 2:
                    v.wait_ge(sm("y_stored"), 16 * (NT * l + t - 1))
                v.tensor_tensor(f_o[t % 2], f_z[t % 2], f_x[t % 2], ALU.add).then_inc(sm("res_done"), 1)
            phase_end(v)

        GN = 512
        lr = Region()
        ob = lr.take(NT * QW).rearrange("p (t n) -> p t n", n=QW)
        l_v = lr.take(NT * QW).rearrange("p (t n) -> p t n", n=QW)
        l_qb = lr.take(NT * 256).rearrange("p (t n) -> p t n", n=256)
        l_kb = lr.take(NT * 256).rearrange("p (t n) -> p t n", n=256)
        l_dec = lr.take(NT * 8).rearrange("p (t n) -> p t n", n=8)
        l_up = lr.take(GN)
        l_rT = lr.take(P)
        l_abs = lr.take(GN)
        l_e = lr.take(GN)
        l_ln = lr.take(GN)
        l_g = lr.take(GN)
        l_ex = [lr.take(GN) for _ in range(3)]
        l_q = lr.take(GN)
        l_k = lr.take(GN)
        l_kf = lr.take(256)
        l_qT = lr.take(GN)
        l_kT = lr.take(GN)
        l_at = [lr.take(GN) for _ in range(2)]
        l_att = lr.take(GN)
        l_S = [[lr.take(256) for _ in range(3)] for _ in range(2)]
        l_on = lr.take(P)
        l_sq = lr.take(GN)
        l_st = lr.take(12)

        def gla_tiles(direction):
            return list(range(NS)) + [NS] if direction == 0 else list(range(NS))[::-1] + [NS]

        def state_view(ap, i):
            return ap[0, 0, i].rearrange("(r two) k v -> two k r v", two=2)

        def gla_sp(sp, n):
            phase_seen(sp, n)
            d = sm("gla_in")
            for i in range(2):
                sp.dma_start(l_up[16 * i:16 * i + 16, 256 * i:256 * i + 256], gla_gk_up[0, i]).then_inc(d, 16)
                sp.dma_start(l_up[16 * i:16 * i + 16, 256 * (1 - i):256 * (2 - i)], zeros_dram(16, 256)).then_inc(d, 16)
            sp.dma_start(l_up[32:33, :], gla_gk_bias.rearrange("a i n -> a (i n)")).then_inc(d, 16)
            sp.dma_start(l_on, gla_onorm[0].partition_broadcast(P)).then_inc(d, 16)
            for i in range(2):
                sv = state_view(state_gla, i)
                for two in range(2):
                    sp.dma_start(l_S[i][0][64 * two:64 * two + 64, :].rearrange("p (r v) -> p r v", v=DV), sv[two]).then_inc(d, 16)
            gla_state_out(sp, 0)

        def gla_state_out(sp, i):
            sp.wait_ge(sm(f"S_final{i}"), 1)
            sv = state_view(new_gla_state, i)
            for two in range(2):
                sp.dma_start(sv[two], l_S[i][2][64 * two:64 * two + 64, :].rearrange("p (r v) -> p r v", v=DV)).then_inc(sm("S_stored"), 16)
            sp.wait_ge(sm("S_stored"), 32 * (i + 1))

        def zeros_dram(a, b):
            o, _ = CONST_AT["sel"]
            return consts[2:2 + a, o:o + b]

        GLA_IN = 16 * 10

        def gla_pe(pe):
            wqk, wv = weights(pe, "bqk"), weights(pe, "bvr")
            pe.wait_ge(sm("gla_in"), GLA_IN)
            pe.wait_ge(sm("l_one"), 1)
            for t in range(NT):
                tok = slice(t * P, (t + 1) * P)
                if t:
                    pe.wait_ge(sm("l_o_out"), t)
                    pe.wait_ge(sm("l_u_used"), 2 * t)
                for k in range(KD):
                    pe.matmul(ps[0:32, 0, 0:P], wv[:, k, 512:544], hT[:, k, tok], start=(k == 0), stop=(k == KD - 1))
                for k in range(KD):
                    pe.matmul(ps[:, 1, :], hT[:, k, tok], wqk[:, k, :], start=(k == 0), stop=(k == KD - 1))
                for k in range(KD):
                    mm = pe.matmul(ps[:, 2, :], hT[:, k, tok], wv[:, k, 0:512], start=(k == 0), stop=(k == KD - 1))
                mm.then_inc(sm("l_qkv_ps"), 1)
                if t == NT - 1:
                    pe.drain().then_inc(sm("w_used"), 2)
                pe.wait_ge(sm("l_rT"), t + 1)
                pe.matmul(ps[:, 3, :], l_rT[0:33, :], l_up[0:33, :], start=True, stop=True).then_inc(sm("l_gk_ps"), 1)
                pe.wait_ge(sm("l_g"), t + 1)
                for i in range(2):
                    g = l_g[:, 256 * i:256 * i + 256]
                    pe.matmul(ps[:, 4, 256 * i:256 * i + 256], cst("upto", i, P), g, start=True, stop=True)
                    pe.matmul(ps[:, 5, 256 * i:256 * i + 256], cst("beyond", i, P), g, start=True, stop=True)
                for i in range(2):
                    for r in range(2):
                        mm = pe.matmul(ps[:, 0, 4 * i + 2 * r:4 * i + 2 * r + 2], l_g[:, 256 * i + P * r:256 * i + P * r + P],
                                       cst("chunkcol"), start=True, stop=True)
                mm.then_inc(sm("l_B_ps"), 1)
                pe.wait_ge(sm("l_qk"), t + 1)
                for j in range(4):
                    pe.transpose(ps[:, 6, j * P:(j + 1) * P], l_q[:, j * P:(j + 1) * P], ident)
                for j in range(4):
                    mm = pe.transpose(ps[:, 7, j * P:(j + 1) * P], l_k[:, j * P:(j + 1) * P], ident)
                mm.then_inc(sm("l_T_ps"), 1)
                pe.wait_ge(sm("l_qT"), t + 1)
                pe.wait_ge(sm("l_kT"), t + 1)
                for i in range(2):
                    for h in range(4):
                        r, o = h // 2, 64 * (h % 2)
                        cs = slice(256 * i + P * r, 256 * i + P * r + P)
                        mm = pe.matmul(ps[:, 4 + h % 2, (2 * i + r) * P:(2 * i + r + 1) * P], l_kT[o:o + 64, cs], l_qT[o:o + 64, cs], start=True, stop=True)
                mm.then_inc(sm("l_A_ps"), 1)
                pe.wait_ge(sm("l_kf"), t + 1)
                pe.wait_ge(sm("l_v"), t + 1)
                for cc in range(2):
                    gla_u(pe, t, cc, l_kf, (3, 0)[cc])
                pe.wait_ge(sm("l_att"), t + 1)
                for h in range(4):
                    r, e = h // 2, h % 2
                    pe.matmul(ps[:, 1 + e, r * P:(r + 1) * P], l_att[:, (2 * e + r) * P:(2 * e + r + 1) * P],
                              l_v[:, t, h * P:(h + 1) * P], start=(r == 0), stop=False, skip_group_check=True)
                for cc in range(2):
                    if cc:
                        pe.wait_ge(sm("l_S"), 2 * t + 1)
                    elif t:
                        pe.wait_ge(sm("l_S_in"), t)
                    gla_inter(pe, cc, l_qT[:, 0:256], l_S[0][cc], 1)
                pe.drain().then_inc(sm("l_o_ps"), 1)
            phase_end(pe)

        def o_parity(t, e):
            return ob[:, t, :].rearrange("p (r e n) -> p e r n", e=2, n=DV)[:, e]

        def gla_u(pe, t, cc, k_end, bank):
            rows = slice(64 * cc, 64 * cc + 64)
            for h in range(4):
                r, o = h // 2, 64 * (h % 2)
                mm = pe.matmul(ps[o:o + 64, bank, r * P:r * P + P], k_end[rows, h * 64:h * 64 + 64],
                               l_v[rows, t, h * P:(h + 1) * P], start=True, stop=True, skip_group_check=True)
            mm.then_inc(sm("l_u_ps"), 1)

        def gla_inter(pe, cc, qTd, state, bank, first=False):
            for h in range(4):
                r, o = h // 2, 64 * (h % 2)
                mm = pe.matmul(ps[64 * cc:64 * cc + 64, bank + h % 2, r * P:(r + 1) * P], qTd[o:o + 64, r * P + 64 * cc:r * P + 64 * cc + 64],
                               state[o:o + 64, r * P:(r + 1) * P], start=first and r == 0, stop=True, skip_group_check=True)
            return mm

        def gla_act(act):
            for t in range(NT):
                act.wait_ge(sm("l_qkv_ps"), t + 1)
                act.activation(l_rT[0:32, :], ps[0:32, 0, 0:P], ACT.Copy).then_inc(sm("l_rT"), 1)
                act.activation(l_v[:, t, :], ps[:, 2, :], ACT.Copy).then_inc(sm("l_v"), 1)
                act.wait_ge(sm("l_gk_ps"), t + 1)
                act.activation(l_abs, ps[:, 3, :], ACT.Abs)
                act.drain()
                act.activation(l_e, l_abs, ACT.Exp, scale=-1.0)
                act.drain()
                act.activation(l_ln, l_e, ACT.Ln, bias=1.0).then_inc(sm("l_ln"), 1)
                act.wait_ge(sm("l_B_ps"), t + 1)
                if t:
                    act.wait_ge(sm("l_kf"), t)
                act.activation(l_ex[0], ps[:, 4, :], ACT.Exp, scale=1 / 16.0)
                act.activation(l_ex[1], ps[:, 4, :], ACT.Exp, scale=-1 / 16.0)
                act.activation(l_ex[2], ps[:, 5, :], ACT.Exp, scale=1 / 16.0)
                act.activation(l_dec[:, t, :], ps[:, 0, 0:8], ACT.Exp, scale=1 / 16.0).then_inc(sm("l_ex"), 1)
                act.wait_ge(sm("l_T_ps"), t + 1)
                if t:
                    act.wait_ge(sm("l_o_ps"), t)
                act.activation(l_qT, ps[:, 6, :], ACT.Copy).then_inc(sm("l_qT"), 1)
                act.activation(l_qb[:, t, :], ps[:, 6, 256:512], ACT.Copy)
                act.wait_ge(sm("l_o_ps"), t + 1)
                for e in range(2):
                    mm = act.activation(o_parity(t, e), ps[:, 1 + e, 0:256].rearrange("p (r n) -> p r n", r=2), ACT.Copy)
                mm.then_inc(sm("l_o_out"), 1)
            phase_end(act)

        def gla_dve(v):
            v.memset(l_rT[32:33, :], 1.0).then_inc(sm("l_one"), 1)
            v.wait_ge(sm("gla_in"), GLA_IN)
            for t in range(NT):
                v.wait_ge(sm("l_ln"), t + 1)
                v.scalar_tensor_tensor(l_g, ps[:, 3, :], 0.0, l_ln, ALU.min, ALU.subtract).then_inc(sm("l_g"), 1)
                v.wait_ge(sm("l_ex"), t + 1)
                two = lambda ap: ap.rearrange("p (i n) -> p i n", i=2)
                qps = ps[:, 1, 0:256].unsqueeze(1).to_broadcast([P, 2, 256])
                kps = ps[:, 1, 256:512].unsqueeze(1).to_broadcast([P, 2, 256])
                v.scalar_tensor_tensor(two(l_q), qps, 0.125, two(l_ex[0]), ALU.mult, ALU.mult)
                v.tensor_tensor(two(l_k), kps, two(l_ex[1]), ALU.mult).then_inc(sm("l_qk"), 1)
                v.tensor_tensor(l_kf, ps[:, 1, 256:512], l_ex[2][:, 0:256], ALU.mult)
                v.tensor_tensor(l_kb[:, t, :], ps[:, 1, 256:512], l_ex[2][:, 256:512], ALU.mult).then_inc(sm("l_kf"), 1)
                v.wait_ge(sm("l_T_ps"), t + 1)
                v.tensor_copy(l_kT, ps[:, 7, :]).then_inc(sm("l_kT"), 1)
                v.wait_ge(sm("l_A_ps"), t + 1)
                for e in range(2):
                    v.tensor_tensor(l_at[e].rearrange("p (i r n) -> p i r n", i=2, n=P), ps[:, 4 + e, :].rearrange("p (i r n) -> p i r n", i=2, n=P),
                                    cst("upto").rearrange("p (i n) -> p i n", i=2).unsqueeze(2).to_broadcast([P, 2, 2, P]), ALU.mult)
                v.drain()
                v.tensor_tensor(l_att[:, 0:256], l_at[0][:, 0:256], l_at[0][:, 256:512], ALU.add)
                v.tensor_tensor(l_att[:, 256:512], l_at[1][:, 0:256], l_at[1][:, 256:512], ALU.add).then_inc(sm("l_att"), 1)
                if t:
                    v.wait_ge(sm("l_o_ps"), t)
                    if t == NS:
                        v.memset(l_S[0][0], 0.0)
                    else:
                        v.tensor_copy(l_S[0][0], l_S[0][2])
                    v.drain().then_inc(sm("l_S_in"), 1)
                for cc in range(2):
                    v.wait_ge(sm("l_u_ps"), 2 * t + cc + 1)
                    for r in range(2):
                        s = v.scalar_tensor_tensor(l_S[0][cc + 1][:, r * P:(r + 1) * P], l_S[0][cc][:, r * P:(r + 1) * P],
                                                   l_dec[:, t, 2 * r + cc:2 * r + cc + 1],
                                                   ps[:, (3, 0)[cc], r * P:r * P + P], ALU.mult, ALU.add)
                    v.drain().then_inc(sm("l_S"), 1)
                    v.drain().then_inc(sm("l_u_used"), 1)
            v.drain().then_inc(sm("S_final0"), 1)
            phase_end(v)

        def glab_sp(sp, n):
            phase_seen(sp, n)
            gla_state_out(sp, 1)
            sp.sem_inc(sm("phase_sp"), 1)

        def glab_pe(pe):
            for m, t in enumerate(gla_tiles(1)):
                b = 4 * (m % 2)
                if m >= 2:
                    pe.wait_ge(sm("m_o_used"), m - 1)
                    pe.wait_ge(sm("m_S"), 2 * (m - 1))
                for cc in (1, 0):
                    gla_u(pe, t, cc, l_kb[:, t, :], b + cc)
                for n, cc in enumerate((1, 0)):
                    if n:
                        pe.wait_ge(sm("m_S"), 2 * m + 1)
                    elif m:
                        pe.wait_ge(sm("m_S_in"), m)
                    mm = gla_inter(pe, cc, l_qb[:, t, :], l_S[1][n], b + 2, first=True)
                mm.then_inc(sm("m_o_ps"), 1)
            phase_end(pe)

        def glab_dve(v):
            for m, t in enumerate(gla_tiles(1)):
                b = 4 * (m % 2)
                if m:
                    v.wait_ge(sm("m_o_ps"), m)
                    if t == NS:
                        v.memset(l_S[1][0], 0.0)
                    else:
                        v.tensor_copy(l_S[1][0], l_S[1][2])
                    v.drain().then_inc(sm("m_S_in"), 1)
                for n, cc in enumerate((1, 0)):
                    v.wait_ge(sm("l_u_ps"), 2 * NT + 2 * m + n + 1)
                    for r in range(2):
                        v.scalar_tensor_tensor(l_S[1][n + 1][:, r * P:(r + 1) * P], l_S[1][n][:, r * P:(r + 1) * P],
                                               l_dec[:, t, 4 + 2 * r + cc:4 + 2 * r + cc + 1],
                                               ps[:, b + cc, r * P:r * P + P], ALU.mult, ALU.add)
                    v.drain().then_inc(sm("m_S"), 1)
                v.wait_ge(sm("m_o_ps"), m + 1)
                for e in range(2):
                    mm = v.tensor_tensor(o_parity(t, e), ps[:, b + 2 + e, 0:256].rearrange("p (r n) -> p r n", r=2), o_parity(t, e), ALU.add)
                mm.then_inc(sm("m_o_used"), 1)
                onorm_dve(v, m, t, l_sq, l_st, l_on)
            v.drain().then_inc(sm("S_final1"), 1)
            phase_end(v)

        def onorm_dve(v, m, t, sq, st, wn):
            o4 = ob[:, t, :].rearrange("p (h n) -> p h n", n=DV)
            v.wait_ge(sm("on_sq"), m + 1)
            v.tensor_reduce(st[:, 0:4], sq.rearrange("p (h n) -> p h n", n=DV), AX.X, ALU.add).then_inc(sm("on_ss"), 1)
            v.wait_ge(sm("on_rs"), m + 1)
            v.tensor_tensor(o4, o4, st[:, 8:12].unsqueeze(2).to_broadcast([P, 4, DV]), ALU.mult)
            v.drain()
            v.tensor_tensor(o4, o4, wn.unsqueeze(1).to_broadcast([P, 4, DV]), ALU.mult)

        def onorm_act(act, m, t, sq, st, ready):
            if ready is not None:
                act.wait_ge(sm(ready), m + 1)
            act.activation(sq, ob[:, t, :], ACT.Square).then_inc(sm("on_sq"), 1)
            act.wait_ge(sm("on_ss"), m + 1)
            act.activation(st[:, 4:8], st[:, 0:4], ACT.Ln, scale=1.0 / DV, bias=eps_col)
            act.drain()
            act.activation(st[:, 8:12], st[:, 4:8], ACT.Exp, scale=-0.5).then_inc(sm("on_rs"), 1)

        def glab_act(act):
            for m, t in enumerate(gla_tiles(1)):
                onorm_act(act, m, t, l_sq, l_st, "m_o_used")
            phase_end(act)

        NZ = T + 6
        NC2 = T + 2
        N72 = 2 * NT * 4
        er_ = Region(NT * QW)
        c_z = er_.take(NT * 16)
        c_in = er_.take(32)
        c_rows = er_.take(P)
        c_w = er_.take(60)
        c_sp = er_.take(NT * 8)
        c_t = er_.take(NT * 8)
        c_g, c_gc, c_beta, c_eg, c_er, c_nb = (er_.take(N72) for _ in range(6))
        c_dec = er_.take(2 * N72)
        d_qT, d_kT = er_.take(T), er_.take(T)
        d_k = er_.take(T).rearrange("p (t n) -> p t n", n=P)
        d_v = er_.take(T).rearrange("p (t n) -> p t n", n=P)
        r1 = er_.at
        zp = er_.take(3 * NZ).rearrange("p (b n) -> p b n", b=3)
        zc = er_.take(3 * NC2)
        zcb = zc.rearrange("p (b n) -> p b n", b=3)
        z_sq = er_.take(2 * NC2)
        z_rn = er_.take(2 * NC2)
        er2 = Region(r1)
        d_Z, d_A, d_W, d_Q, d_K, d_V = (er2.take(2 * T).rearrange("p (i t n) -> p i t n", i=2, n=P) for _ in range(6))
        r3 = er2.at
        d_D, d_DT, d_E, d_T, d_X, d_Y = (er2.take(3 * P) for _ in range(6))
        er3 = Region(r3)
        d_S = [[er3.take(P) for _ in range(3)] for _ in range(2)]
        d_vn = [er3.take(P) for _ in range(2)]
        o_sq = Region(r1).take(QW)
        o_st = Region(r1 + QW).take(12)
        o_on = Region(r1 + QW + 12).take(P)

        def col(ap, i, t, h):
            n = (i * NT + t) * 4 + h
            return ap[:, n:n + 1]

        def ab_sp(sp, n):
            phase_seen(sp, n)
            d = sm("ab_in")
            sp.dma_start(c_in[:, 0:8], dt_bias_d[0].rearrange("i h -> (i h)").partition_broadcast(P)).then_inc(d, 16)
            sp.dma_start(c_in[:, 8:16], a_log_d[0].rearrange("i h -> (i h)").partition_broadcast(P)).then_inc(d, 16)
            sp.dma_start(c_rows[0:60, :], conv_d[0].rearrange("k (b p) -> (k b) p", p=P)).then_inc(d, 16)

        def ab_pe(pe):
            w = weights(pe, "ab")
            for t in range(NT):
                for k in range(KD):
                    pe.matmul(ps[:, 0, 16 * t:16 * t + 16], hT[:, k, t * P:(t + 1) * P], w[:, k, :], start=(k == 0), stop=(k == KD - 1))
            pe.drain().then_inc(sm("w_used"), 1)
            pe.wait_ge(sm("ab_in"), 48)
            pe.transpose(ps[:, 1, 0:60], c_rows[0:60, :], ident[0:60, 0:60]).then_inc(sm("ab_ps"), 1)
            pe.wait_ge(sm("c_g"), 1)
            for i in range(2):
                g = c_g[:, 36 * i:36 * i + 36]
                pe.matmul(ps[:, 2, 36 * i:36 * i + 36], cst("upto", i, P), g, start=True, stop=True)
                pe.matmul(ps[:, 3, 36 * i:36 * i + 36], cst("beyond", i, P), g, start=True, stop=True)
            for cc in range(2):
                mm = pe.matmul(ps[:, 4, N72 * cc:N72 * cc + N72], cst("inchunk", cc, P), c_g, start=True, stop=True)
            mm.then_inc(sm("c_ps"), 1)
            phase_end(pe)

        def ab_act(act):
            act.wait_ge(sm("ab_ps"), 1)
            act.activation(c_w, ps[:, 1, 0:60], ACT.Copy)
            act.activation(c_in[:, 16:24], c_in[:, 8:16], ACT.Exp)
            act.wait_ge(sm("c_a"), 1)
            act.activation(c_z.rearrange("p (t n) -> p t n", n=16)[:, :, 8:16], ps[:, 0, 0:NT * 16].rearrange("p (t n) -> p t n", n=16)[:, :, 8:16],
                           ACT.Exp, scale=-1.0)
            act.activation(c_t, c_sp, ACT.Abs)
            act.drain()
            act.activation(c_t, c_t, ACT.Exp, scale=-1.0)
            act.drain()
            act.activation(c_t, c_t, ACT.Ln, bias=1.0).then_inc(sm("c_ln"), 1)
            act.wait_ge(sm("c_ps"), 1)
            act.activation(c_gc, ps[:, 2, 0:N72], ACT.Copy)
            act.activation(c_eg, ps[:, 2, 0:N72], ACT.Exp)
            act.activation(c_er, ps[:, 3, 0:N72], ACT.Exp)
            act.activation(c_dec, ps[:, 4, 0:2 * N72], ACT.Exp).then_inc(sm("c_ex"), 1)
            phase_end(act)

        def ab_dve(v):
            v.memset(ob.rearrange("p t n -> p (t n)"), 0.0)
            v.wait_ge(sm("ab_in"), 48)
            v.wait_ge(sm("ab_ps"), 1)
            tih = lambda ap, n: ap.rearrange("p (t n) -> p t n", n=n)
            v.tensor_tensor(tih(c_sp, 8), tih(ps[:, 0, 0:NT * 16], 16)[:, :, 0:8], c_in[:, 0:8].unsqueeze(1).to_broadcast([P, NT, 8]), ALU.add)
            v.drain().then_inc(sm("c_a"), 1)
            v.wait_ge(sm("c_ln"), 1)
            v.scalar_tensor_tensor(c_sp, c_sp, 0.0, c_t, ALU.max, ALU.add)
            v.drain()
            v.scalar_tensor_tensor(tih(c_sp, 8), tih(c_sp, 8), -1.0, c_in[:, 16:24].unsqueeze(1).to_broadcast([P, NT, 8]), ALU.mult, ALU.mult)
            z8 = c_z.rearrange("p (t n) -> p t n", n=16)[:, :, 8:16]
            v.tensor_scalar(z8, z8, 1.0, None, ALU.add)
            v.drain()
            for i in range(2):
                v.tensor_copy(c_g[:, 36 * i:36 * i + 36].rearrange("p (t h) -> p t h", h=4), tih(c_sp, 8)[:, :, 4 * i:4 * i + 4])
            v.drain().then_inc(sm("c_g"), 1)
            for i in range(2):
                v.reciprocal(c_beta[:, 36 * i:36 * i + 36].rearrange("p (t h) -> p t h", h=4), z8[:, :, 4 * i:4 * i + 4])
            v.drain()
            v.wait_ge(sm("c_ex"), 1)
            v.scalar_tensor_tensor(c_nb, c_beta, -1.0, c_eg, ALU.mult, ALU.mult)
            phase_end(v)

        TOK = [(0, 512, 2), (512, 512, 514), (T_S, T_P, T_S + 4)]
        NORM = [(a, min(512, 2 * NC2 - a)) for a in range(0, 2 * NC2, 512)]

        def pre_pe(pe, h):
            w = weights(pe, f"dh{h}")
            for n in range(9):
                b, (o, m, _) = n // 3, TOK[n % 3]
                if n == 8:
                    pe.wait_ge(sm("zp"), 9 * h + 1)
                for k in range(KD):
                    mm = pe.matmul(ps[:, n % 8, 0:m], w[:, k, b * P:(b + 1) * P], hT[:, k, o:o + m], start=(k == 0), stop=(k == KD - 1))
                mm.then_inc(sm("zp_ps"), 1)
            pe.drain().then_inc(sm("w_used"), 1)
            pe.wait_ge(sm("z_sq"), h + 1)
            for n, (o, m) in enumerate(NORM):
                mm = pe.matmul(ps[:, n, 0:m], ones, z_sq[:, o:o + m], start=True, stop=True)
            mm.then_inc(sm("z_ss"), 1)
            pe.wait_ge(sm("d_qkT"), h + 1)
            for t in range(NT):
                if t >= 2:
                    pe.wait_ge(sm("d_kv"), NT * h + t - 1)
                vo = t * P + (2 if t == NS else 0)
                pe.transpose(ps[:, 6 + t % 2, 0:P], d_kT[:, t * P:(t + 1) * P], ident)
                pe.transpose(ps[:, 6 + t % 2, P:2 * P], zcb[:, 2, vo:vo + P], ident).then_inc(sm("d_kv_ps"), 1)
            phase_end(pe)

        def pre_act(act, h):
            for n in range(9):
                b, (_, m, o) = n // 3, TOK[n % 3]
                act.wait_ge(sm("zp_ps"), 9 * h + n + 1)
                act.activation(zp[:, b, o:o + m], ps[:, n % 8, 0:m], ACT.Copy).then_inc(sm("zp"), 1)
            act.wait_ge(sm("zc"), h + 1)
            act.activation(zc, zc, ACT.Silu)
            act.drain()
            act.activation(z_sq, zc[:, 0:2 * NC2], ACT.Square).then_inc(sm("z_sq"), 1)
            act.wait_ge(sm("z_ss"), h + 1)
            act.activation(z_rn, ps[:, 0:5, :].rearrange("p a n -> p (a n)")[:, 0:2 * NC2], ACT.Ln, bias=eps_col)
            act.drain()
            act.activation(z_rn, z_rn, ACT.Exp, scale=-0.5).then_inc(sm("z_rn"), 1)
            for t in range(NT):
                act.wait_ge(sm("d_kv_ps"), NT * h + t + 1)
                act.activation(d_k[:, t, :], ps[:, 6 + t % 2, 0:P], ACT.Copy)
                act.activation(d_v[:, t, :], ps[:, 6 + t % 2, P:2 * P], ACT.Copy).then_inc(sm("d_kv"), 1)
            phase_end(act)

        def pre_dve(v, h):
            for a in (0, 2 + T_S, 4 + T):
                v.memset(zp[:, :, a:a + 2], 0.0)
            v.drain()
            for k in range(5):
                for b in range(3):
                    if k == 0:
                        v.wait_ge(sm("zp"), 9 * h + 3 * b + 3)
                    tap = c_w[:, 12 * k + 4 * b + h:12 * k + 4 * b + h + 1]
                    if k == 0:
                        v.tensor_scalar(zcb[:, b, :], zp[:, b, k:k + NC2], tap, None, ALU.mult)
                    else:
                        v.scalar_tensor_tensor(zcb[:, b, :], zp[:, b, k:k + NC2], tap, zcb[:, b, :], ALU.mult, ALU.add)
                v.drain()
            v.drain().then_inc(sm("zc"), 1)
            v.wait_ge(sm("z_rn"), h + 1)
            for dst, b, s in ((d_qT, 0, P ** -0.5), (d_kT, 1, 1.0)):
                for o, n, x in ((0, T_S, 0), (T_S, T_P, 2)):
                    a = b * NC2 + o + x
                    v.scalar_tensor_tensor(dst[:, o:o + n], z_rn[:, a:a + n], s, zc[:, a:a + n], ALU.mult, ALU.mult)
            v.drain().then_inc(sm("d_qkT"), 1)
            phase_end(v)

        GROUPS = [(i, 3 * a) for i in range(2) for a in range(3)]

        def tiles3(ap):
            return ap.rearrange("p (a n) -> p a n", n=P)

        def sys_pe(pe, h):
            for n, (i, t0) in enumerate(GROUPS):
                N = 6 * h + n
                for a in range(3):
                    t = t0 + a
                    ks = d_kT[:, t * P:(t + 1) * P]
                    pe.matmul(ps[:, 0, a * P:(a + 1) * P], col(c_g, i, t, h).to_broadcast([P, P]), cst("upto", i, P), start=True, stop=True)
                    pe.matmul(ps[:, 1, a * P:(a + 1) * P], ks, ks, start=True, stop=True)
                    mm = pe.matmul(ps[:, 2, a * P:(a + 1) * P], ks, d_qT[:, t * P:(t + 1) * P], start=True, stop=True)
                mm.then_inc(sm("s_G_ps"), 1)
                pe.wait_ge(sm("s_X1"), N + 1)
                for a in range(3):
                    mm = pe.transpose(ps[:, 3, a * P:(a + 1) * P], d_X[:, a * P:(a + 1) * P], ident)
                mm.then_inc(sm("s_Z1_ps"), 1)
                for k in range(1, NLEV):
                    pe.wait_ge(sm("s_ZX"), 5 * N + k)
                    for a in range(3):
                        mm = pe.matmul(ps[:, 4, a * P:(a + 1) * P], d_T[:, a * P:(a + 1) * P], d_Z[:, i, t0 + a, :], start=True, stop=True)
                    mm.then_inc(sm("s_Y_ps"), 1)
                    pe.wait_ge(sm("s_Y"), 5 * N + k)
                    for a in range(3):
                        y, x = d_Y[:, a * P:(a + 1) * P], d_X[:, a * P:(a + 1) * P]
                        mm = pe.matmul(ps[:, 5, a * P:(a + 1) * P], x, y, start=True, stop=True)
                        if k < NLEV - 1:
                            mm = pe.matmul(ps[:, 6, a * P:(a + 1) * P], y, x, start=True, stop=True)
                    mm.then_inc(sm("s_ZY_ps"), 1)
                pe.wait_ge(sm("s_Z"), N + 1)
                pe.wait_ge(sm("s_kb"), N + 1)
                for a in range(3):
                    mm = pe.matmul(ps[:, 7, a * P:(a + 1) * P], d_D[:, a * P:(a + 1) * P], d_Z[:, i, t0 + a, :], start=True, stop=True)
                mm.then_inc(sm("s_W_ps"), 1)
                pe.wait_ge(sm("s_E"), N + 1)
            phase_end(pe)

        def sys_act(act, h):
            for n, (i, t0) in enumerate(GROUPS):
                N = 6 * h + n
                act.wait_ge(sm("s_G_ps"), N + 1)
                if n:
                    act.wait_ge(sm("s_Q"), N)
                act.activation(d_E, ps[:, 0, 0:384], ACT.Exp).then_inc(sm("s_E"), 1)
                act.wait_ge(sm("s_D"), N + 1)
                act.activation(d_D, d_D, ACT.Exp, scale=-1.0)
                act.activation(d_DT, d_DT, ACT.Exp).then_inc(sm("s_ex"), 1)
                for a in range(3):
                    t = t0 + a
                    act.activation(d_V[:, i, t, :], d_v[:, t, :], ACT.Copy, scale=col(c_beta, i, t, h))
                    act.activation(d_K[:, i, t, :], d_k[:, t, :], ACT.Copy, scale=col(c_er, i, t, h))
                act.wait_ge(sm("s_X1"), N + 1)
                for a in range(3):
                    mm = act.activation(d_D[:, a * P:(a + 1) * P], d_k[:, t0 + a, :], ACT.Copy, scale=col(c_nb, i, t0 + a, h))
                mm.then_inc(sm("s_kb"), 1)
                act.wait_ge(sm("s_W_ps"), N + 1)
                act.activation(d_W[:, i, t0:t0 + 3, :], tiles3(ps[:, 7, 0:384]), ACT.Copy).then_inc(sm("s_W"), 1)
            phase_end(act)

        def sys_dve(v, h):
            for n, (i, t0) in enumerate(GROUPS):
                N = 6 * h + n
                v.wait_ge(sm("s_G_ps"), N + 1)
                if n:
                    v.wait_ge(sm("s_W"), N)
                v.wait_ge(sm("s_E"), N + 1)
                for a in range(3):
                    t, s = t0 + a, slice(a * P, (a + 1) * P)
                    v.scalar_tensor_tensor(d_D[:, s], ps[:, 0, s], col(c_gc, i, t, h), cst("strict", i, P), ALU.subtract, ALU.max)
                    v.scalar_tensor_tensor(d_DT[:, s], ps[:, 0, s], col(c_gc, i, t, h), cst("incl", i, P), ALU.subtract, ALU.min)
                v.drain().then_inc(sm("s_D"), 1)
                v.wait_ge(sm("s_ex"), N + 1)
                for a in range(3):
                    t, s = t0 + a, slice(a * P, (a + 1) * P)
                    v.scalar_tensor_tensor(d_T[:, s], ps[:, 1, s], col(c_beta, i, t, h), d_D[:, s], ALU.mult, ALU.mult)
                v.drain()
                lv = cst("level0", 1 - i, P).unsqueeze(1).to_broadcast([P, 3, P])
                v.scalar_tensor_tensor(tiles3(d_X), tiles3(d_T), -1.0, lv, ALU.mult, ALU.mult)
                v.drain()
                v.tensor_tensor(tiles3(d_X), tiles3(d_X), ident.unsqueeze(1).to_broadcast([P, 3, P]), ALU.add).then_inc(sm("s_X1"), 1)
                v.tensor_tensor(d_A[:, i, t0:t0 + 3, :], tiles3(ps[:, 2, 0:384]), tiles3(d_DT), ALU.mult)
                v.tensor_tensor(d_Q[:, i, t0:t0 + 3, :], tiles3(d_qT[:, t0 * P:t0 * P + 384]), tiles3(d_E), ALU.mult).then_inc(sm("s_Q"), 1)
                v.wait_ge(sm("s_Z1_ps"), N + 1)
                Z = d_Z[:, i, t0:t0 + 3, :]
                v.tensor_copy(Z, tiles3(ps[:, 3, 0:384])).then_inc(sm("s_ZX"), 1)
                for k in range(1, NLEV):
                    v.wait_ge(sm("s_Y_ps"), 5 * N + k)
                    lv = cst(f"level{k}", i, P).unsqueeze(1).to_broadcast([P, 3, P])
                    v.tensor_tensor(tiles3(d_Y), tiles3(ps[:, 4, 0:384]), lv, ALU.mult).then_inc(sm("s_Y"), 1)
                    v.wait_ge(sm("s_ZY_ps"), 5 * N + k)
                    z = v.scalar_tensor_tensor(Z, tiles3(ps[:, 5, 0:384]), -1.0, Z, ALU.mult, ALU.add)
                    if k < NLEV - 1:
                        v.scalar_tensor_tensor(d_X, ps[:, 6, 0:384], -1.0, d_X, ALU.mult, ALU.add).then_inc(sm("s_ZX"), 1)
                    else:
                        z.then_inc(sm("s_Z"), 1)
            phase_end(v)

        STEPS = [(s, False) for s in range(2 * NS)] + [(s, True) for s in range(2)]

        def step_of(i, n):
            s, prompt = STEPS[n]
            if prompt:
                cc = s if i == 0 else 1 - s
                return NS, cc, (2, 1)[s], (1, 0)[s]
            g = s if i == 0 else 2 * NS - 1 - s
            return g // 2, g % 2, n % 2, (n + 1) % 2

        NST = len(STEPS)

        def scan_sp(sp, h, n):
            phase_seen(sp, n)
            for i in range(2):
                sp.dma_start(d_S[i][0], state_delta[0, 0, i, h]).then_inc(sm("d_S_in"), 16)
            for i in range(2):
                sp.wait_ge(sm(f"d_S{i}"), NST * (h + 1))
                sp.dma_start(new_delta_state[0, 0, i, h], d_S[i][0]).then_inc(sm("d_S_stored"), 16)
            sp.wait_ge(sm("d_S_stored"), 32 * (h + 1))
            sp.sem_inc(sm("phase_sp"), 1)

        def scan_pe(pe, h):
            pe.wait_ge(sm("d_S_in"), 32 * (h + 1))
            pe.wait_ge(sm("d_S_zero"), h + 1)
            for n in range(NST):
                N = NST * h + n
                for i in range(2):
                    t, cc, a, _ = step_of(i, n)
                    rows = slice(64 * cc, 64 * cc + 64)
                    pe.matmul(ps[rows, 3 * i, 0:P], d_Z[:, i, t, rows], d_V[:, i, t, :], start=True, stop=False)
                    if n:
                        pe.wait_ge(sm(f"d_S{i}"), N)
                    pe.matmul(ps[rows, 3 * i, 0:P], d_W[:, i, t, rows], d_S[i][a], start=False, stop=True).then_inc(sm(f"d_vn_ps{i}"), 1)
                    if n:
                        pe.wait_ge(sm(f"d_o{i}"), N)
                    pe.matmul(ps[rows, 3 * i + 1, 0:P], d_Q[:, i, t, rows], d_S[i][a], start=True, stop=False)
                for i in range(2):
                    t, cc, a, _ = step_of(i, n)
                    rows = slice(64 * cc, 64 * cc + 64)
                    pe.wait_ge(sm(f"d_vn{i}"), N + 1)
                    pe.matmul(ps[:, 3 * i + 2, 0:P], d_K[rows, i, t, :], d_vn[i][rows, :], start=True, stop=True).then_inc(sm(f"d_kS_ps{i}"), 1)
                    pe.matmul(ps[rows, 3 * i + 1, 0:P], d_A[rows, i, t, rows], d_vn[i][rows, :], start=False, stop=True).then_inc(sm(f"d_o_ps{i}"), 1)
            phase_end(pe)

        def scan_act(act, h):
            for n in range(NST):
                for i in range(2):
                    t, cc, a, _ = step_of(i, n)
                    rows = slice(64 * cc, 64 * cc + 64)
                    act.wait_ge(sm(f"d_vn_ps{i}"), NST * h + n + 1)
                    if n:
                        act.wait_ge(sm(f"d_o_ps{i}"), NST * h + n)
                    act.activation(d_vn[i][rows, :], ps[rows, 3 * i, 0:P], ACT.Copy).then_inc(sm(f"d_vn{i}"), 1)
            phase_end(act)

        def scan_dve(v, h):
            for i in range(2):
                v.memset(d_S[i][2], 0.0)
            v.drain().then_inc(sm("d_S_zero"), 1)
            v.wait_ge(sm("d_S_in"), 32 * (h + 1))
            for n in range(NST):
                N = NST * h + n
                for i in range(2):
                    t, cc, a, b = step_of(i, n)
                    m = cc * N72 + (i * NT + t) * 4 + h
                    v.wait_ge(sm(f"d_kS_ps{i}"), N + 1)
                    v.scalar_tensor_tensor(d_S[i][b], d_S[i][a], c_dec[:, m:m + 1], ps[:, 3 * i + 2, 0:P], ALU.mult, ALU.add).then_inc(sm(f"d_S{i}"), 1)
                for i in range(2):
                    t, cc, a, b = step_of(i, n)
                    rows = slice(64 * cc, 64 * cc + 64)
                    v.wait_ge(sm(f"d_o_ps{i}"), N + 1)
                    o = ob[rows, t, h * P:(h + 1) * P]
                    v.tensor_tensor(o, ps[rows, 3 * i + 1, 0:P], o, ALU.add).then_inc(sm(f"d_o{i}"), 1)
            phase_end(v)

        def don_sp(sp, n):
            phase_seen(sp, n)
            sp.dma_start(o_on, delta_onorm[0].partition_broadcast(P)).then_inc(sm("don_in"), 16)

        def don_act(act):
            for t in range(NT):
                if t:
                    act.wait_ge(sm("on_ss"), NT + t)
                onorm_act(act, NT + t, t, o_sq, o_st, None)
            phase_end(act)

        def don_dve(v):
            v.wait_ge(sm("don_in"), 16)
            for t in range(NT):
                onorm_dve(v, NT + t, t, o_sq, o_st, o_on)
            phase_end(v)

        eps_col = small[:, 0:1]
        STAGES = ["mod0", "ada0", "qkv0", "att0", "gateA0", "gla", "glab", "gateB0", "fin0",
                  "mod1", "ada1", "qkv1", "att1", "gateA1", "dab"]
        STAGES += [f"{s}{h}" for h in range(4) for s in ("dpre", "dsys", "dscan")]
        STAGES += ["don", "gateB1", "fin1"]
        no = STAGES.index
        STORING = [s for s in STAGES if s.startswith(("qkv", "gate", "glab", "dscan"))]

        def stores_done(eng, stage):
            eng.wait_ge(sm("phase_sp"), STORING.index(stage) + 1)

        block = ctx.enter_context(nc.Block())

        @block.gpsimd
        def _(pool):
            for i, (name, parts, n) in enumerate(chunks):
                if i >= RING:
                    pool.wait_ge(sm("w_used"), i - RING + 1)
                o = 0
                for src in parts:
                    m = src.shape[2]
                    pool.dma_start(wslot(i, n)[:, :, o:o + m], src).then_inc(sm(f"w_loaded{i % RING}"), 16)
                    o += m

        @block.sync
        def _(sp):
            sp.dma_start(con[:, :], consts).then_inc(sm("const_in"), 16)
            for l in range(2):
                mod_sp(sp, l, no(f"mod{l}"))
                ada_sp(sp, l, no(f"ada{l}"))
                qkv_sp(sp, l, no(f"qkv{l}"))
                att_sp(sp, l, no(f"att{l}"))
                gate_sp(sp, 2 * l)
                if l == 0:
                    gla_sp(sp, no("gla"))
                    glab_sp(sp, no("glab"))
                else:
                    ab_sp(sp, no("dab"))
                    for h in range(4):
                        scan_sp(sp, h, no(f"dscan{h}"))
                    don_sp(sp, no("don"))
                gate_sp(sp, 2 * l + 1)
                fin_sp(sp, l, no(f"fin{l}"))

        @block.tensor
        def _(pe):
            pe.wait_ge(sm("const_in"), 16)
            for l in range(2):
                mod_pe(pe, l)
                ada_pe(pe, l)
                qkv_pe(pe, l)
                stores_done(pe, f"qkv{l}")
                att_pe(pe, l)
                gate_pe(pe, 2 * l, f"ga{l}")
                stores_done(pe, f"gateA{l}")
                if l == 0:
                    gla_pe(pe)
                    glab_pe(pe)
                    stores_done(pe, "glab")
                else:
                    ab_pe(pe)
                    for h in range(4):
                        pre_pe(pe, h)
                        sys_pe(pe, h)
                        scan_pe(pe, h)
                        stores_done(pe, f"dscan{h}")
                    phase_end(pe)
                gate_pe(pe, 2 * l + 1, f"gb{l}")
                stores_done(pe, f"gateB{l}")
                fin_pe(pe, l)

        @block.scalar
        def _(act):
            act.wait_ge(sm("eps"), 1)
            act.wait_ge(sm("const_in"), 16)
            for l in range(2):
                mod_act(act, l)
                ada_act(act, l)
                qkv_act(act, l)
                stores_done(act, f"qkv{l}")
                att_act(act, l)
                gate_act(act, 2 * l)
                stores_done(act, f"gateA{l}")
                if l == 0:
                    gla_act(act)
                    glab_act(act)
                    stores_done(act, "glab")
                else:
                    ab_act(act)
                    for h in range(4):
                        pre_act(act, h)
                        sys_act(act, h)
                        scan_act(act, h)
                        stores_done(act, f"dscan{h}")
                    don_act(act)
                gate_act(act, 2 * l + 1)
                stores_done(act, f"gateB{l}")
                fin_act(act, l)

        @block.vector
        def _(v):
            v.memset(small[:, 0:1], EPS).then_inc(sm("eps"), 1)
            v.wait_ge(sm("const_in"), 16)
            for l in range(2):
                mod_dve(v, l)
                ada_dve(v, l)
                qkv_dve(v, l)
                stores_done(v, f"qkv{l}")
                att_dve(v, l)
                gate_dve(v, 2 * l, oa)
                stores_done(v, f"gateA{l}")
                if l == 0:
                    gla_dve(v)
                    glab_dve(v)
                    stores_done(v, "glab")
                else:
                    ab_dve(v)
                    for h in range(4):
                        pre_dve(v, h)
                        sys_dve(v, h)
                        scan_dve(v, h)
                        stores_done(v, f"dscan{h}")
                    don_dve(v)
                gate_dve(v, 2 * l + 1, ob)
                stores_done(v, f"gateB{l}")
                fin_dve(v, l)


_OUTS = [("y_prompt", (1, T_P, D)), ("y_sample", (1, T_S, D)), ("new_attn_k", (1, 1, T_P, 2, HD)),
         ("new_attn_v", (1, 1, T_P, 2, HD)), ("new_gla_state", (1, 1, 2, 4, 64, 128)),
         ("new_swa_k", (1, 1, T_P, 2, HD)), ("new_swa_v", (1, 1, T_P, 2, HD)),
         ("new_delta_state", (1, 1, 2, 4, 128, 128))]
_INS = ["x_prompt", "x_sample", "c", "cache_attn_k", "cache_attn_v", "state_gla", "cache_swa_k", "cache_swa_v",
        "state_delta", "c_ctx", "w_mod", "b_mod", "g_pre", "g_post", "w_in_even", "w_out_even", "qnorm_a", "knorm_a",
        "gla_gk_up", "gla_gk_bias", "gla_onorm", "w_in_odd", "w_out_odd", "sink_c", "conv_d", "a_log_d", "dt_bias_d",
        "delta_onorm"]


def kernel(**inputs):
    import numpy as _np
    import concourse.bacc as _bacc
    from concourse import mybir as _mybir
    from concourse.bass_utils import run_bass_kernel_spmd as _run

    nc = _bacc.Bacc("TRN2", target_bir_lowering=False, num_devices=1)
    arrays, args = {}, {}
    for name in _INS:
        a = _np.ascontiguousarray(inputs[name])
        arrays[f"in_{name}"] = a
        args[name] = nc.dram_tensor(f"in_{name}", a.shape, _mybir.dt.from_np(a.dtype), kind="ExternalInput").ap()
    arrays["in_consts"] = CONSTS
    args["consts"] = nc.dram_tensor("in_consts", CONSTS.shape, _mybir.dt.float32, kind="ExternalInput").ap()
    for name, shape in _OUTS:
        args[name] = nc.dram_tensor(f"out_{name}", shape, _mybir.dt.float32, kind="ExternalOutput").ap()
    backbone(nc, **args)
    r = _run(nc, [arrays], core_ids=[0])
    return tuple(r.results[0][f"out_{name}"] for name, _ in _OUTS)
```

```python
from contextlib import ExitStack

import numpy as np

import concourse.bass as bass
from concourse import mybir

F32 = mybir.dt.float32
F32R = mybir.dt.float32r
ALU = mybir.AluOpType
ACT = mybir.ActivationFunctionType
AX = mybir.AxisListType

P = 128
D = 1024
KD = D // P
T_S = 1024
T_P = 128
NS = T_S // P
NT = NS + 1
T = T_S + T_P
HD = 64
CH = 64
QW = 512
EPS = 1e-6
BIG = 1e30
EXP_LN = "natural_log_exp_and_others"
DV = 128
NLEV = 6
CTX = NS
PROMPT_KEYS = NS + 1
SLOT = 544
RING = 2

E_Q, E_K, E_V, E_G, E_BQ, E_BV, E_BG = 0, 512, 640, 768, 1280, 1792, 2336
O_Q, O_K, O_V, O_G, O_DQ, O_DK, O_DV, O_AB, O_DG = 0, 512, 640, 768, 1280, 1792, 2304, 2816, 2832


def constant_tables():
    a = np.arange(P)
    row, col = a[:, None], a[None, :]
    same = row // CH == col // CH
    parts, at = [], {}

    def put(name, m):
        at[name] = (sum(x.shape[1] for x in parts), m.shape[1])
        parts.append(m.astype(np.float32))

    put("ident", row == col)
    put("ones", np.ones((P, P)))
    put("upto", np.concatenate([(row <= col) & same, (row >= col) & same], 1))
    put("beyond", np.concatenate([(row > col) & same, (row < col) & same], 1))
    put("inchunk", np.concatenate([(row // CH == c) & (col >= 0) for c in range(2)], 1))
    put("strict", np.concatenate([np.where((row > col) & same, 0, BIG), np.where((row < col) & same, 0, BIG)], 1))
    put("incl", np.concatenate([np.where((row <= col) & same, 0, -BIG), np.where((row >= col) & same, 0, -BIG)], 1))
    for k in range(NLEV):
        s = 2 ** k
        pair = row // (2 * s) == col // (2 * s)
        low = (row // s % 2 == 0) & (col // s % 2 == 1) & pair
        put(f"level{k}", np.concatenate([low, low.T], 1))
    prev, nxt = np.where(col >= row, 0, -BIG), np.where(col <= row, 0, -BIG)
    zero = np.zeros((P, P))
    put("window", np.concatenate([prev, zero, zero, nxt], 1))
    put("windowT", np.concatenate([np.where(row <= col, 0, -BIG), zero, np.where(row >= col, 0, -BIG)], 1))
    put("chunkcol", np.stack([a // CH == c for c in range(2)], 1))
    sel = np.zeros((P, 2 * P))
    sel[0, :P] = 1
    sel[1, P:] = 1
    put("sel", sel)
    tok = np.arange(T_S)
    inv = np.power(np.float32(10000.0), np.arange(16, dtype=np.float32) * np.float32(-2.0 / 32)).astype(np.float32)
    cos, sin = [], []
    for pos in (tok // 64, tok % 64):
        ang = pos.astype(np.float32)[:, None] * inv[None, :]
        cos += [np.cos(ang), np.cos(ang)]
        sin += [-np.sin(ang), np.sin(ang)]
    for name, m in (("cos", cos), ("sin", sin)):
        m = np.concatenate(m, 1).reshape(NS, P, HD).transpose(1, 0, 2).reshape(P, NS * HD)
        put(name, m)
    return np.concatenate(parts, 1), at


CONSTS, CONST_AT = constant_tables()
NCONST = CONSTS.shape[1]


def backbone(nc, x_prompt, x_sample, c, cache_attn_k, cache_attn_v, state_gla, cache_swa_k, cache_swa_v,
             state_delta, c_ctx, w_mod, b_mod, g_pre, g_post, w_in_even, w_out_even, qnorm_a, knorm_a,
             gla_gk_up, gla_gk_bias, gla_onorm, w_in_odd, w_out_odd, sink_c, conv_d, a_log_d, dt_bias_d,
             delta_onorm, consts, y_prompt, y_sample, new_attn_k, new_attn_v, new_gla_state, new_swa_k,
             new_swa_v, new_delta_state):
    ctx = ExitStack()
    with ctx:
        def sb(name, *shape):
            return ctx.enter_context(nc.sbuf_tensor(name, [P, *shape], F32))

        def sem(name):
            return ctx.enter_context(nc.semaphore(name))

        con = sb("con", NCONST)
        hT = sb("hT", KD, T)
        wring = sb("wring", RING, KD * SLOT)
        gg = sb("gg", 2, D)
        mods = sb("mods", 3, KD, 2)
        vecs = sb("vecs", 128)
        vecsT = sb("vecsT", 128)
        sc = sb("sc", 16)
        small = sb("small", 8)
        WORK = (nc.sbuf_bytes_remaining - 1024) // 4
        work_base = (nc.sbuf_base + 31) // 32 * 32
        work = sb("work", WORK)
        ps = ctx.enter_context(nc.psum_tensor("ps", [P, 8, 512], F32))
        yA_dram = nc.dram_tensor("yA_gated", (4, P, T), F32, kind="Internal").ap()
        yB_dram = nc.dram_tensor("yB_gated", (T, QW), F32, kind="Internal").ap()

        def rounded(name, at, n):
            assert at + n <= WORK
            return nc.alloc_sbuf_tensor_at(name, [P, n], F32R, offset=work_base + 4 * at)


        class Region:
            def __init__(self, at=0):
                self.at = at

            def take(self, n):
                a = self.at
                self.at += n
                assert self.at <= WORK, (self.at, WORK)
                return work[:, a:self.at]

        def cst(name, i=0, n=None):
            o, w = CONST_AT[name]
            n = w if n is None else n
            return con[:, o + i * n:o + (i + 1) * n]

        ident, ones = cst("ident"), cst("ones")

        def wslot(i, n):
            return wring[:, i % RING, 0:KD * n].rearrange("p (k n) -> p k n", n=n)

        S = {}

        def sm(name):
            if name not in S:
                S[name] = sem(name)
            return S[name]

        phase_no = {}

        def phase_end(eng):
            n = phase_no.get(id(eng), 0) + 1
            phase_no[id(eng)] = n
            eng.drain().then_inc(sm("phase"), 1)
            eng.wait_ge(sm("phase"), 3 * n)

        def phase_seen(sp, n):
            if n:
                sp.wait_ge(sm("phase"), 3 * n)

        chunks = []
        for l, (w_in, w_out) in enumerate(((w_in_even, w_out_even), (w_in_odd, w_out_odd))):
            def cols(w, a, b):
                return [w[:, a:b].rearrange("(k p) n -> p k n", p=P)]
            chunks += [(f"mod{l}.{j}", cols(w_mod[l], 512 * j, 512 * j + 512), 512) for j in range(6)]
            w = w_in[0]
            if l == 0:
                chunks += [("q0", cols(w, E_Q, E_K), 512), ("kv0", cols(w, E_K, E_G), 256),
                           ("ga0", cols(w, E_G, E_BQ), 512), ("bqk", cols(w, E_BQ, E_BV), 512),
                           ("bvr", cols(w, E_BV, E_BG), 544), ("gb0", cols(w, E_BG, E_BG + 512), 512)]
            else:
                chunks += [("q1", cols(w, O_Q, O_K), 512), ("kv1", cols(w, O_K, O_G), 256),
                           ("ga1", cols(w, O_G, O_DQ), 512), ("ab", cols(w, O_AB, O_DG), 16)]
                for h in range(4):
                    chunks.append((f"dh{h}", cols(w, O_DQ + 128 * h, O_DQ + 128 * h + 128)
                                   + cols(w, O_DK + 128 * h, O_DK + 128 * h + 128)
                                   + cols(w, O_DV + 128 * h, O_DV + 128 * h + 128), 384))
                chunks += [("gb1", cols(w, O_DG, O_DG + 512), 512)]
            chunks += [(f"out{l}.{j}", cols(w_out[0], 512 * j, 512 * j + 512), 512) for j in range(2)]
        chunk_no = {name: i for i, (name, _, _) in enumerate(chunks)}
        chunk_parts = [len(p) for _, p, _ in chunks]

        def weights(pe, name):
            i = chunk_no[name]
            n = sum(chunk_parts[j] for j in range(i % RING, i + 1, RING))
            pe.wait_ge(sm(f"w_loaded{i % RING}"), 16 * n)
            return wslot(i, chunks[i][2])

        gpost_b = Region().take(D)
        gb2 = Region(D).take(D)
        grow = Region(2 * D).take(D)

        def mod_sp(sp, l, n):
            phase_seen(sp, n)
            d = sm("vec_loaded")
            sp.dma_start(vecs[0:24, :], b_mod[l].rearrange("(r p) -> r p", p=P)).then_inc(d, 16)
            sp.dma_start(vecs[24:32, :], g_pre[l].rearrange("(r p) -> r p", p=P)).then_inc(d, 16)
            sp.dma_start(vecs[32:40, :], c[0].rearrange("(r p) -> r p", p=P)).then_inc(d, 16)
            sp.dma_start(vecs[40:48, :], c_ctx.rearrange("(r p) -> r p", p=P)).then_inc(d, 16)
            sp.dma_start(gpost_b, g_post[l].partition_broadcast(P)).then_inc(d, 16)
            sp.dma_start(gb2[0:2, :], b_mod[l, 2 * D:].partition_broadcast(2)).then_inc(d, 16)

        def mod_pe(pe, l):
            pe.wait_ge(sm("vec_loaded"), 96 * (l + 1))
            pe.transpose(ps[:, 0, 0:48], vecs[0:48, :], ident[0:48, 0:48]).then_inc(sm("vecT_ps"), 1)
            pe.wait_ge(sm("cond_silu"), l + 1)
            scv = sc[:, :].rearrange("p (c k) -> p k c", c=2)
            for j in range(4):
                w = weights(pe, f"mod{l}.{j}")
                for b in range(4):
                    o = (4 * j + b) * 2
                    for k in range(KD):
                        mm = pe.matmul(ps[:, 1, o:o + 2], w[:, k, b * P:(b + 1) * P], scv[:, k, :],
                                       start=(k == 0), stop=(k == KD - 1))
                mm.then_inc(sm("w_used"), 1)
            for j in range(2):
                w = weights(pe, f"mod{l}.{4 + j}")
                for k in range(KD):
                    mm = pe.matmul(ps[0:2, 2 + j, :], scv[:, k, :], w[:, k, :], start=(k == 0), stop=(k == KD - 1))
                mm.then_inc(sm("w_used"), 1)
            pe.drain().then_inc(sm("mod_ps"), 1)
            pe.wait_ge(sm("gate_rows"), l + 1)
            for cnd in range(2):
                for j in range(2):
                    mm = pe.matmul(ps[:, 4 + 2 * cnd + j, :], cst("sel", cnd, P)[0:2, :],
                                   grow[0:2, j * 512:(j + 1) * 512], start=True, stop=True)
            mm.then_inc(sm("gate_ps"), 1)
            phase_end(pe)

        def mod_act(act, l):
            act.wait_ge(sm("vecT_ps"), l + 1)
            act.activation(vecsT[:, 0:48], ps[:, 0, 0:48], ACT.Copy)
            act.activation(sc[:, :], ps[:, 0, 32:48], ACT.Silu).then_inc(sm("cond_silu"), 1)
            phase_end(act)

        def mod_dve(v, l):
            v.wait_ge(sm("mod_ps"), l + 1)
            v.wait_ge(sm("cond_silu"), l + 1)
            m = ps[:, 1, 0:32].rearrange("p (m k c) -> p m k c", m=2, c=2)
            for i in range(2):
                bias = vecsT[:, 8 * i:8 * i + 8].unsqueeze(2).to_broadcast([P, 8, 2])
                v.tensor_tensor(mods[:, i, :, :], m[:, i], bias, ALU.add)
            v.drain()
            v.tensor_scalar(mods[:, 2, :, :], mods[:, 1, :, :], 1.0, None, ALU.add)
            v.tensor_tensor(grow[0:2, :].rearrange("p (a n) -> p a n", a=2), ps[0:2, 2:4, :],
                            gb2[0:2, :].rearrange("p (a n) -> p a n", a=2), ALU.add).then_inc(sm("gate_rows"), 1)
            v.drain()
            v.tensor_tensor(mods[:, 1, :, :], mods[:, 2, :, :],
                            vecsT[:, 24:32].unsqueeze(2).to_broadcast([P, 8, 2]), ALU.mult)
            v.wait_ge(sm("gate_ps"), l + 1)
            for cnd in range(2):
                v.tensor_tensor(gg[:, cnd, :].rearrange("p (a n) -> p a n", a=2), ps[:, 4 + 2 * cnd:6 + 2 * cnd, :],
                                gpost_b.rearrange("p (a n) -> p a n", a=2), ALU.mult)
            phase_end(v)

        ar = Region()
        a_x = [ar.take(D) for _ in range(2)]
        a_xh = [ar.take(D) for _ in range(2)]
        a_junk = ar.take(D)
        a_st = ar.take(8)

        def x_rows(l, t):
            if l == 0:
                return x_prompt[0] if t == NS else x_sample[0, t * P:(t + 1) * P, :]
            return y_prompt[0] if t == NS else y_sample[0, t * P:(t + 1) * P, :]

        def ada_sp(sp, l, n):
            phase_seen(sp, n)
            for t in range(NT):
                if t >= 2:
                    sp.wait_ge(sm("xh_done"), NT * l + t - 1)
                sp.dma_start(a_x[t % 2], x_rows(l, t)).then_inc(sm(f"x_loaded{t % 2}"), 16)

        def x_load_count(l, t):
            per = [(NT + 1) // 2, NT // 2][t % 2]
            return 16 * (per * l + t // 2 + 1)

        def ada_act(act, l):
            for t in range(NT):
                act.wait_ge(sm(f"x_loaded{t % 2}"), x_load_count(l, t))
                if t >= 1:
                    act.wait_ge(sm("xh_done"), NT * l + t)
                act.activation(a_junk, a_x[t % 2], ACT.Square, accum_out=a_st[:, 0:1])
                act.drain()
                act.activation(a_st[:, 1:2], a_st[:, 0:1], ACT.Ln, scale=1.0 / D, bias=eps_col)
                act.drain()
                act.activation(a_st[:, 2:3], a_st[:, 1:2], ACT.Exp, scale=-0.5).then_inc(sm("x_rs"), 1)
                if t >= 1:
                    ada_evac_act(act, l, t - 1)
            ada_evac_act(act, l, NT - 1)
            phase_end(act)

        def ada_evac_act(act, l, t):
            act.wait_ge(sm("xT_ps"), NT * l + t + 1)
            cnd = int(t == NS)
            for k in range(4, KD):
                mm = act.activation(hT[:, k, t * P:(t + 1) * P], ps[:, 2 * (t % 2) + 1, (k - 4) * P:(k - 3) * P],
                                    ACT.Identity, scale=mods[:, 1, k, cnd:cnd + 1], bias=mods[:, 0, k, cnd:cnd + 1])
            mm.then_inc(sm("hT_act"), 1)

        def ada_dve(v, l):
            for t in range(NT):
                v.wait_ge(sm("x_rs"), NT * l + t + 1)
                if t >= 2:
                    v.wait_ge(sm("xT_ps"), NT * l + t - 1)
                v.tensor_scalar(a_xh[t % 2], a_x[t % 2], a_st[:, 2:3], None, ALU.mult).then_inc(sm("xh_done"), 1)
                if t >= 1:
                    ada_evac_dve(v, l, t - 1)
            ada_evac_dve(v, l, NT - 1)
            phase_end(v)

        def ada_evac_dve(v, l, t):
            v.wait_ge(sm("xT_ps"), NT * l + t + 1)
            cnd = int(t == NS)
            for k in range(4):
                mm = v.tensor_scalar(hT[:, k, t * P:(t + 1) * P], ps[:, 2 * (t % 2) + k // 4, (k % 4) * P:(k % 4 + 1) * P],
                                     mods[:, 1, k, cnd:cnd + 1], mods[:, 0, k, cnd:cnd + 1], ALU.mult, ALU.add)
            mm.then_inc(sm("hT_dve"), 1)

        def ada_pe(pe, l):
            for t in range(NT):
                pe.wait_ge(sm("xh_done"), NT * l + t + 1)
                if t >= 2:
                    pe.wait_ge(sm("hT_act"), NT * l + t - 1)
                    pe.wait_ge(sm("hT_dve"), NT * l + t - 1)
                for k in range(KD):
                    mm = pe.transpose(ps[:, 2 * (t % 2) + k // 4, (k % 4) * P:(k % 4 + 1) * P],
                                      a_xh[t % 2][:, k * P:(k + 1) * P], ident)
                mm.then_inc(sm("xT_ps"), 1)
            phase_end(pe)

        R65 = slice(0, HD + 1)
        qr = Region()
        qT = qr.take(4 * T).rearrange("p (j t) -> p j t", j=4)
        kaug = qr.take(2 * 10 * P).rearrange("p (g n) -> p g n", g=2)
        vaug = qr.take(2 * 10 * P).rearrange("p (g t n) -> p g t n", g=2, n=P)
        yA = qr.take(4 * T).rearrange("p (b t) -> p b t", b=4)
        at_rounded = qr.at
        qTr = rounded("qTr", at_rounded, 4 * T)[:, :].rearrange("p (j t) -> p j t", j=4)
        kTr = rounded("kTr", at_rounded + 4 * T, 2 * 10 * P)[:, :].rearrange("p (g n) -> p g n", g=2)
        qr.at += 4 * T + 2 * 10 * P
        at_qkv = qr.at
        q_sq = qr.take(640)
        q_n = [qr.take(640) for _ in range(2)]
        q_t1 = qr.take(640)
        q_t2 = qr.take(640)
        q_r = [qr.take(640) for _ in range(2)]
        q_st = qr.take(32)
        ck = qr.take(P)
        wqk = qr.take(128)
        ar2 = Region(at_qkv)
        qaug = [ar2.take(T) for _ in range(2)]
        ES = slice(96, 97)
        pT = [ar2.take(512) for _ in range(3)]
        ssb = ar2.take(512)
        a_mx = ar2.take(2)
        a_nm = [ar2.take(NT) for _ in range(2)]
        a_ri = [ar2.take(512) for _ in range(2)]
        sinks = ar2.take(16)
        sumrow = ar2.take(P)

        def heads(ap, g=2):
            return ap.rearrange("p (g j d) -> p g j d", g=g, d=HD)

        def qkv_sp(sp, l, n):
            phase_seen(sp, n)
            d = sm("qkv_in")
            kc, vc = ((cache_attn_k, cache_attn_v), (cache_swa_k, cache_swa_v))[l]
            sp.dma_start(ck, kc[0, 0].rearrange("t g d -> t (g d)")).then_inc(d, 16)
            sp.dma_start(vaug[:, :, CTX, 0:HD], vc[0, 0]).then_inc(d, 16)
            if l == 0:
                sp.dma_start(wqk[:, 0:HD], qnorm_a[0].partition_broadcast(P)).then_inc(d, 16)
                sp.dma_start(wqk[:, HD:2 * HD], knorm_a[0].partition_broadcast(P)).then_inc(d, 16)
            ko, vo = ((new_attn_k, new_attn_v), (new_swa_k, new_swa_v))[l]
            sp.wait_ge(sm("qkr_done"), NT * (l + 1))
            sp.dma_start(ko[0, 0].rearrange("t g d -> t (g d)"), q_r[NS % 2][:, 512:640]).then_inc(sm("kv_stored"), 16)
            sp.wait_ge(sm("v_done"), NT * (l + 1))
            sp.dma_start(vo[0, 0], vaug[:, :, PROMPT_KEYS, 0:HD]).then_inc(sm("kv_stored"), 16)
            sp.wait_ge(sm("kv_stored"), 32 * (l + 1))
            sp.sem_inc(sm("phase_sp"), 1)

        def qkv_in_count(l):
            return (64, 96)[l]

        def qkv_pe(pe, l):
            wq, wkv = weights(pe, f"q{l}"), weights(pe, f"kv{l}")
            pe.wait_ge(sm("qkv_in"), qkv_in_count(l))
            for t in range(NT + 1):
                if t < NT:
                    if t >= 2:
                        pe.wait_ge(sm("qk_free"), NT * l + t - 1)
                        pe.wait_ge(sm("v_done"), NT * l + t - 1)
                    for w, b, n in ((wq, 0, 512), (wkv, 1, 256)):
                        for k in range(KD):
                            mm = pe.matmul(ps[:, 2 * (t % 2) + b, 0:n], hT[:, k, t * P:(t + 1) * P], w[:, k, :],
                                           start=(k == 0), stop=(k == KD - 1))
                    mm.then_inc(sm("qkv_ps"), 1)
                    if t == NT - 1:
                        pe.drain().then_inc(sm("w_used"), 2)
                if t == 0:
                    pe.transpose(ps[:, 7, 128:256], ck, ident).then_inc(sm("ckT_ps"), 1)
                if t >= 1:
                    u = t - 1
                    pe.wait_ge(sm("qkr_done"), NT * l + u + 1)
                    if u >= 2:
                        pe.wait_ge(sm("qkT_done"), NT * l + u - 1)
                    if u == 1:
                        pe.wait_ge(sm("ckT_done"), l + 1)
                    r = q_r[u % 2]
                    for j in range(5):
                        mm = pe.transpose(ps[:, 4 + 2 * (u % 2) + j // 4, (j % 4) * P:(j % 4 + 1) * P],
                                          r[:, j * P:(j + 1) * P], ident)
                    mm.then_inc(sm("qkT_ps"), 1)
            phase_end(pe)

        def keys_out(act, src, tile):
            cols = slice(tile * P, (tile + 1) * P)
            for g in range(2):
                half = slice(HD * g, HD * g + HD)
                act.activation(kTr[half, g, cols], src[half, :], ACT.Copy)
            act.activation(kaug[0:HD, 0, cols], src[0:HD, :], ACT.Copy)
            return act.activation(kaug[0:HD, 1, cols], src[HD:P, :], ACT.Copy)

        def qkv_act(act, l):
            act.wait_ge(sm("ckT_ps"), l + 1)
            keys_out(act, ps[:, 7, 128:256], CTX).then_inc(sm("ckT_done"), 1)
            for t in range(NT + 1):
                if t < NT:
                    a, b = ps[:, 2 * (t % 2), :], ps[:, 2 * (t % 2) + 1, :]
                    act.wait_ge(sm("qkv_ps"), NT * l + t + 1)
                    if l == 0:
                        if t >= 1:
                            act.wait_ge(sm("qk_ss"), t)
                        act.activation(q_sq[:, 0:512], a, ACT.Square)
                        act.activation(q_sq[:, 512:640], b[:, 0:128], ACT.Square).then_inc(sm("qk_sq"), 1)
                    if l == 1:
                        act.wait_ge(sm("qk_free"), NT * l + t + 1)
                    vdst = PROMPT_KEYS if t == NS else t
                    act.activation(vaug[:, :, vdst, 0:HD], b[:, 128:256].rearrange("p (g d) -> p g d", g=2), ACT.Copy).then_inc(sm("v_done"), 1)
                    if l == 0:
                        act.wait_ge(sm("qk_ss"), t + 1)
                        if t >= 1:
                            act.wait_ge(sm("qk_free"), t)
                        act.activation(q_st[:, 10:20], q_st[:, 0:10], ACT.Ln, scale=1.0 / HD, bias=eps_col)
                        act.drain()
                        act.activation(q_st[:, 20:30], q_st[:, 10:20], ACT.Exp, scale=-0.5).then_inc(sm("qk_rs"), 1)
                if t >= 1:
                    u = t - 1
                    act.wait_ge(sm("qkT_ps"), NT * l + u + 1)
                    bk = 4 + 2 * (u % 2)
                    src = ps[:, bk, :].rearrange("p (j t) -> p j t", j=4)
                    act.activation(qT[:, :, u * P:(u + 1) * P], src, ACT.Copy)
                    act.activation(qTr[:, :, u * P:(u + 1) * P], src, ACT.Copy)
                    keys_out(act, ps[:, bk + 1, 0:P], PROMPT_KEYS if u == NS else u).then_inc(sm("qkT_done"), 1)
            phase_end(act)

        def qkv_dve(v, l):
            v.memset(vaug[:, :, :, HD:P], 1.0)
            v.memset(kaug[HD:HD + 1, :, :], 1.0)
            for g in range(2):
                other = slice(HD * (1 - g), HD * (1 - g) + HD)
                v.memset(kTr[other, g, :].bitcast(F32), 0.0)
            v.wait_ge(sm("qkv_in"), qkv_in_count(l))
            for t in range(NT):
                a, b = ps[:, 2 * (t % 2), :], ps[:, 2 * (t % 2) + 1, 0:128]
                n, r = q_n[t % 2], q_r[t % 2]
                if l == 0:
                    v.wait_ge(sm("qk_sq"), t + 1)
                    if t >= 1:
                        v.wait_ge(sm("qk_rs"), t)
                    v.tensor_reduce(q_st[:, 0:10], q_sq.rearrange("p (h d) -> p h d", d=HD), AX.X, ALU.add).then_inc(sm("qk_ss"), 1)
                    v.wait_ge(sm("qk_rs"), t + 1)
                    rsb = q_st[:, 20:30].unsqueeze(2).to_broadcast([P, 10, HD])
                    v.tensor_tensor(q_t1[:, 0:512].rearrange("p (h d) -> p h d", d=HD), a.rearrange("p (h d) -> p h d", d=HD), rsb[:, 0:8, :], ALU.mult)
                    v.tensor_tensor(q_t1[:, 512:640].rearrange("p (h d) -> p h d", d=HD), b.rearrange("p (h d) -> p h d", d=HD), rsb[:, 8:10, :], ALU.mult).then_inc(sm("qk_free"), 1)
                    v.drain()
                    for o, m, w in ((0, 8, wqk[:, 0:HD]), (512, 2, wqk[:, HD:2 * HD])):
                        v.tensor_tensor(n[:, o:o + m * HD].rearrange("p (h d) -> p h d", d=HD),
                                        q_t1[:, o:o + m * HD].rearrange("p (h d) -> p h d", d=HD),
                                        w.unsqueeze(1).to_broadcast([P, m, HD]), ALU.mult)
                    v.drain()
                else:
                    v.wait_ge(sm("qkv_ps"), NT * l + t + 1)
                    v.tensor_copy(n[:, 0:512], a)
                    v.tensor_copy(n[:, 512:640], b).then_inc(sm("qk_free"), 1)
                    v.drain()
                if t >= 2:
                    v.wait_ge(sm("qkT_ps"), NT * l + t - 1)
                rq = r[:, 0:512].rearrange("p (j g d) -> p g j d", g=2, d=HD)
                if t == NS:
                    for g in range(2):
                        v.tensor_copy(rq[:, g], heads(n[:, 0:512])[:, g])
                    v.tensor_copy(r[:, 512:640], n[:, 512:640]).then_inc(sm("qkr_done"), 1)
                else:
                    cosb = cst("cos", t, HD).unsqueeze(1).to_broadcast([P, 10, HD])
                    sinb = cst("sin", t, HD)
                    v.tensor_tensor(q_t1.rearrange("p (h d) -> p h d", d=HD), n.rearrange("p (h d) -> p h d", d=HD), cosb, ALU.mult)
                    nh = n.rearrange("p (h a s f) -> p h a s f", a=2, s=2, f=16)
                    th = q_t2.rearrange("p (h a s f) -> p h a s f", a=2, s=2, f=16)
                    sh = sinb.rearrange("p (a s f) -> p a s f", a=2, s=2)
                    for s in range(2):
                        v.tensor_tensor(th[:, :, :, s, :], nh[:, :, :, 1 - s, :],
                                        sh[:, :, s, :].unsqueeze(1).to_broadcast([P, 10, 2, 16]), ALU.mult)
                    v.drain()
                    for g in range(2):
                        v.tensor_tensor(rq[:, g], heads(q_t1[:, 0:512])[:, g], heads(q_t2[:, 0:512])[:, g], ALU.add)
                    v.tensor_tensor(r[:, 512:640], q_t1[:, 512:640], q_t2[:, 512:640], ALU.add).then_inc(sm("qkr_done"), 1)
            phase_end(v)

        def key_tiles(l, b):
            if b == NS:
                return [PROMPT_KEYS]
            if l == 0:
                return list(range(NS + 1))
            return ([b - 1] if b > 0 else []) + [b, CTX] + ([b + 1] if b < NS - 1 else [])

        CHUNKS = [(0, 4), (4, 8), (8, 9)]

        def products(l):
            out = []
            for h in range(8):
                for c_, (qa, qb) in enumerate(CHUNKS):
                    if c_ == 2:
                        of = [(PROMPT_KEYS, qa, qb)]
                    elif l == 0:
                        of = [(k, qa, qb) for k in range(NS + 1)]
                    else:
                        of = [(CTX, qa, qb)] + [(k, max(k - 1, qa), min(k + 2, qb)) for k in range(max(qa - 1, 0), min(qb + 1, NS))]
                    out += [(h, k, a, b, c_, i == 0, i == len(of) - 1) for i, (k, a, b) in enumerate(of)]
            return out

        PRODUCTS = [products(l) for l in range(2)]
        AHEAD = [1, 2]
        ST_BANKS = [(3, 4), (1, 2, 3, 4)]
        MAX_AT = [lambda i: [i] if i < NT else [], lambda i: [i] if i < NT else []]

        def att_steps(l):
            items = PRODUCTS[l]
            per = len(items) // 8
            for u in range(NT):
                yield "max", 0, u
            for r in range(3):
                yield "row", 0, r
            for i in range(len(items) + AHEAD[l]):
                if i < len(items):
                    h, p = i // per, i % per
                    yield "scores", i, 0
                    if h < 7:
                        if p < NT:
                            yield "max", h + 1, p
                        if NT < p <= NT + 3:
                            yield "row", h + 1, p - NT - 1
                if i >= AHEAD[l]:
                    yield "values", i - AHEAD[l], 0
                    if items[i - AHEAD[l]][6]:
                        yield "out", items[i - AHEAD[l]][0], items[i - AHEAD[l]][4]

        def last_product(l, h, c_=2):
            return max(i for i, x in enumerate(PRODUCTS[l]) if x[0] == h and x[4] == c_)

        def masked(l, i):
            h, kt, qa, qb, c_, _, _ = PRODUCTS[l][i]
            return l == 1 and kt not in (CTX, PROMPT_KEYS)

        def masks_before(l, i):
            return sum(masked(l, j) for j in range(i)) if l else 0

        def att_sp(sp, l, n):
            if l == 1:
                phase_seen(sp, n)
                sp.dma_start(sinks[:, 0:8], sink_c[0].partition_broadcast(P)).then_inc(sm("sink_in"), 16)

        ROW_TILES = [(0, 4), (4, 8), (8, 9)]

        def att_pe(pe, l):
            base = l * len(PRODUCTS[0])
            for what, x, y in att_steps(l):
                if what == "max":
                    h, u = x, y
                    g, j = h // 4, h % 4
                    n = 72 * l + 9 * h + u
                    if n > 72 * l:
                        pe.wait_ge(sm("nm_done"), n)
                    if u == 0 and h:
                        pe.wait_ge(sm("row_out"), 3 * (8 * l + h))
                    tiles = key_tiles(l, u)
                    q = qTr[:, j, u * P:(u + 1) * P]
                    i = 0
                    while i < len(tiles):
                        m = 1
                        while i + m < len(tiles) and tiles[i + m] == tiles[i] + m and (i % 4) + m < 4:
                            m += 1
                        mm = pe.matmul(ps[:, i // 4, (i % 4) * P:(i % 4 + m) * P], q,
                                       kTr[:, g, tiles[i] * P:(tiles[i] + m) * P], start=True, stop=True)
                        i += m
                    mm.then_inc(sm("mx_ps"), 1)
                elif what == "row":
                    h, r = x, y
                    pe.wait_ge(sm("nm_done"), 72 * l + 9 * h + 9)
                    if r:
                        pe.wait_ge(sm("row_out"), 3 * (8 * l + h) + r)
                    for t in range(*ROW_TILES[r]):
                        mm = pe.matmul(ps[HD:HD + 1, 0, (t - ROW_TILES[r][0]) * P:(t - ROW_TILES[r][0] + 1) * P],
                                       a_nm[h % 2][:, t:t + 1], ident, start=True, stop=True)
                    mm.then_inc(sm("row_ps"), 1)
                elif what == "scores":
                    i = x
                    h, kt, qa, qb, c_, first, last = PRODUCTS[l][i]
                    nb = len(ST_BANKS[l])
                    if first and c_ == 0:
                        pe.wait_ge(sm("row_out"), 3 * (8 * l + h) + 3)
                    if i >= nb:
                        pe.wait_ge(sm("p_done"), base + i - nb + 1)
                    pe.matmul(ps[:, ST_BANKS[l][i % nb], 0:(qb - qa) * P], kaug[R65, h // 4, kt * P:(kt + 1) * P],
                              qaug[h % 2][R65, qa * P:qb * P], start=True, stop=True).then_inc(sm("s_ps"), 1)
                elif what == "values":
                    i = x
                    h, kt, qa, qb, c_, first, last = PRODUCTS[l][i]
                    q0, q1 = CHUNKS[c_]
                    if first and h:
                        pe.wait_ge(sm("y_done"), 3 * (8 * l + h - 1) + c_ + 1)
                    pe.wait_ge(sm("p_done"), base + i + 1)
                    if first and l == 1:
                        pe.matmul(ps[:, 5 + c_, 0:(q1 - q0) * P], sumrow[ES, :], qaug[h % 2][ES, q0 * P:q1 * P],
                                  start=True, stop=False, skip_group_check=True)
                    pe.matmul(ps[:, 5 + c_, (qa - q0) * P:(qb - q0) * P], vaug[:, h // 4, kt, :],
                              pT[i % 3][:, 0:(qb - qa) * P], start=(first and l == 0), stop=last,
                              skip_group_check=True).then_inc(sm("pv_ps"), 1)
            phase_end(pe)

        def att_dve(v, l):
            v.memset(sumrow[ES, 0:HD], 0.0)
            v.memset(sumrow[ES, HD:P], 1.0)
            base = l * len(PRODUCTS[0])
            if l == 1:
                v.wait_ge(sm("sink_in"), 16)
                v.tensor_scalar(sinks[:, 8:16], sinks[:, 0:8], -8.0, None, ALU.mult)
            v.drain()
            for what, x, y in att_steps(l):
                if what == "max":
                    h, u = x, y
                    n = 72 * l + 9 * h + u
                    v.wait_ge(sm("mx_ps"), n + 1)
                    if u == 0 and h >= 2:
                        v.wait_ge(sm("row_ps"), 3 * (8 * l + h - 1))
                    m = len(key_tiles(l, u)) * P
                    src = ps[:, 0:3, :].rearrange("p a n -> p (a n)")[:, 0:m]
                    if l == 1:
                        if u == NS:
                            v.tensor_copy(ssb[:, 0:m], src)
                        else:
                            o = 0 if u > 0 else 1
                            v.tensor_tensor(ssb[:, 0:m], src, cst("window")[:, o * P:o * P + m], ALU.add)
                        v.drain()
                        src = ssb[:, 0:m]
                    v.tensor_reduce(a_mx[:, 0:1], src, AX.X, ALU.max)
                    v.drain()
                    if l == 0:
                        v.tensor_scalar(a_nm[h % 2][:, u:u + 1], a_mx[:, 0:1], -1.0, None, ALU.mult)
                    else:
                        v.tensor_scalar(a_nm[h % 2][:, u:u + 1], a_mx[:, 0:1], -1.0, sinks[:, 8 + h:9 + h], ALU.mult, ALU.min)
                    v.drain().then_inc(sm("nm_done"), 1)
                elif what == "scores" and masked(l, x):
                    _, kt, qa, qb, _, _, _ = PRODUCTS[l][x]
                    v.wait_ge(sm("s_ps"), base + x + 1)
                    s = ps[:, ST_BANKS[l][x % len(ST_BANKS[l])], 0:(qb - qa) * P]
                    o = qa - (kt - 1)
                    v.tensor_tensor(s, s, cst("windowT")[:, o * P:(o + qb - qa) * P], ALU.add).then_inc(sm("masked"), 1)
                elif what == "out":
                    h, c_ = x, y
                    q0, q1 = CHUNKS[c_]
                    v.wait_ge(sm("ri_done"), 3 * (8 * l + h) + c_ + 1)
                    v.tensor_tensor(yA[HD * (h % 2):HD * (h % 2) + HD, h // 2, q0 * P:q1 * P], ps[0:HD, 5 + c_, 0:(q1 - q0) * P],
                                    a_ri[(3 * h + c_) % 2][0:HD, 0:(q1 - q0) * P], ALU.mult).then_inc(sm("y_done"), 1)
            phase_end(v)

        def att_act(act, l):
            base = l * len(PRODUCTS[0])
            if l == 1:
                act.wait_ge(sm("sink_in"), 16)
            for what, x, y in att_steps(l):
                if what == "row":
                    h, r = x, y
                    if r == 0:
                        if h >= 2:
                            act.wait_ge(sm("pv_ps"), base + last_product(l, h - 2) + 1)
                        act.activation(qaug[h % 2][0:HD, :], qT[HD * (h // 4):HD * (h // 4) + HD, h % 4, :], ACT.Copy)
                    act.wait_ge(sm("row_ps"), 3 * (8 * l + h) + r + 1)
                    t0, t1 = ROW_TILES[r]
                    row = ps[HD:HD + 1, 0, 0:(t1 - t0) * P]
                    mm = act.activation(qaug[h % 2][HD:HD + 1, t0 * P:t1 * P], row, ACT.Copy)
                    if l == 1:
                        mm = act.activation(qaug[h % 2][ES, t0 * P:t1 * P], row, ACT.Exp, scale=0.125, bias=sinks[HD:HD + 1, h:h + 1])
                    mm.then_inc(sm("row_out"), 1)
                elif what == "scores":
                    i = x
                    _, kt, qa, qb, _, _, _ = PRODUCTS[l][i]
                    if masked(l, i):
                        act.wait_ge(sm("masked"), masks_before(l, i) + 1)
                    else:
                        act.wait_ge(sm("s_ps"), base + i + 1)
                    if i >= 3:
                        act.wait_ge(sm("pv_ps"), base + i - 2)
                    n = (qb - qa) * P
                    act.activation(pT[i % 3][:, 0:n], ps[:, ST_BANKS[l][i % len(ST_BANKS[l])], 0:n], ACT.Exp, scale=0.125).then_inc(sm("p_done"), 1)
                elif what == "out":
                    h, c_ = x, y
                    n = 3 * (8 * l + h) + c_
                    m = (CHUNKS[c_][1] - CHUNKS[c_][0]) * P
                    act.wait_ge(sm("pv_ps"), base + last_product(l, h, c_) + 1)
                    if n >= 2:
                        act.wait_ge(sm("y_done"), n - 1)
                    act.drain()
                    act.activation(a_ri[(3 * h + c_) % 2][HD:P, 0:m], ps[HD:P, 5 + c_, 0:m], ACT.Ln)
                    act.drain()
                    act.activation(a_ri[(3 * h + c_) % 2][0:HD, 0:m], a_ri[(3 * h + c_) % 2][HD:P, 0:m], ACT.Exp, scale=-1.0).then_inc(sm("ri_done"), 1)
            phase_end(act)

        gr_ = Region(WORK - 2200)
        g_sl = [gr_.take(QW) for _ in range(2)]
        g_y = [gr_.take(QW) for _ in range(2)]
        TOKENS = [(0, 512), (512, 512), (T_S, T_P)]

        def gateA_pe(pe, l):
            w = weights(pe, f"ga{l}")
            for n in range(12):
                b, (o, m) = n // 3, TOKENS[n % 3]
                if n >= 2:
                    pe.wait_ge(sm("gA_silu"), 12 * l + n - 1)
                for k in range(KD):
                    mm = pe.matmul(ps[:, n % 2, 0:m], w[:, k, b * P:(b + 1) * P], hT[:, k, o:o + m], start=(k == 0), stop=(k == KD - 1))
                mm.then_inc(sm("gA_mm"), 1)
            pe.drain().then_inc(sm("w_used"), 1)
            phase_end(pe)

        def gateA_act(act, l):
            for n in range(12):
                m = TOKENS[n % 3][1]
                act.wait_ge(sm("gA_mm"), 12 * l + n + 1)
                if n >= 2:
                    act.wait_ge(sm("gA_done"), 12 * l + n - 1)
                act.activation(g_sl[n % 2][:, 0:m], ps[:, n % 2, 0:m], ACT.Silu).then_inc(sm("gA_silu"), 1)
            phase_end(act)

        def gateA_dve(v, l):
            for n in range(12):
                b, (o, m) = n // 3, TOKENS[n % 3]
                v.wait_ge(sm("gA_silu"), 12 * l + n + 1)
                y = yA[:, b, o:o + m]
                v.tensor_tensor(y, g_sl[n % 2][:, 0:m], y, ALU.mult).then_inc(sm("gA_done"), 1)
            phase_end(v)

        def gateA_sp(sp, l):
            for b in range(4):
                sp.wait_ge(sm("gA_done"), 12 * l + 3 * b + 3)
                sp.dma_start(yA_dram[b], yA[:, b, :]).then_inc(sm("yA_stored"), 16)
            sp.wait_ge(sm("yA_stored"), 64 * (l + 1))
            sp.sem_inc(sm("phase_sp"), 1)

        def gate_pe(pe, l):
            w = weights(pe, f"gb{l}")
            for t in range(NT):
                if t >= 2:
                    pe.wait_ge(sm("gate_silu"), NT * l + t - 1)
                for k in range(KD):
                    mm = pe.matmul(ps[:, t % 2, :], hT[:, k, t * P:(t + 1) * P], w[:, k, :], start=(k == 0), stop=(k == KD - 1))
                mm.then_inc(sm("gate_mm"), 1)
            pe.drain().then_inc(sm("w_used"), 1)
            phase_end(pe)

        def gate_act(act, l):
            for t in range(NT):
                act.wait_ge(sm("gate_mm"), NT * l + t + 1)
                if t >= 2:
                    act.wait_ge(sm("gated"), NT * l + t - 1)
                act.activation(g_sl[t % 2], ps[:, t % 2, :], ACT.Silu).then_inc(sm("gate_silu"), 1)
            phase_end(act)

        def gate_dve(v, l):
            for t in range(NT):
                v.wait_ge(sm("gate_silu"), NT * l + t + 1)
                if t >= 2:
                    v.wait_ge(sm(f"ym_stored{t % 2}"), ym_count(l, t - 2))
                v.tensor_tensor(g_y[t % 2], g_sl[t % 2], ob[:, t, :], ALU.mult).then_inc(sm("gated"), 1)
            phase_end(v)

        def ym_count(l, t):
            per = [(NT + 1) // 2, NT // 2][t % 2]
            return 16 * (per * l + t // 2 + 1)

        def gate_sp(sp, l):
            for t in range(NT):
                sp.wait_ge(sm("gated"), NT * l + t + 1)
                sp.dma_start(yB_dram[t * P:(t + 1) * P, :], g_y[t % 2]).then_inc(sm(f"ym_stored{t % 2}"), 16)
            sp.wait_ge(sm("ym_stored0"), ym_count(l, NT - 1))
            sp.wait_ge(sm("ym_stored1"), ym_count(l, NT - 2))
            sp.sem_inc(sm("phase_sp"), 1)

        fr = Region()
        NF = 3
        f_y = [fr.take(QW) for _ in range(NF)]
        f_x = [fr.take(D) for _ in range(NF)]
        f_yT = [fr.take(D) for _ in range(NF)]
        f_z = [fr.take(D) for _ in range(2)]
        f_o = [fr.take(D) for _ in range(2)]
        f_junk = fr.take(D)
        f_st = fr.take(8)

        def fin_sp(sp, l, n):
            phase_seen(sp, n)
            for t in range(NT + 2):
                if t < NT:
                    if t >= NF:
                        sp.wait_ge(sm("z_ps"), NT * l + t - NF + 1)
                        sp.wait_ge(sm("res_done"), NT * l + t - NF + 1)
                    d = sm(f"f_loaded{t % NF}")
                    sp.dma_start(f_yT[t % NF][:, 0:QW].rearrange("p (b n) -> p b n", b=4),
                                 yA_dram[:, :, t * P:(t + 1) * P].rearrange("b p n -> p b n")).then_inc(d, 16)
                    sp.dma_start(f_y[t % NF], yB_dram[t * P:(t + 1) * P, :]).then_inc(d, 16)
                    sp.dma_start(f_x[t % NF], x_rows(l, t)).then_inc(d, 16)
                if t >= 2:
                    u = t - 2
                    sp.wait_ge(sm("res_done"), NT * l + u + 1)
                    sp.dma_start(x_rows(1, u), f_o[u % 2]).then_inc(sm(f"y_stored{u % 2}"), 16)
            for u in (NT - 1, NT - 2):
                sp.wait_ge(sm(f"y_stored{u % 2}"), ym_count(l, u))

        def f_count(l, t):
            return 48 * (NT // NF * l + t // NF + 1)

        def fin_pe(pe, l):
            w = [weights(pe, f"out{l}.{j}") for j in range(2)]

            def turn(t):
                pe.wait_ge(sm(f"f_loaded{t % NF}"), f_count(l, t))
                if t >= 2:
                    pe.wait_ge(sm("yT_done"), NT * l + t - 1)
                for k in range(4):
                    mm = pe.transpose(ps[:, t % 2, k * P:(k + 1) * P], f_y[t % NF][:, k * P:(k + 1) * P], ident)
                mm.then_inc(sm("yT_ps"), 1)

            turn(0)
            for t in range(NT):
                if t < NT - 1:
                    turn(t + 1)
                pe.wait_ge(sm("yT_done"), NT * l + t + 1)
                if t >= 3:
                    pe.wait_ge(sm("z_free"), NT * l + t - 2)
                for j in range(2):
                    for k in range(KD):
                        mm = pe.matmul(ps[:, 2 + 2 * (t % 3) + j, :], f_yT[t % NF][:, k * P:(k + 1) * P], w[j][:, k, :],
                                       start=(k == 0), stop=(k == KD - 1))
                mm.then_inc(sm("z_ps"), 1)
            pe.drain().then_inc(sm("w_used"), 2)
            phase_end(pe)

        def fin_act(act, l):
            for t in range(NT + 1):
                if t < NT:
                    act.wait_ge(sm("yT_ps"), NT * l + t + 1)
                    act.activation(f_yT[t % NF][:, QW:D], ps[:, t % 2, :], ACT.Copy).then_inc(sm("yT_done"), 1)
                if t >= 1:
                    u = t - 1
                    b = 2 + 2 * (u % 3)
                    act.wait_ge(sm("z_ps"), NT * l + u + 1)
                    if u >= 1:
                        act.wait_ge(sm("z_free"), NT * l + u)
                    act.drain()
                    act.activation(f_junk.rearrange("p (a n) -> p a n", a=2), ps[:, b:b + 2, :], ACT.Square, accum_out=f_st[:, 0:1])
                    act.drain()
                    act.activation(f_st[:, 1:2], f_st[:, 0:1], ACT.Ln, scale=1.0 / D, bias=eps_col)
                    act.drain()
                    act.activation(f_st[:, 2:3], f_st[:, 1:2], ACT.Exp, scale=-0.5).then_inc(sm("z_rs"), 1)
            phase_end(act)

        def fin_dve(v, l):
            for t in range(NT):
                cnd = int(t == NS)
                b = 2 + 2 * (t % 3)
                v.wait_ge(sm("z_rs"), NT * l + t + 1)
                v.wait_ge(sm(f"f_loaded{t % NF}"), f_count(l, t))
                if t >= 2:
                    v.wait_ge(sm("res_done"), NT * l + t - 1)
                v.scalar_tensor_tensor(f_z[t % 2].rearrange("p (a n) -> p a n", a=2), ps[:, b:b + 2, :], f_st[:, 2:3],
                                       gg[:, cnd, :].rearrange("p (a n) -> p a n", a=2), ALU.mult, ALU.mult).then_inc(sm("z_free"), 1)
                v.drain()
                if t >= 2:
                    v.wait_ge(sm(f"y_stored{t % 2}"), ym_count(l, t - 2))
                v.tensor_tensor(f_o[t % 2], f_z[t % 2], f_x[t % NF], ALU.add).then_inc(sm("res_done"), 1)
            phase_end(v)

        GN = 512
        lr = Region()
        ob = lr.take(NT * QW).rearrange("p (t n) -> p t n", n=QW)
        l_v = lr.take(NT * QW).rearrange("p (t n) -> p t n", n=QW)
        l_qb = lr.take(NT * 256).rearrange("p (t n) -> p t n", n=256)
        l_kb = lr.take(NT * 256).rearrange("p (t n) -> p t n", n=256)
        l_dec = lr.take(NT * 8).rearrange("p (t n) -> p t n", n=8)
        l_up = lr.take(GN)
        l_rT = lr.take(P)
        l_abs = lr.take(GN)
        l_e = lr.take(GN)
        l_ln = lr.take(GN)
        l_g = lr.take(GN)
        l_ex = [lr.take(GN) for _ in range(3)]
        l_q = lr.take(GN)
        l_k = lr.take(GN)
        l_kf = lr.take(256)
        l_qT = lr.take(GN)
        l_kT = lr.take(GN)
        l_at = [lr.take(GN) for _ in range(2)]
        l_att = lr.take(GN)
        l_S = [[lr.take(256) for _ in range(3)] for _ in range(2)]
        l_on = lr.take(P)
        l_sq = lr.take(GN)
        l_st = lr.take(12)

        def gla_tiles(direction):
            return list(range(NS)) + [NS] if direction == 0 else list(range(NS))[::-1] + [NS]

        def state_view(ap, i):
            return ap[0, 0, i].rearrange("(r two) k v -> two k r v", two=2)

        def gla_sp(sp, n):
            phase_seen(sp, n)
            d = sm("gla_in")
            for i in range(2):
                sp.dma_start(l_up[16 * i:16 * i + 16, 256 * i:256 * i + 256], gla_gk_up[0, i]).then_inc(d, 16)
                sp.dma_start(l_up[16 * i:16 * i + 16, 256 * (1 - i):256 * (2 - i)], zeros_dram(16, 256)).then_inc(d, 16)
            sp.dma_start(l_up[32:33, :], gla_gk_bias.rearrange("a i n -> a (i n)")).then_inc(d, 16)
            sp.dma_start(l_on, gla_onorm[0].partition_broadcast(P)).then_inc(d, 16)
            for i in range(2):
                sv = state_view(state_gla, i)
                for two in range(2):
                    sp.dma_start(l_S[i][0][64 * two:64 * two + 64, :].rearrange("p (r v) -> p r v", v=DV), sv[two]).then_inc(d, 16)
            gla_state_out(sp, 0)

        def gla_state_out(sp, i):
            sp.wait_ge(sm(f"S_final{i}"), 1)
            sv = state_view(new_gla_state, i)
            for two in range(2):
                sp.dma_start(sv[two], l_S[i][2][64 * two:64 * two + 64, :].rearrange("p (r v) -> p r v", v=DV)).then_inc(sm("S_stored"), 16)
            sp.wait_ge(sm("S_stored"), 32 * (i + 1))

        def zeros_dram(a, b):
            o, _ = CONST_AT["sel"]
            return consts[2:2 + a, o:o + b]

        GLA_IN = 16 * 10

        def gla_pe(pe):
            wqk, wv = weights(pe, "bqk"), weights(pe, "bvr")
            pe.wait_ge(sm("gla_in"), GLA_IN)
            pe.wait_ge(sm("l_one"), 1)
            for t in range(NT):
                tok = slice(t * P, (t + 1) * P)
                if t:
                    pe.wait_ge(sm("l_o_out"), t)
                    pe.wait_ge(sm("l_u_used"), 2 * t)
                for k in range(KD):
                    pe.matmul(ps[0:32, 0, 0:P], wv[:, k, 512:544], hT[:, k, tok], start=(k == 0), stop=(k == KD - 1))
                for k in range(KD):
                    pe.matmul(ps[:, 1, :], hT[:, k, tok], wqk[:, k, :], start=(k == 0), stop=(k == KD - 1))
                for k in range(KD):
                    mm = pe.matmul(ps[:, 2, :], hT[:, k, tok], wv[:, k, 0:512], start=(k == 0), stop=(k == KD - 1))
                mm.then_inc(sm("l_qkv_ps"), 1)
                if t == NT - 1:
                    pe.drain().then_inc(sm("w_used"), 2)
                pe.wait_ge(sm("l_rT"), t + 1)
                pe.matmul(ps[:, 3, :], l_rT[0:33, :], l_up[0:33, :], start=True, stop=True).then_inc(sm("l_gk_ps"), 1)
                pe.wait_ge(sm("l_g"), t + 1)
                for i in range(2):
                    g = l_g[:, 256 * i:256 * i + 256]
                    pe.matmul(ps[:, 4, 256 * i:256 * i + 256], cst("upto", i, P), g, start=True, stop=True)
                    pe.matmul(ps[:, 5, 256 * i:256 * i + 256], cst("beyond", i, P), g, start=True, stop=True)
                for i in range(2):
                    for r in range(2):
                        mm = pe.matmul(ps[:, 0, 4 * i + 2 * r:4 * i + 2 * r + 2], l_g[:, 256 * i + P * r:256 * i + P * r + P],
                                       cst("chunkcol"), start=True, stop=True)
                mm.then_inc(sm("l_B_ps"), 1)
                pe.wait_ge(sm("l_qk"), t + 1)
                for j in range(4):
                    pe.transpose(ps[:, 6, j * P:(j + 1) * P], l_q[:, j * P:(j + 1) * P], ident)
                for j in range(4):
                    mm = pe.transpose(ps[:, 7, j * P:(j + 1) * P], l_k[:, j * P:(j + 1) * P], ident)
                mm.then_inc(sm("l_T_ps"), 1)
                pe.wait_ge(sm("l_qT"), t + 1)
                pe.wait_ge(sm("l_kT"), t + 1)
                for i in range(2):
                    for h in range(4):
                        r, o = h // 2, 64 * (h % 2)
                        cs = slice(256 * i + P * r, 256 * i + P * r + P)
                        mm = pe.matmul(ps[:, 4 + h % 2, (2 * i + r) * P:(2 * i + r + 1) * P], l_kT[o:o + 64, cs], l_qT[o:o + 64, cs], start=True, stop=True)
                mm.then_inc(sm("l_A_ps"), 1)
                pe.wait_ge(sm("l_kf"), t + 1)
                pe.wait_ge(sm("l_v"), t + 1)
                for cc in range(2):
                    gla_u(pe, t, cc, l_kf, (3, 0)[cc])
                pe.wait_ge(sm("l_att"), t + 1)
                for h in range(4):
                    r, e = h // 2, h % 2
                    pe.matmul(ps[:, 1 + e, r * P:(r + 1) * P], l_att[:, (2 * e + r) * P:(2 * e + r + 1) * P],
                              l_v[:, t, h * P:(h + 1) * P], start=(r == 0), stop=False, skip_group_check=True)
                for cc in range(2):
                    if cc:
                        pe.wait_ge(sm("l_S"), 2 * t + 1)
                    elif t:
                        pe.wait_ge(sm("l_S_in"), t)
                    gla_inter(pe, cc, l_qT[:, 0:256], l_S[0][cc], 1)
                pe.drain().then_inc(sm("l_o_ps"), 1)
            phase_end(pe)

        def o_parity(t, e):
            return ob[:, t, :].rearrange("p (r e n) -> p e r n", e=2, n=DV)[:, e]

        def gla_u(pe, t, cc, k_end, bank):
            rows = slice(64 * cc, 64 * cc + 64)
            for h in range(4):
                r, o = h // 2, 64 * (h % 2)
                mm = pe.matmul(ps[o:o + 64, bank, r * P:r * P + P], k_end[rows, h * 64:h * 64 + 64],
                               l_v[rows, t, h * P:(h + 1) * P], start=True, stop=True, skip_group_check=True)
            mm.then_inc(sm("l_u_ps"), 1)

        def gla_inter(pe, cc, qTd, state, bank, first=False):
            for h in range(4):
                r, o = h // 2, 64 * (h % 2)
                mm = pe.matmul(ps[64 * cc:64 * cc + 64, bank + h % 2, r * P:(r + 1) * P], qTd[o:o + 64, r * P + 64 * cc:r * P + 64 * cc + 64],
                               state[o:o + 64, r * P:(r + 1) * P], start=first and r == 0, stop=True, skip_group_check=True)
            return mm

        def gla_act(act):
            for t in range(NT):
                act.wait_ge(sm("l_qkv_ps"), t + 1)
                act.activation(l_rT[0:32, :], ps[0:32, 0, 0:P], ACT.Copy).then_inc(sm("l_rT"), 1)
                act.activation(l_v[:, t, :], ps[:, 2, :], ACT.Copy).then_inc(sm("l_v"), 1)
                act.wait_ge(sm("l_gk_ps"), t + 1)
                act.activation(l_abs, ps[:, 3, :], ACT.Abs)
                act.drain()
                act.activation(l_e, l_abs, ACT.Exp, scale=-1.0)
                act.drain()
                act.activation(l_ln, l_e, ACT.Ln, bias=1.0).then_inc(sm("l_ln"), 1)
                act.wait_ge(sm("l_B_ps"), t + 1)
                if t:
                    act.wait_ge(sm("l_kf"), t)
                act.activation(l_ex[0], ps[:, 4, :], ACT.Exp, scale=1 / 16.0)
                act.activation(l_ex[1], ps[:, 4, :], ACT.Exp, scale=-1 / 16.0)
                act.activation(l_ex[2], ps[:, 5, :], ACT.Exp, scale=1 / 16.0)
                act.activation(l_dec[:, t, :], ps[:, 0, 0:8], ACT.Exp, scale=1 / 16.0).then_inc(sm("l_ex"), 1)
                act.wait_ge(sm("l_T_ps"), t + 1)
                if t:
                    act.wait_ge(sm("l_o_ps"), t)
                act.activation(l_qT, ps[:, 6, :], ACT.Copy).then_inc(sm("l_qT"), 1)
                act.activation(l_qb[:, t, :], ps[:, 6, 256:512], ACT.Copy)
                act.wait_ge(sm("l_o_ps"), t + 1)
                for e in range(2):
                    mm = act.activation(o_parity(t, e), ps[:, 1 + e, 0:256].rearrange("p (r n) -> p r n", r=2), ACT.Copy)
                mm.then_inc(sm("l_o_out"), 1)
            phase_end(act)

        def gla_dve(v):
            v.memset(l_rT[32:33, :], 1.0).then_inc(sm("l_one"), 1)
            v.wait_ge(sm("gla_in"), GLA_IN)
            for t in range(NT):
                v.wait_ge(sm("l_ln"), t + 1)
                v.scalar_tensor_tensor(l_g, ps[:, 3, :], 0.0, l_ln, ALU.min, ALU.subtract).then_inc(sm("l_g"), 1)
                v.wait_ge(sm("l_ex"), t + 1)
                two = lambda ap: ap.rearrange("p (i n) -> p i n", i=2)
                qps = ps[:, 1, 0:256].unsqueeze(1).to_broadcast([P, 2, 256])
                kps = ps[:, 1, 256:512].unsqueeze(1).to_broadcast([P, 2, 256])
                v.scalar_tensor_tensor(two(l_q), qps, 0.125, two(l_ex[0]), ALU.mult, ALU.mult)
                v.tensor_tensor(two(l_k), kps, two(l_ex[1]), ALU.mult).then_inc(sm("l_qk"), 1)
                v.tensor_tensor(l_kf, ps[:, 1, 256:512], l_ex[2][:, 0:256], ALU.mult)
                v.tensor_tensor(l_kb[:, t, :], ps[:, 1, 256:512], l_ex[2][:, 256:512], ALU.mult).then_inc(sm("l_kf"), 1)
                v.wait_ge(sm("l_T_ps"), t + 1)
                v.tensor_copy(l_kT, ps[:, 7, :]).then_inc(sm("l_kT"), 1)
                v.wait_ge(sm("l_A_ps"), t + 1)
                for e in range(2):
                    v.tensor_tensor(l_at[e].rearrange("p (i r n) -> p i r n", i=2, n=P), ps[:, 4 + e, :].rearrange("p (i r n) -> p i r n", i=2, n=P),
                                    cst("upto").rearrange("p (i n) -> p i n", i=2).unsqueeze(2).to_broadcast([P, 2, 2, P]), ALU.mult)
                v.drain()
                v.tensor_tensor(l_att[:, 0:256], l_at[0][:, 0:256], l_at[0][:, 256:512], ALU.add)
                v.tensor_tensor(l_att[:, 256:512], l_at[1][:, 0:256], l_at[1][:, 256:512], ALU.add).then_inc(sm("l_att"), 1)
                if t:
                    v.wait_ge(sm("l_o_ps"), t)
                    if t == NS:
                        v.memset(l_S[0][0], 0.0)
                    else:
                        v.tensor_copy(l_S[0][0], l_S[0][2])
                    v.drain().then_inc(sm("l_S_in"), 1)
                for cc in range(2):
                    v.wait_ge(sm("l_u_ps"), 2 * t + cc + 1)
                    for r in range(2):
                        s = v.scalar_tensor_tensor(l_S[0][cc + 1][:, r * P:(r + 1) * P], l_S[0][cc][:, r * P:(r + 1) * P],
                                                   l_dec[:, t, 2 * r + cc:2 * r + cc + 1],
                                                   ps[:, (3, 0)[cc], r * P:r * P + P], ALU.mult, ALU.add)
                    v.drain().then_inc(sm("l_S"), 1)
                    v.drain().then_inc(sm("l_u_used"), 1)
            v.drain().then_inc(sm("S_final0"), 1)
            phase_end(v)

        def glab_sp(sp, n):
            phase_seen(sp, n)
            gla_state_out(sp, 1)
            sp.sem_inc(sm("phase_sp"), 1)

        def glab_pe(pe):
            for m, t in enumerate(gla_tiles(1)):
                b = 4 * (m % 2)
                if m >= 2:
                    pe.wait_ge(sm("m_o_used"), m - 1)
                    pe.wait_ge(sm("m_S"), 2 * (m - 1))
                for cc in (1, 0):
                    gla_u(pe, t, cc, l_kb[:, t, :], b + cc)
                for n, cc in enumerate((1, 0)):
                    if n:
                        pe.wait_ge(sm("m_S"), 2 * m + 1)
                    elif m:
                        pe.wait_ge(sm("m_S_in"), m)
                    mm = gla_inter(pe, cc, l_qb[:, t, :], l_S[1][n], b + 2, first=True)
                mm.then_inc(sm("m_o_ps"), 1)
            phase_end(pe)

        def glab_dve(v):
            for m, t in enumerate(gla_tiles(1)):
                b = 4 * (m % 2)
                if m:
                    v.wait_ge(sm("m_o_ps"), m)
                    if t == NS:
                        v.memset(l_S[1][0], 0.0)
                    else:
                        v.tensor_copy(l_S[1][0], l_S[1][2])
                    v.drain().then_inc(sm("m_S_in"), 1)
                for n, cc in enumerate((1, 0)):
                    v.wait_ge(sm("l_u_ps"), 2 * NT + 2 * m + n + 1)
                    for r in range(2):
                        v.scalar_tensor_tensor(l_S[1][n + 1][:, r * P:(r + 1) * P], l_S[1][n][:, r * P:(r + 1) * P],
                                               l_dec[:, t, 4 + 2 * r + cc:4 + 2 * r + cc + 1],
                                               ps[:, b + cc, r * P:r * P + P], ALU.mult, ALU.add)
                    v.drain().then_inc(sm("m_S"), 1)
                v.wait_ge(sm("m_o_ps"), m + 1)
                for e in range(2):
                    mm = v.tensor_tensor(o_parity(t, e), ps[:, b + 2 + e, 0:256].rearrange("p (r n) -> p r n", r=2), o_parity(t, e), ALU.add)
                mm.then_inc(sm("m_o_used"), 1)
                onorm_dve(v, m, t, l_sq, l_st, l_on)
            v.drain().then_inc(sm("S_final1"), 1)
            phase_end(v)

        def onorm_dve(v, m, t, sq, st, wn):
            o4 = ob[:, t, :].rearrange("p (h n) -> p h n", n=DV)
            v.wait_ge(sm("on_sq"), m + 1)
            v.tensor_reduce(st[:, 0:4], sq.rearrange("p (h n) -> p h n", n=DV), AX.X, ALU.add).then_inc(sm("on_ss"), 1)
            v.wait_ge(sm("on_rs"), m + 1)
            v.tensor_tensor(o4, o4, st[:, 8:12].unsqueeze(2).to_broadcast([P, 4, DV]), ALU.mult)
            v.drain()
            v.tensor_tensor(o4, o4, wn.unsqueeze(1).to_broadcast([P, 4, DV]), ALU.mult)

        def onorm_act(act, m, t, sq, st, ready):
            if ready is not None:
                act.wait_ge(sm(ready), m + 1)
            act.activation(sq, ob[:, t, :], ACT.Square).then_inc(sm("on_sq"), 1)
            act.wait_ge(sm("on_ss"), m + 1)
            act.activation(st[:, 4:8], st[:, 0:4], ACT.Ln, scale=1.0 / DV, bias=eps_col)
            act.drain()
            act.activation(st[:, 8:12], st[:, 4:8], ACT.Exp, scale=-0.5).then_inc(sm("on_rs"), 1)

        def glab_act(act):
            for m, t in enumerate(gla_tiles(1)):
                onorm_act(act, m, t, l_sq, l_st, "m_o_used")
            phase_end(act)

        NZ = T + 6
        NC2 = T + 2
        N72 = 2 * NT * 4
        er_ = Region(NT * QW)
        c_z = er_.take(NT * 16)
        c_in = er_.take(32)
        c_rows = er_.take(P)
        c_w = er_.take(60)
        c_sp = er_.take(NT * 8)
        c_t = er_.take(NT * 8)
        c_g, c_gc, c_beta, c_eg, c_er, c_nb = (er_.take(N72) for _ in range(6))
        c_dec = er_.take(2 * N72)
        d_qT, d_kT = er_.take(T), er_.take(T)
        d_k = er_.take(T).rearrange("p (t n) -> p t n", n=P)
        d_v = er_.take(T).rearrange("p (t n) -> p t n", n=P)
        r1 = er_.at
        zp = er_.take(3 * NZ).rearrange("p (b n) -> p b n", b=3)
        zc = er_.take(3 * NC2)
        zcb = zc.rearrange("p (b n) -> p b n", b=3)
        z_sq = er_.take(2 * NC2)
        z_rn = er_.take(2 * NC2)
        er2 = Region(r1)
        d_Z, d_A, d_W, d_Q, d_K, d_V = (er2.take(2 * T).rearrange("p (i t n) -> p i t n", i=2, n=P) for _ in range(6))
        r3 = er2.at
        d_D, d_Y, d_T, d_X = ([er2.take(3 * P) for _ in range(2)] for _ in range(4))
        er3 = Region(r3)
        d_S = [[er3.take(P) for _ in range(3)] for _ in range(2)]
        d_vn = [[er3.take(P) for _ in range(2)] for _ in range(2)]
        o_sq = Region(r1).take(QW)
        o_st = Region(r1 + QW).take(12)
        o_on = Region(r1 + QW + 12).take(P)

        def col(ap, i, t, h):
            n = (i * NT + t) * 4 + h
            return ap[:, n:n + 1]

        def ab_sp(sp, n):
            phase_seen(sp, n)
            d = sm("ab_in")
            sp.dma_start(c_in[:, 0:8], dt_bias_d[0].rearrange("i h -> (i h)").partition_broadcast(P)).then_inc(d, 16)
            sp.dma_start(c_in[:, 8:16], a_log_d[0].rearrange("i h -> (i h)").partition_broadcast(P)).then_inc(d, 16)
            sp.dma_start(c_rows[0:60, :], conv_d[0].rearrange("k (b p) -> (k b) p", p=P)).then_inc(d, 16)

        def ab_pe(pe):
            w = weights(pe, "ab")
            for t in range(NT):
                for k in range(KD):
                    pe.matmul(ps[:, 0, 16 * t:16 * t + 16], hT[:, k, t * P:(t + 1) * P], w[:, k, :], start=(k == 0), stop=(k == KD - 1))
            pe.drain().then_inc(sm("w_used"), 1)
            pe.wait_ge(sm("ab_in"), 48)
            pe.transpose(ps[:, 1, 0:60], c_rows[0:60, :], ident[0:60, 0:60]).then_inc(sm("ab_ps"), 1)
            pe.wait_ge(sm("c_g"), 1)
            for i in range(2):
                g = c_g[:, 36 * i:36 * i + 36]
                pe.matmul(ps[:, 2, 36 * i:36 * i + 36], cst("upto", i, P), g, start=True, stop=True)
                pe.matmul(ps[:, 3, 36 * i:36 * i + 36], cst("beyond", i, P), g, start=True, stop=True)
            for cc in range(2):
                mm = pe.matmul(ps[:, 4, N72 * cc:N72 * cc + N72], cst("inchunk", cc, P), c_g, start=True, stop=True)
            mm.then_inc(sm("c_ps"), 1)
            phase_end(pe)

        def ab_act(act):
            act.wait_ge(sm("ab_ps"), 1)
            act.activation(c_w, ps[:, 1, 0:60], ACT.Copy)
            act.activation(c_in[:, 16:24], c_in[:, 8:16], ACT.Exp)
            act.wait_ge(sm("c_a"), 1)
            act.activation(c_z.rearrange("p (t n) -> p t n", n=16)[:, :, 8:16], ps[:, 0, 0:NT * 16].rearrange("p (t n) -> p t n", n=16)[:, :, 8:16],
                           ACT.Exp, scale=-1.0)
            act.activation(c_t, c_sp, ACT.Abs)
            act.drain()
            act.activation(c_t, c_t, ACT.Exp, scale=-1.0)
            act.drain()
            act.activation(c_t, c_t, ACT.Ln, bias=1.0).then_inc(sm("c_ln"), 1)
            act.wait_ge(sm("c_ps"), 1)
            act.activation(c_gc, ps[:, 2, 0:N72], ACT.Copy)
            act.activation(c_eg, ps[:, 2, 0:N72], ACT.Exp)
            act.activation(c_er, ps[:, 3, 0:N72], ACT.Exp)
            act.activation(c_dec, ps[:, 4, 0:2 * N72], ACT.Exp).then_inc(sm("c_ex"), 1)
            phase_end(act)

        def ab_dve(v):
            v.memset(ob.rearrange("p t n -> p (t n)"), 0.0)
            v.wait_ge(sm("ab_in"), 48)
            v.wait_ge(sm("ab_ps"), 1)
            tih = lambda ap, n: ap.rearrange("p (t n) -> p t n", n=n)
            v.tensor_tensor(tih(c_sp, 8), tih(ps[:, 0, 0:NT * 16], 16)[:, :, 0:8], c_in[:, 0:8].unsqueeze(1).to_broadcast([P, NT, 8]), ALU.add)
            v.drain().then_inc(sm("c_a"), 1)
            v.wait_ge(sm("c_ln"), 1)
            v.scalar_tensor_tensor(c_sp, c_sp, 0.0, c_t, ALU.max, ALU.add)
            v.drain()
            v.scalar_tensor_tensor(tih(c_sp, 8), tih(c_sp, 8), -1.0, c_in[:, 16:24].unsqueeze(1).to_broadcast([P, NT, 8]), ALU.mult, ALU.mult)
            z8 = c_z.rearrange("p (t n) -> p t n", n=16)[:, :, 8:16]
            v.tensor_scalar(z8, z8, 1.0, None, ALU.add)
            v.drain()
            for i in range(2):
                v.tensor_copy(c_g[:, 36 * i:36 * i + 36].rearrange("p (t h) -> p t h", h=4), tih(c_sp, 8)[:, :, 4 * i:4 * i + 4])
            v.drain().then_inc(sm("c_g"), 1)
            for i in range(2):
                v.reciprocal(c_beta[:, 36 * i:36 * i + 36].rearrange("p (t h) -> p t h", h=4), z8[:, :, 4 * i:4 * i + 4])
            v.drain()
            v.wait_ge(sm("c_ex"), 1)
            v.scalar_tensor_tensor(c_nb, c_beta, -1.0, c_eg, ALU.mult, ALU.mult)
            phase_end(v)

        TOK = [(0, 512, 2), (512, 512, 514), (T_S, T_P, T_S + 4)]
        NORM = [(a, min(512, 2 * NC2 - a)) for a in range(0, 2 * NC2, 512)]

        def pre_pe(pe, h):
            w = weights(pe, f"dh{h}")
            for n in range(9):
                b, (o, m, _) = n // 3, TOK[n % 3]
                if n == 8:
                    pe.wait_ge(sm("zp"), 9 * h + 1)
                for k in range(KD):
                    mm = pe.matmul(ps[:, n % 8, 0:m], w[:, k, b * P:(b + 1) * P], hT[:, k, o:o + m], start=(k == 0), stop=(k == KD - 1))
                mm.then_inc(sm("zp_ps"), 1)
            pe.drain().then_inc(sm("w_used"), 1)
            pe.wait_ge(sm("z_sq"), h + 1)
            for n, (o, m) in enumerate(NORM):
                mm = pe.matmul(ps[:, n, 0:m], ones, z_sq[:, o:o + m], start=True, stop=True)
            mm.then_inc(sm("z_ss"), 1)
            pe.wait_ge(sm("d_qkT"), h + 1)
            for t in range(NT):
                if t >= 2:
                    pe.wait_ge(sm("d_kv"), NT * h + t - 1)
                vo = t * P + (2 if t == NS else 0)
                pe.transpose(ps[:, 6 + t % 2, 0:P], d_kT[:, t * P:(t + 1) * P], ident)
                pe.transpose(ps[:, 6 + t % 2, P:2 * P], zcb[:, 2, vo:vo + P], ident).then_inc(sm("d_kv_ps"), 1)
            phase_end(pe)

        def pre_act(act, h):
            for n in range(9):
                b, (_, m, o) = n // 3, TOK[n % 3]
                act.wait_ge(sm("zp_ps"), 9 * h + n + 1)
                act.activation(zp[:, b, o:o + m], ps[:, n % 8, 0:m], ACT.Copy).then_inc(sm("zp"), 1)
            act.wait_ge(sm("zc"), h + 1)
            act.activation(zc, zc, ACT.Silu)
            act.preload_act_table_set(EXP_LN)
            act.drain()
            act.activation(z_sq, zc[:, 0:2 * NC2], ACT.Square).then_inc(sm("z_sq"), 1)
            act.wait_ge(sm("z_ss"), h + 1)
            act.activation(z_rn, ps[:, 0:5, :].rearrange("p a n -> p (a n)")[:, 0:2 * NC2], ACT.Ln, bias=eps_col)
            act.drain()
            act.activation(z_rn, z_rn, ACT.Exp, scale=-0.5).then_inc(sm("z_rn"), 1)
            for t in range(NT):
                act.wait_ge(sm("d_kv_ps"), NT * h + t + 1)
                act.activation(d_k[:, t, :], ps[:, 6 + t % 2, 0:P], ACT.Copy)
                act.activation(d_v[:, t, :], ps[:, 6 + t % 2, P:2 * P], ACT.Copy).then_inc(sm("d_kv"), 1)
            phase_end(act)

        def pre_dve(v, h):
            for a in (0, 2 + T_S, 4 + T):
                v.memset(zp[:, :, a:a + 2], 0.0)
            v.drain()
            for k in range(5):
                for b in range(3):
                    if k == 0:
                        v.wait_ge(sm("zp"), 9 * h + 3 * b + 3)
                    tap = c_w[:, 12 * k + 4 * b + h:12 * k + 4 * b + h + 1]
                    if k == 0:
                        v.tensor_scalar(zcb[:, b, :], zp[:, b, k:k + NC2], tap, None, ALU.mult)
                    else:
                        v.scalar_tensor_tensor(zcb[:, b, :], zp[:, b, k:k + NC2], tap, zcb[:, b, :], ALU.mult, ALU.add)
                v.drain()
            v.drain().then_inc(sm("zc"), 1)
            v.wait_ge(sm("z_rn"), h + 1)
            for dst, b, s in ((d_qT, 0, P ** -0.5), (d_kT, 1, 1.0)):
                for o, n, x in ((0, T_S, 0), (T_S, T_P, 2)):
                    a = b * NC2 + o + x
                    v.scalar_tensor_tensor(dst[:, o:o + n], z_rn[:, a:a + n], s, zc[:, a:a + n], ALU.mult, ALU.mult)
            v.drain().then_inc(sm("d_qkT"), 1)
            phase_end(v)

        GROUPS = [(i, 3 * a) for a in range(3) for i in range(2)]
        ROWS, KK, KQ, Z1 = range(4)
        LY, LZ, LX, LW = range(4)

        def sbank(n, b):
            return 4 * (n % 2) + b

        def tiles3(ap):
            return ap.rearrange("p (a n) -> p a n", n=P)

        def sys_steps():
            for n in range(0, len(GROUPS), 2):
                for m in (n, n + 1):
                    yield "start", m, 0
                for m in (n, n + 1):
                    yield "first", m, 0
                for k in range(1, NLEV):
                    for m in (n, n + 1):
                        yield "y", m, k
                    for m in (n, n + 1):
                        yield "zx", m, k
                for m in (n, n + 1):
                    yield "w", m, 0

        def sys_pe(pe, h):
            for what, n, k in sys_steps():
                i, t0 = GROUPS[n]
                N = 6 * h + n
                p = n % 2
                cols = [slice(a * P, (a + 1) * P) for a in range(3)]
                if what == "start":
                    if n >= 2:
                        pe.wait_ge(sm("s_Z"), N - 1)
                    for a in range(3):
                        t = t0 + a
                        ks = d_kT[:, t * P:(t + 1) * P]
                        pe.matmul(ps[:, sbank(n, ROWS), cols[a]], col(c_g, i, t, h).to_broadcast([P, P]), cst("upto", i, P), start=True, stop=True)
                        pe.matmul(ps[:, sbank(n, KK), cols[a]], ks, ks, start=True, stop=True)
                        mm = pe.matmul(ps[:, sbank(n, KQ), cols[a]], ks, d_qT[:, t * P:(t + 1) * P], start=True, stop=True)
                    mm.then_inc(sm("s_G_ps"), 1)
                elif what == "first":
                    pe.wait_ge(sm("s_X1"), N + 1)
                    if n >= 2:
                        pe.wait_ge(sm("s_W"), N - 1)
                    for a in range(3):
                        mm = pe.transpose(ps[:, sbank(n, Z1), cols[a]], d_X[p][:, cols[a]], ident)
                    mm.then_inc(sm("s_Z1_ps"), 1)
                elif what == "y":
                    pe.wait_ge(sm(f"s_ZX{p}"), 5 * (N // 2) + k)
                    if k == 1:
                        pe.wait_ge(sm("s_Q"), N + 1)
                    for a in range(3):
                        mm = pe.matmul(ps[:, sbank(n, LY), cols[a]], d_T[p][:, cols[a]], d_Z[:, i, t0 + a, :], start=True, stop=True)
                    mm.then_inc(sm(f"s_Y_ps{p}"), 1)
                elif what == "zx":
                    pe.wait_ge(sm(f"s_Y{p}"), 5 * (N // 2) + k)
                    for a in range(3):
                        mm = pe.matmul(ps[:, sbank(n, LZ), cols[a]], d_X[p][:, cols[a]], d_Y[p][:, cols[a]], start=True, stop=True)
                        if k < NLEV - 1:
                            mm = pe.matmul(ps[:, sbank(n, LX), cols[a]], d_Y[p][:, cols[a]], d_X[p][:, cols[a]], start=True, stop=True)
                    mm.then_inc(sm(f"s_ZY_ps{p}"), 1)
                else:
                    pe.wait_ge(sm("s_Z"), N + 1)
                    pe.wait_ge(sm("s_kb"), N + 1)
                    for a in range(3):
                        mm = pe.matmul(ps[:, sbank(n, LW), cols[a]], d_D[p][:, cols[a]], d_Z[:, i, t0 + a, :], start=True, stop=True)
                    mm.then_inc(sm("s_W_ps"), 1)
            phase_end(pe)

        def sys_act(act, h):
            for what, n, k in sys_steps():
                i, t0 = GROUPS[n]
                N = 6 * h + n
                p = n % 2
                if what == "start":
                    act.wait_ge(sm("s_D"), N + 1)
                    act.activation(d_D[p], d_D[p], ACT.Exp, scale=-1.0)
                    act.activation(d_Y[p], d_Y[p], ACT.Exp).then_inc(sm("s_ex"), 1)
                    act.activation(ps[:, sbank(n, ROWS), 0:384], ps[:, sbank(n, ROWS), 0:384], ACT.Exp).then_inc(sm("s_E"), 1)
                    for a in range(3):
                        t = t0 + a
                        act.activation(d_V[:, i, t, :], d_v[:, t, :], ACT.Copy, scale=col(c_beta, i, t, h))
                        act.activation(d_K[:, i, t, :], d_k[:, t, :], ACT.Copy, scale=col(c_er, i, t, h))
                elif what == "first":
                    act.wait_ge(sm("s_X1"), N + 1)
                    for a in range(3):
                        mm = act.activation(d_D[p][:, a * P:(a + 1) * P], d_k[:, t0 + a, :], ACT.Copy, scale=col(c_nb, i, t0 + a, h))
                    mm.then_inc(sm("s_kb"), 1)
                elif what == "w":
                    act.wait_ge(sm("s_W_ps"), N + 1)
                    act.activation(d_W[:, i, t0:t0 + 3, :], tiles3(ps[:, sbank(n, LW), 0:384]), ACT.Copy).then_inc(sm("s_W"), 1)
            phase_end(act)

        def sys_dve(v, h):
            for what, n, k in sys_steps():
                i, t0 = GROUPS[n]
                N = 6 * h + n
                p = n % 2
                Z = d_Z[:, i, t0:t0 + 3, :]
                if what == "start":
                    v.wait_ge(sm("s_G_ps"), N + 1)
                    if n >= 2:
                        v.wait_ge(sm("s_W_ps"), N - 1)
                    for a in range(3):
                        t, s = t0 + a, slice(a * P, (a + 1) * P)
                        row = ps[:, sbank(n, ROWS), s]
                        v.scalar_tensor_tensor(d_D[p][:, s], row, col(c_gc, i, t, h), cst("strict", i, P), ALU.subtract, ALU.max)
                        v.scalar_tensor_tensor(d_Y[p][:, s], row, col(c_gc, i, t, h), cst("incl", i, P), ALU.subtract, ALU.min)
                    v.drain().then_inc(sm("s_D"), 1)
                elif what == "first":
                    v.wait_ge(sm("s_ex"), N + 1)
                    for a in range(3):
                        t, s = t0 + a, slice(a * P, (a + 1) * P)
                        v.scalar_tensor_tensor(d_T[p][:, s], ps[:, sbank(n, KK), s], col(c_beta, i, t, h), d_D[p][:, s], ALU.mult, ALU.mult)
                    v.drain()
                    lv = cst("level0", 1 - i, P).unsqueeze(1).to_broadcast([P, 3, P])
                    v.scalar_tensor_tensor(tiles3(d_X[p]), tiles3(d_T[p]), -1.0, lv, ALU.mult, ALU.mult)
                    v.drain()
                    v.tensor_tensor(tiles3(d_X[p]), tiles3(d_X[p]), ident.unsqueeze(1).to_broadcast([P, 3, P]), ALU.add).then_inc(sm("s_X1"), 1)
                    v.tensor_tensor(d_A[:, i, t0:t0 + 3, :], tiles3(ps[:, sbank(n, KQ), 0:384]), tiles3(d_Y[p]), ALU.mult)
                    v.wait_ge(sm("s_E"), N + 1)
                    v.tensor_tensor(d_Q[:, i, t0:t0 + 3, :], tiles3(d_qT[:, t0 * P:t0 * P + 384]), tiles3(ps[:, sbank(n, ROWS), 0:384]), ALU.mult).then_inc(sm("s_Q"), 1)
                    v.wait_ge(sm("s_Z1_ps"), N + 1)
                    v.tensor_copy(Z, tiles3(ps[:, sbank(n, Z1), 0:384])).then_inc(sm(f"s_ZX{p}"), 1)
                elif what == "y":
                    v.wait_ge(sm(f"s_Y_ps{p}"), 5 * (N // 2) + k)
                    lv = cst(f"level{k}", i, P).unsqueeze(1).to_broadcast([P, 3, P])
                    v.tensor_tensor(tiles3(d_Y[p]), tiles3(ps[:, sbank(n, LY), 0:384]), lv, ALU.mult).then_inc(sm(f"s_Y{p}"), 1)
                elif what == "zx":
                    v.wait_ge(sm(f"s_ZY_ps{p}"), 5 * (N // 2) + k)
                    z = v.scalar_tensor_tensor(Z, tiles3(ps[:, sbank(n, LZ), 0:384]), -1.0, Z, ALU.mult, ALU.add)
                    if k < NLEV - 1:
                        v.scalar_tensor_tensor(d_X[p], ps[:, sbank(n, LX), 0:384], -1.0, d_X[p], ALU.mult, ALU.add).then_inc(sm(f"s_ZX{p}"), 1)
                    else:
                        z.then_inc(sm("s_Z"), 1)
            phase_end(v)

        STEPS = [(s, False) for s in range(2 * NS)] + [(s, True) for s in range(2)]

        def step_of(i, n):
            s, prompt = STEPS[n]
            if prompt:
                cc = s if i == 0 else 1 - s
                return NS, cc, (2, 1)[s], (1, 0)[s]
            g = s if i == 0 else 2 * NS - 1 - s
            return g // 2, g % 2, n % 2, (n + 1) % 2

        NST = len(STEPS)

        def scan_sp(sp, h, n):
            phase_seen(sp, n)
            for i in range(2):
                sp.dma_start(d_S[i][0], state_delta[0, 0, i, h]).then_inc(sm("d_S_in"), 16)
            for i in range(2):
                sp.wait_ge(sm(f"d_S{i}"), NST * (h + 1))
                sp.dma_start(new_delta_state[0, 0, i, h], d_S[i][0]).then_inc(sm("d_S_stored"), 16)
            sp.wait_ge(sm("d_S_stored"), 32 * (h + 1))
            sp.sem_inc(sm("phase_sp"), 1)

        def scan_pe(pe, h):
            pe.wait_ge(sm("d_S_in"), 32 * (h + 1))
            pe.wait_ge(sm("d_S_zero"), h + 1)
            for n in range(NST):
                N = NST * h + n
                for i in range(2):
                    t, cc, a, _ = step_of(i, n)
                    rows = slice(64 * cc, 64 * cc + 64)
                    pe.matmul(ps[rows, 3 * i, 0:P], d_Z[:, i, t, rows], d_V[:, i, t, :], start=True, stop=False)
                    if n:
                        pe.wait_ge(sm(f"d_S{i}"), N)
                    pe.matmul(ps[rows, 3 * i, 0:P], d_W[:, i, t, rows], d_S[i][a], start=False, stop=True).then_inc(sm(f"d_vn_ps{i}"), 1)
                    if n:
                        pe.wait_ge(sm(f"d_o{i}"), N)
                    pe.matmul(ps[rows, 3 * i + 1, 0:P], d_Q[:, i, t, rows], d_S[i][a], start=True, stop=False)
                for i in range(2):
                    t, cc, a, _ = step_of(i, n)
                    rows = slice(64 * cc, 64 * cc + 64)
                    pe.wait_ge(sm(f"d_vn{i}"), N + 1)
                    pe.matmul(ps[:, 3 * i + 2, 0:P], d_K[:, i, t, :], d_vn[i][cc], start=True, stop=True).then_inc(sm(f"d_kS_ps{i}"), 1)
                    pe.matmul(ps[rows, 3 * i + 1, 0:P], d_A[:, i, t, rows], d_vn[i][cc], start=False, stop=True).then_inc(sm(f"d_o_ps{i}"), 1)
            phase_end(pe)

        def scan_act(act, h):
            for n in range(NST):
                for i in range(2):
                    t, cc, a, _ = step_of(i, n)
                    rows = slice(64 * cc, 64 * cc + 64)
                    act.wait_ge(sm(f"d_vn_ps{i}"), NST * h + n + 1)
                    if n:
                        act.wait_ge(sm(f"d_o_ps{i}"), NST * h + n)
                    act.activation(d_vn[i][cc][rows, :], ps[rows, 3 * i, 0:P], ACT.Copy).then_inc(sm(f"d_vn{i}"), 1)
            phase_end(act)

        def scan_dve(v, h):
            for i in range(2):
                v.memset(d_S[i][2], 0.0)
                for cc in range(2):
                    v.memset(d_vn[i][cc][64 * (1 - cc):64 * (1 - cc) + 64, :], 0.0)
            v.drain().then_inc(sm("d_S_zero"), 1)
            v.wait_ge(sm("d_S_in"), 32 * (h + 1))
            for n in range(NST):
                N = NST * h + n
                for i in range(2):
                    t, cc, a, b = step_of(i, n)
                    m = cc * N72 + (i * NT + t) * 4 + h
                    v.wait_ge(sm(f"d_kS_ps{i}"), N + 1)
                    v.scalar_tensor_tensor(d_S[i][b], d_S[i][a], c_dec[:, m:m + 1], ps[:, 3 * i + 2, 0:P], ALU.mult, ALU.add).then_inc(sm(f"d_S{i}"), 1)
                for i in range(2):
                    t, cc, a, b = step_of(i, n)
                    rows = slice(64 * cc, 64 * cc + 64)
                    v.wait_ge(sm(f"d_o_ps{i}"), N + 1)
                    o = ob[rows, t, h * P:(h + 1) * P]
                    v.tensor_tensor(o, ps[rows, 3 * i + 1, 0:P], o, ALU.add).then_inc(sm(f"d_o{i}"), 1)
            phase_end(v)

        def don_sp(sp, n):
            phase_seen(sp, n)
            sp.dma_start(o_on, delta_onorm[0].partition_broadcast(P)).then_inc(sm("don_in"), 16)

        def don_act(act):
            for t in range(NT):
                if t:
                    act.wait_ge(sm("on_ss"), NT + t)
                onorm_act(act, NT + t, t, o_sq, o_st, None)
            phase_end(act)

        def don_dve(v):
            v.wait_ge(sm("don_in"), 16)
            for t in range(NT):
                onorm_dve(v, NT + t, t, o_sq, o_st, o_on)
            phase_end(v)

        eps_col = small[:, 0:1]
        STAGES = ["mod0", "ada0", "qkv0", "att0", "gateA0", "gla", "glab", "gateB0", "fin0",
                  "mod1", "ada1", "qkv1", "att1", "gateA1", "dab"]
        STAGES += [f"{s}{h}" for h in range(4) for s in ("dpre", "dsys", "dscan")]
        STAGES += ["don", "gateB1", "fin1"]
        no = STAGES.index
        STORING = [s for s in STAGES if s.startswith(("qkv", "gate", "glab", "dscan"))]

        def stores_done(eng, stage):
            eng.wait_ge(sm("phase_sp"), STORING.index(stage) + 1)

        block = ctx.enter_context(nc.Block())

        @block.gpsimd
        def _(pool):
            for i, (name, parts, n) in enumerate(chunks):
                if i >= RING:
                    pool.wait_ge(sm("w_used"), i - RING + 1)
                o = 0
                for src in parts:
                    m = src.shape[2]
                    pool.dma_start(wslot(i, n)[:, :, o:o + m], src).then_inc(sm(f"w_loaded{i % RING}"), 16)
                    o += m

        @block.sync
        def _(sp):
            sp.dma_start(con[:, :], consts).then_inc(sm("const_in"), 16)
            for l in range(2):
                mod_sp(sp, l, no(f"mod{l}"))
                ada_sp(sp, l, no(f"ada{l}"))
                qkv_sp(sp, l, no(f"qkv{l}"))
                att_sp(sp, l, no(f"att{l}"))
                gateA_sp(sp, l)
                if l == 0:
                    gla_sp(sp, no("gla"))
                    glab_sp(sp, no("glab"))
                else:
                    ab_sp(sp, no("dab"))
                    for h in range(4):
                        scan_sp(sp, h, no(f"dscan{h}"))
                    don_sp(sp, no("don"))
                gate_sp(sp, l)
                fin_sp(sp, l, no(f"fin{l}"))

        @block.tensor
        def _(pe):
            pe.wait_ge(sm("const_in"), 16)
            for l in range(2):
                mod_pe(pe, l)
                ada_pe(pe, l)
                qkv_pe(pe, l)
                stores_done(pe, f"qkv{l}")
                att_pe(pe, l)
                gateA_pe(pe, l)
                stores_done(pe, f"gateA{l}")
                if l == 0:
                    gla_pe(pe)
                    glab_pe(pe)
                    stores_done(pe, "glab")
                else:
                    ab_pe(pe)
                    for h in range(4):
                        pre_pe(pe, h)
                        sys_pe(pe, h)
                        scan_pe(pe, h)
                        stores_done(pe, f"dscan{h}")
                    phase_end(pe)
                gate_pe(pe, l)
                stores_done(pe, f"gateB{l}")
                fin_pe(pe, l)

        @block.scalar
        def _(act):
            act.wait_ge(sm("eps"), 1)
            act.wait_ge(sm("const_in"), 16)
            for l in range(2):
                mod_act(act, l)
                act.preload_act_table_set(EXP_LN)
                ada_act(act, l)
                qkv_act(act, l)
                stores_done(act, f"qkv{l}")
                att_act(act, l)
                gateA_act(act, l)
                stores_done(act, f"gateA{l}")
                act.preload_act_table_set(EXP_LN)
                if l == 0:
                    gla_act(act)
                    glab_act(act)
                    stores_done(act, "glab")
                else:
                    ab_act(act)
                    for h in range(4):
                        pre_act(act, h)
                        sys_act(act, h)
                        scan_act(act, h)
                        stores_done(act, f"dscan{h}")
                    don_act(act)
                gate_act(act, l)
                act.preload_act_table_set(EXP_LN)
                stores_done(act, f"gateB{l}")
                fin_act(act, l)

        @block.vector
        def _(v):
            v.memset(small[:, 0:1], EPS).then_inc(sm("eps"), 1)
            v.wait_ge(sm("const_in"), 16)
            for l in range(2):
                mod_dve(v, l)
                ada_dve(v, l)
                qkv_dve(v, l)
                stores_done(v, f"qkv{l}")
                att_dve(v, l)
                gateA_dve(v, l)
                stores_done(v, f"gateA{l}")
                if l == 0:
                    gla_dve(v)
                    glab_dve(v)
                    stores_done(v, "glab")
                else:
                    ab_dve(v)
                    for h in range(4):
                        pre_dve(v, h)
                        sys_dve(v, h)
                        scan_dve(v, h)
                        stores_done(v, f"dscan{h}")
                    don_dve(v)
                gate_dve(v, l)
                stores_done(v, f"gateB{l}")
                fin_dve(v, l)


_OUTS = [("y_prompt", (1, T_P, D)), ("y_sample", (1, T_S, D)), ("new_attn_k", (1, 1, T_P, 2, HD)),
         ("new_attn_v", (1, 1, T_P, 2, HD)), ("new_gla_state", (1, 1, 2, 4, 64, 128)),
         ("new_swa_k", (1, 1, T_P, 2, HD)), ("new_swa_v", (1, 1, T_P, 2, HD)),
         ("new_delta_state", (1, 1, 2, 4, 128, 128))]
_INS = ["x_prompt", "x_sample", "c", "cache_attn_k", "cache_attn_v", "state_gla", "cache_swa_k", "cache_swa_v",
        "state_delta", "c_ctx", "w_mod", "b_mod", "g_pre", "g_post", "w_in_even", "w_out_even", "qnorm_a", "knorm_a",
        "gla_gk_up", "gla_gk_bias", "gla_onorm", "w_in_odd", "w_out_odd", "sink_c", "conv_d", "a_log_d", "dt_bias_d",
        "delta_onorm"]


def kernel(**inputs):
    import numpy as _np
    import concourse.bacc as _bacc
    from concourse import mybir as _mybir
    from concourse.bass_utils import run_bass_kernel_spmd as _run

    nc = _bacc.Bacc("TRN2", target_bir_lowering=False, num_devices=1)
    arrays, args = {}, {}
    for name in _INS:
        a = _np.ascontiguousarray(inputs[name])
        arrays[f"in_{name}"] = a
        args[name] = nc.dram_tensor(f"in_{name}", a.shape, _mybir.dt.from_np(a.dtype), kind="ExternalInput").ap()
    arrays["in_consts"] = CONSTS
    args["consts"] = nc.dram_tensor("in_consts", CONSTS.shape, _mybir.dt.float32, kind="ExternalInput").ap()
    for name, shape in _OUTS:
        args[name] = nc.dram_tensor(f"out_{name}", shape, _mybir.dt.float32, kind="ExternalOutput").ap()
    backbone(nc, **args)
    r = _run(nc, [arrays], core_ids=[0])
    return tuple(r.results[0][f"out_{name}"] for name, _ in _OUTS)
```

```python
from contextlib import ExitStack

import numpy as np

import concourse.bass as bass
from concourse import mybir

F32 = mybir.dt.float32
F32R = mybir.dt.float32r
ALU = mybir.AluOpType
ACT = mybir.ActivationFunctionType
AX = mybir.AxisListType

P = 128
D = 1024
KD = D // P
T_S = 1024
T_P = 128
NS = T_S // P
NT = NS + 1
T = T_S + T_P
HD = 64
CH = 64
QW = 512
EPS = 1e-6
BIG = 1e30
EXP_LN = "natural_log_exp_and_others"
DV = 128
NLEV = 6
CTX = NS
PROMPT_KEYS = NS + 1
SLOT = 544
RING = 2

E_Q, E_K, E_V, E_G, E_BQ, E_BV, E_BG = 0, 512, 640, 768, 1280, 1792, 2336
O_Q, O_K, O_V, O_G, O_DQ, O_DK, O_DV, O_AB, O_DG = 0, 512, 640, 768, 1280, 1792, 2304, 2816, 2832


def constant_tables():
    a = np.arange(P)
    row, col = a[:, None], a[None, :]
    same = row // CH == col // CH
    parts, at = [], {}

    def put(name, m):
        at[name] = (sum(x.shape[1] for x in parts), m.shape[1])
        parts.append(m.astype(np.float32))

    put("ident", row == col)
    put("eps", np.full((P, 1), EPS))
    put("ones", np.ones((P, P)))
    put("upto", np.concatenate([(row <= col) & same, (row >= col) & same], 1))
    put("beyond", np.concatenate([(row > col) & same, (row < col) & same], 1))
    put("inchunk", np.concatenate([(row // CH == c) & (col >= 0) for c in range(2)], 1))
    put("strict", np.concatenate([np.where((row > col) & same, 0, BIG), np.where((row < col) & same, 0, BIG)], 1))
    put("incl", np.concatenate([np.where((row <= col) & same, 0, -BIG), np.where((row >= col) & same, 0, -BIG)], 1))
    for k in range(NLEV):
        s = 2 ** k
        pair = row // (2 * s) == col // (2 * s)
        low = (row // s % 2 == 0) & (col // s % 2 == 1) & pair
        put(f"level{k}", np.concatenate([low, low.T], 1))
    prev, nxt = np.where(col >= row, 0, -BIG), np.where(col <= row, 0, -BIG)
    zero = np.zeros((P, P))
    put("window", np.concatenate([prev, zero, nxt], 1))
    put("chunkcol", np.stack([a // CH == c for c in range(2)], 1))
    sel = np.zeros((P, 2 * P))
    sel[0, :P] = 1
    sel[1, P:] = 1
    put("sel", sel)
    tok = np.arange(T_S)
    inv = np.power(np.float32(10000.0), np.arange(16, dtype=np.float32) * np.float32(-2.0 / 32)).astype(np.float32)
    cos, sin = [], []
    for pos in (tok // 64, tok % 64):
        ang = pos.astype(np.float32)[:, None] * inv[None, :]
        cos += [np.cos(ang), np.cos(ang)]
        sin += [-np.sin(ang), np.sin(ang)]
    for name, m in (("cos", cos), ("sin", sin)):
        m = np.concatenate(m, 1).reshape(NS, P, HD).transpose(1, 0, 2).reshape(P, NS * HD)
        put(name, m)
    return np.concatenate(parts, 1), at


CONSTS, CONST_AT = constant_tables()
FIRST = CONST_AT["ones"][0] + P
NCONST = CONSTS.shape[1]


def backbone(nc, x_prompt, x_sample, c, cache_attn_k, cache_attn_v, state_gla, cache_swa_k, cache_swa_v,
             state_delta, c_ctx, w_mod, b_mod, g_pre, g_post, w_in_even, w_out_even, qnorm_a, knorm_a,
             gla_gk_up, gla_gk_bias, gla_onorm, w_in_odd, w_out_odd, sink_c, conv_d, a_log_d, dt_bias_d,
             delta_onorm, consts, y_prompt, y_sample, new_attn_k, new_attn_v, new_gla_state, new_swa_k,
             new_swa_v, new_delta_state):
    ctx = ExitStack()
    with ctx:
        def sb(name, *shape):
            return ctx.enter_context(nc.sbuf_tensor(name, [P, *shape], F32))

        def sem(name):
            return ctx.enter_context(nc.semaphore(name))

        con = sb("con", NCONST)
        hT_base = (nc.sbuf_base + 31) // 32 * 32
        hT = sb("hT", KD, T)
        wring_base = (nc.sbuf_base + 31) // 32 * 32
        wring = sb("wring", RING, KD * SLOT)
        gg = sb("gg", 2, D)
        mods = sb("mods", 3, KD, 2)
        vecs = sb("vecs", 128)
        vecsT = sb("vecsT", 128)
        sc = sb("sc", 16)
        sinks = sb("sinks", 16)
        abz = sb("abz", NT * 16)
        WORK = (nc.sbuf_bytes_remaining - 1024) // 4
        work_base = (nc.sbuf_base + 31) // 32 * 32
        work = sb("work", WORK)
        ps = ctx.enter_context(nc.psum_tensor("ps", [P, 8, 512], F32))
        yA_dram = nc.dram_tensor("yA_gated", (4, P, T), F32, kind="Internal").ap()
        yB_dram = nc.dram_tensor("yB_gated", (T, QW), F32, kind="Internal").ap()

        def rounded(name, at, n):
            assert at + n <= WORK
            return nc.alloc_sbuf_tensor_at(name, [P, n], F32R, offset=work_base + 4 * at)


        hT_r = nc.alloc_sbuf_tensor_at("hT_r", [P, KD * T], F32R, offset=hT_base)
        wring_r = nc.alloc_sbuf_tensor_at("wring_r", [P, RING * KD * SLOT], F32R, offset=wring_base)

        class Region:
            def __init__(self, at=0):
                self.at = at

            def take(self, n):
                a = self.at
                self.at += n
                assert self.at <= WORK, (self.at, WORK)
                return work[:, a:self.at]

        def cst(name, i=0, n=None):
            o, w = CONST_AT[name]
            n = w if n is None else n
            return con[:, o + i * n:o + (i + 1) * n]

        ident, ones = cst("ident"), cst("ones")

        def wslot(i, n):
            return wring[:, i % RING, 0:KD * n].rearrange("p (k n) -> p k n", n=n)

        S = {}

        def sm(name):
            if name not in S:
                S[name] = sem(name)
            return S[name]

        phase_no = {}

        def phase_end(eng):
            n = phase_no.get(id(eng), 0) + 1
            phase_no[id(eng)] = n
            eng.drain().then_inc(sm("phase"), 1)
            eng.wait_ge(sm("phase"), 3 * n)

        def phase_seen(sp, n):
            if n:
                sp.wait_ge(sm("phase"), 3 * n)

        chunks = []
        for l, (w_in, w_out) in enumerate(((w_in_even, w_out_even), (w_in_odd, w_out_odd))):
            def cols(w, a, b):
                return [w[:, a:b].rearrange("(k p) n -> p k n", p=P)]
            chunks += [(f"mod{l}.{j}", cols(w_mod[l], 512 * j, 512 * j + 512), 512) for j in range(2 if l == 0 else 0)]
            w = w_in[0]
            if l == 0:
                chunks += [("q0", cols(w, E_Q, E_K), 512), ("kv0", cols(w, E_K, E_G), 256),
                           ("ga0", cols(w, E_G, E_BQ), 512), ("bqk", cols(w, E_BQ, E_BV), 512),
                           ("bvr", cols(w, E_BV, E_BG), 544), ("gb0", cols(w, E_BG, E_BG + 512), 512)]
            else:
                chunks += [("q1", cols(w, O_Q, O_K), 512), ("kv1", cols(w, O_K, O_G) + cols(w, O_AB, O_DG), 272),
                           ("ga1", cols(w, O_G, O_DQ), 512)]
                for h in range(4):
                    chunks.append((f"dh{h}", cols(w, O_DQ + 128 * h, O_DQ + 128 * h + 128)
                                   + cols(w, O_DK + 128 * h, O_DK + 128 * h + 128)
                                   + cols(w, O_DV + 128 * h, O_DV + 128 * h + 128), 384))
                chunks += [("gb1", cols(w, O_DG, O_DG + 512), 512)]
            chunks += [(f"out{l}.{j}", cols(w_out[0], 512 * j, 512 * j + 512), 512) for j in range(1)]
        chunk_no = {name: i for i, (name, _, _) in enumerate(chunks)}
        chunk_parts = [len(p) for _, p, _ in chunks]

        def weights(pe, name):
            i = chunk_no[name]
            n = sum(chunk_parts[j] for j in range(i % RING, i + 1, RING))
            pe.wait_ge(sm(f"w_loaded{i % RING}"), 16 * n)
            return wslot(i, chunks[i][2])

        OUT_AT = NT * QW + KD * 1024 + D
        FIN_AT = OUT_AT + KD * 512
        NF = 3
        MOD_AT = {"mod0": 7 * D, "gateA0": 0, "gateB0": NT * QW, "fin0": 3 * QW + 2 * D, "gateA1": 12 * D}
        MOD_PART = {"mod0": (0, 2), "gateA0": (0, 4), "gateB0": (1, 0), "fin0": (1, 2), "gateA1": (1, 4)}
        MOD_ORDER = list(MOD_PART)
        gpost_b = Region(9216).take(D)
        gb2 = Region(9216 + D).take(D)
        grow = Region(9216 + 2 * D).take(D)

        def mod_slots(stage):
            r = Region(MOD_AT[stage])
            slots = [r.take(KD * 512).rearrange("p (k n) -> p k n", n=512)]
            if stage == "gateA1":
                r = Region()
            return slots + [r.take(KD * 512).rearrange("p (k n) -> p k n", n=512)]

        def mod_row(stage):
            return Region(MOD_AT[stage] + 2 * KD * 512).take(D)

        def mod_load(act, stage, halves=(0, 1)):
            l, j0 = MOD_PART[stage]
            for j in halves:
                slot = mod_slots(stage)[j]
                act.dma_start(slot, w_mod[l][:, (j0 + j) * 512:(j0 + j + 1) * 512].rearrange("(k p) n -> p k n", p=P)).then_inc(sm("m_loaded"), 16)

        w_out_b = Region(OUT_AT).take(KD * 512).rearrange("p (k n) -> p k n", n=512)

        def out_load(act, l):
            act.dma_start(w_out_b, (w_out_even, w_out_odd)[l][0][:, 512:1024].rearrange("(k p) n -> p k n", p=P)).then_inc(sm("wo_loaded"), 16)

        def mod_weights(pe, stage):
            pe.wait_ge(sm("m_loaded"), 32 * (MOD_ORDER.index(stage) + 1))
            return mod_slots(stage)

        def bias_sp(sp, l):
            d = sm("vec_loaded")
            sp.dma_start(vecs[0:24, :], b_mod[l].rearrange("(r p) -> r p", p=P)).then_inc(d, 16)
            sp.dma_start(vecs[24:32, :], g_pre[l].rearrange("(r p) -> r p", p=P)).then_inc(d, 16)
            if l == 0:
                sp.dma_start(vecs[32:40, :], c[0].rearrange("(r p) -> r p", p=P)).then_inc(d, 16)
                sp.dma_start(vecs[40:48, :], c_ctx.rearrange("(r p) -> r p", p=P)).then_inc(d, 16)

        scv = sc[:, :].rearrange("p (c k) -> p k c", c=2)

        def rows_pe(pe, w, bank):
            for j in range(2):
                for k in range(KD):
                    mm = pe.matmul(ps[0:2, bank + j, :], scv[:, k, :], w[j][:, k, :], start=(k == 0), stop=(k == KD - 1))
            return mm

        def columns_pe(pe, stage, n, w, bank):
            rows = mod_row(stage)
            rows_pe(pe, w, bank).then_inc(sm("mrow_ps"), 1)
            pe.wait_ge(sm("mrow"), n)
            for k in range(KD):
                mm = pe.transpose(ps[:, bank + 2, 2 * k:2 * k + 2], rows[0:2, k * P:(k + 1) * P], ident[0:2, 0:2])
            mm.then_inc(sm("cols_ps"), 1)

        def columns_dve(v, stage, i, bank, n):
            v.wait_ge(sm("mrow_ps"), n)
            v.tensor_copy(mod_row(stage)[0:2, :].rearrange("p (a n) -> p a n", a=2), ps[0:2, bank:bank + 2, :]).then_inc(sm("mrow"), 1)
            v.wait_ge(sm("cols_ps"), n)
            m = ps[:, bank + 2, 0:16].rearrange("p (k c) -> p k c", c=2)
            bias = vecsT[:, 8 * i:8 * i + 8].unsqueeze(2).to_broadcast([P, 8, 2])
            if i == 0:
                v.tensor_tensor(mods[:, 0, :, :], m, bias, ALU.add)
            else:
                v.tensor_tensor(mods[:, 2, :, :], m, bias, ALU.add)
                v.drain()
                v.scalar_tensor_tensor(mods[:, 1, :, :], mods[:, 2, :, :], 1.0,
                                       vecsT[:, 24:32].unsqueeze(2).to_broadcast([P, 8, 2]), ALU.add, ALU.mult)

        def mod_sp(sp):
            bias_sp(sp, 0)

        def mod_pe(pe):
            pe.wait_ge(sm("vec_loaded"), 64)
            pe.transpose(ps[:, 0, 0:48], vecs[0:48, :], ident[0:48, 0:48]).then_inc(sm("vecT_ps"), 1)
            pe.wait_ge(sm("cond_silu"), 1)
            columns_pe(pe, "mod0", 1, [weights(pe, f"mod0.{j}") for j in range(2)], 1)
            pe.drain().then_inc(sm("w_used"), 2)
            columns_pe(pe, "mod0", 2, mod_weights(pe, "mod0"), 4)
            phase_end(pe)

        def mod_act(act):
            mod_load(act, "mod0")
            act.wait_ge(sm("vecT_ps"), 1)
            act.activation(vecsT[:, 0:48], ps[:, 0, 0:48], ACT.Copy)
            act.activation(sc[:, :], ps[:, 0, 32:48], ACT.Silu).then_inc(sm("cond_silu"), 1)
            phase_end(act)

        def mod_dve(v):
            v.wait_ge(sm("cond_silu"), 1)
            for i in range(2):
                columns_dve(v, "mod0", i, 1 + 3 * i, i + 1)
            phase_end(v)

        def gates_sp(sp, l):
            sp.dma_start(gpost_b, g_post[l].partition_broadcast(P)).then_inc(sm("gate_in"), 16)
            sp.dma_start(gb2[0:2, :], b_mod[l, 2 * D:].partition_broadcast(2)).then_inc(sm("gate_in"), 16)

        def gates_pe(pe, l):
            rows_pe(pe, mod_weights(pe, f"gateA{l}"), 2).then_inc(sm("grow_ps"), 1)
            pe.wait_ge(sm("gate_rows"), l + 1)
            for cnd in range(2):
                for j in range(2):
                    mm = pe.matmul(ps[:, 4 + 2 * cnd + j, :], cst("sel", cnd, P)[0:2, :],
                                   grow[0:2, j * 512:(j + 1) * 512], start=True, stop=True)
            mm.then_inc(sm("gate_ps"), 1)

        def gates_dve(v, l):
            v.wait_ge(sm("gate_in"), (32, 112)[l])
            v.wait_ge(sm("grow_ps"), l + 1)
            v.tensor_tensor(grow[0:2, :].rearrange("p (a n) -> p a n", a=2), ps[0:2, 2:4, :],
                            gb2[0:2, :].rearrange("p (a n) -> p a n", a=2), ALU.add).then_inc(sm("gate_rows"), 1)
            v.wait_ge(sm("gate_ps"), l + 1)
            for cnd in range(2):
                v.tensor_tensor(gg[:, cnd, :].rearrange("p (a n) -> p a n", a=2), ps[:, 4 + 2 * cnd:6 + 2 * cnd, :],
                                gpost_b.rearrange("p (a n) -> p a n", a=2), ALU.mult)

        ar = Region()
        NX = 3
        a_x = [ar.take(D) for _ in range(NX)]
        a_xh = [ar.take(D) for _ in range(2)]
        a_junk = ar.take(D)
        a_st = [ar.take(4) for _ in range(2)]

        def xT_ps(t, k):
            b, j = (0, k) if k < 4 else (1, k - 4) if k < 6 else (2, k - 6)
            return ps[:, 3 * (t % 2) + b, j * P:(j + 1) * P]

        def x_rows(l, t):
            if l == 0:
                return x_prompt[0] if t == NS else x_sample[0, t * P:(t + 1) * P, :]
            return y_prompt[0] if t == NS else y_sample[0, t * P:(t + 1) * P, :]

        def ada_sp(sp, l, n):
            phase_seen(sp, n)
            for t in range(NT):
                if t >= NX:
                    sp.wait_ge(sm("xh_done"), NT * l + t - NX + 1)
                sp.dma_start(a_x[t % NX], x_rows(l, t)).then_inc(sm(f"x_loaded{t % NX}"), 16)
                if l == 0 and t == 1:
                    sp.dma_start(con[:, FIRST:], consts[:, FIRST:]).then_inc(sm("rest_in"), 16)

        def x_load_count(l, t):
            return 16 * (NT // NX * l + t // NX + 1)

        def ada_act(act, l):
            for t in range(NT):
                act.wait_ge(sm(f"x_loaded{t % NX}"), x_load_count(l, t))
                if t >= 2:
                    act.wait_ge(sm("xh_done"), NT * l + t - 1)
                act.activation(a_junk, a_x[t % NX], ACT.Square, accum_out=a_st[t % 2][:, 0:1])
                act.drain()
                act.activation(a_st[t % 2][:, 1:2], a_st[t % 2][:, 0:1], ACT.Ln, scale=1.0 / D, bias=eps_col)
                act.drain()
                act.activation(a_st[t % 2][:, 2:3], a_st[t % 2][:, 1:2], ACT.Exp, scale=-0.5).then_inc(sm("x_rs"), 1)
                if t >= 1:
                    ada_evac_act(act, l, t - 1)
            ada_evac_act(act, l, NT - 1)
            phase_end(act)

        def ada_evac_act(act, l, t):
            act.wait_ge(sm("xT_ps"), NT * l + t + 1)
            cnd = int(t == NS)
            for k in range(6, KD):
                mm = act.activation(hT[:, k, t * P:(t + 1) * P], xT_ps(t, k),
                                    ACT.Identity, scale=mods[:, 1, k, cnd:cnd + 1], bias=mods[:, 0, k, cnd:cnd + 1])
            mm.then_inc(sm("hT_act"), 1)

        def ada_dve(v, l):
            for t in range(NT):
                v.wait_ge(sm("x_rs"), NT * l + t + 1)
                if t >= 2:
                    v.wait_ge(sm("xT_ps"), NT * l + t - 1)
                v.tensor_scalar(a_xh[t % 2], a_x[t % NX], a_st[t % 2][:, 2:3], None, ALU.mult).then_inc(sm("xh_done"), 1)
                if t >= 1:
                    ada_evac_dve(v, l, t - 1)
            ada_evac_dve(v, l, NT - 1)
            phase_end(v)

        def ada_evac_dve(v, l, t):
            v.wait_ge(sm("xT_ps"), NT * l + t + 1)
            cnd = int(t == NS)
            for k in range(6):
                mm = v.tensor_scalar(hT[:, k, t * P:(t + 1) * P], xT_ps(t, k),
                                     mods[:, 1, k, cnd:cnd + 1], mods[:, 0, k, cnd:cnd + 1], ALU.mult, ALU.add)
            mm.then_inc(sm("hT_dve"), 1)

        def ada_pe(pe, l):
            for t in range(NT):
                pe.wait_ge(sm("xh_done"), NT * l + t + 1)
                if t >= 2:
                    pe.wait_ge(sm("hT_act"), NT * l + t - 1)
                    pe.wait_ge(sm("hT_dve"), NT * l + t - 1)
                for k in range(KD):
                    mm = pe.transpose(xT_ps(t, k), a_xh[t % 2][:, k * P:(k + 1) * P], ident)
                mm.then_inc(sm("xT_ps"), 1)
            phase_end(pe)

        R65 = slice(0, HD + 1)
        LOW, HIGH = slice(0, HD), slice(HD, P)
        qr = Region()

        def take_rounded(region, name, n):
            region.at = at = (region.at + 7) // 8 * 8
            region.take(n)
            return rounded(name, at, n)[:, :]

        qA = take_rounded(qr, "qA", 8 * T).rearrange("p (h t) -> p h t", h=8)
        kA = take_rounded(qr, "kA", 2 * 10 * P).rearrange("p (g n) -> p g n", g=2)
        kB = take_rounded(qr, "kB", 2 * 10 * P).rearrange("p (g n) -> p g n", g=2)
        vaug = qr.take(2 * 10 * P).rearrange("p (g t n) -> p g t n", g=2, n=P)
        yA = qr.take(4 * T).rearrange("p (b t) -> p b t", b=4)
        at_qkv = qr.at
        q_sq = qr.take(640)
        q_n = [qr.take(640) for _ in range(2)]
        q_t1 = qr.take(640)
        q_t2 = qr.take(640)
        q_r = [qr.take(640) for _ in range(2)]
        q_st = qr.take(32)
        ck = qr.take(P)
        wqk = qr.take(128)
        ar2 = Region(at_qkv)
        qB_at = ar2.at
        assert qB_at % 8 == T % 8 == 0
        qB = [take_rounded(ar2, f"qB{i}", T) for i in range(2)]
        qB_plain = [Region(qB_at + i * T).take(T) for i in range(2)]
        ES = slice(96, 97)
        pT = [ar2.take(512) for _ in range(3)]
        a_part = ar2.take(3 * NS)
        a_mx = ar2.take(NT)
        a_nm = [ar2.take(NT) for _ in range(2)]
        a_ri = [ar2.take(512) for _ in range(2)]
        ident_r = take_rounded(ar2, "ident_r", P)
        window_r = take_rounded(ar2, "window_r", 3 * P)
        k_out = ar2.take(P)
        assert ar2.at - P >= qr.at
        sumrow = ar2.take(P)

        def heads(ap, g=2):
            return ap.rearrange("p (g j d) -> p g j d", g=g, d=HD)

        def qkv_sp(sp, l, n):
            phase_seen(sp, n)
            d = sm("qkv_in")
            kc, vc = ((cache_attn_k, cache_attn_v), (cache_swa_k, cache_swa_v))[l]
            sp.dma_start(ck, kc[0, 0].rearrange("t g d -> t (g d)")).then_inc(d, 16)
            sp.dma_start(vaug[:, :, CTX, 0:HD], vc[0, 0]).then_inc(d, 16)
            if l == 0:
                sp.dma_start(wqk[:, 0:HD], qnorm_a[0].partition_broadcast(P)).then_inc(d, 16)
                sp.dma_start(wqk[:, HD:2 * HD], knorm_a[0].partition_broadcast(P)).then_inc(d, 16)
            ko, vo = ((new_attn_k, new_attn_v), (new_swa_k, new_swa_v))[l]
            sp.wait_ge(sm("qkr_done"), NT * (l + 1))
            sp.dma_start(ko[0, 0].rearrange("t g d -> t (g d)"), k_out).then_inc(sm("kv_stored"), 16)
            sp.wait_ge(sm("v_done"), NT * (l + 1))
            sp.dma_start(vo[0, 0], vaug[:, :, PROMPT_KEYS, 0:HD]).then_inc(sm("kv_stored"), 16)
            sp.wait_ge(sm("kv_stored"), 32 * (l + 1))
            sp.sem_inc(sm("phase_sp"), 1)

        def qkv_in_count(l):
            return (64, 96)[l]

        def qkv_pe(pe, l):
            wq, wkv = weights(pe, f"q{l}"), weights(pe, f"kv{l}")
            pe.wait_ge(sm("qkv_in"), qkv_in_count(l))
            for t in range(NT + 1):
                if t < NT:
                    if t >= 2:
                        pe.wait_ge(sm("qk_free"), NT * l + t - 1)
                        pe.wait_ge(sm("v_done"), NT * l + t - 1)
                    for w, b, n in ((wq, 0, 512), (wkv, 1, (256, 272)[l])):
                        for k in range(KD):
                            mm = pe.matmul(ps[:, 2 * (t % 2) + b, 0:n], hT[:, k, t * P:(t + 1) * P], w[:, k, :],
                                           start=(k == 0), stop=(k == KD - 1))
                    mm.then_inc(sm("qkv_ps"), 1)
                    if t == NT - 1:
                        pe.drain().then_inc(sm("w_used"), 2)
                if t == 0:
                    pe.transpose(ps[:, 7, 128:256], ck, ident).then_inc(sm("ckT_ps"), 1)
                if t >= 1:
                    u = t - 1
                    pe.wait_ge(sm("qkr_done"), NT * l + u + 1)
                    if u >= 2:
                        pe.wait_ge(sm("qkT_done"), NT * l + u - 1)
                    if u == 1:
                        pe.wait_ge(sm("qkT_done"), NT * l + 1)
                    r = q_r[u % 2]
                    for j in range(5):
                        mm = pe.transpose(ps[:, 4 + 2 * (u % 2) + j // 4, (j % 4) * P:(j % 4 + 1) * P],
                                          r[:, j * P:(j + 1) * P], ident)
                    mm.then_inc(sm("qkT_ps"), 1)
            phase_end(pe)

        def keys_high(act, src, tile):
            cols = slice(tile * P, (tile + 1) * P)
            for g in range(2):
                for half in (LOW, HIGH):
                    mm = act.activation(kA[half, g, cols], src[HD * g:HD * g + HD, :], ACT.Copy)
            return mm

        def keys_low(v, src, tile):
            cols = slice(tile * P, (tile + 1) * P)
            for g in range(2):
                half = slice(HD * g, HD * g + HD)
                mm = v.tensor_tensor(kB[LOW, g, cols], src[half, :], kA[half, g, cols].bitcast(F32), ALU.subtract)
            return mm

        def key_tile(u):
            return PROMPT_KEYS if u == NS else u

        def qkv_act(act, l):
            act.wait_ge(sm("ckT_ps"), l + 1)
            keys_high(act, ps[:, 7, 128:256], CTX)
            for t in range(NT + 1):
                if t < NT:
                    a, b = ps[:, 2 * (t % 2), :], ps[:, 2 * (t % 2) + 1, :]
                    act.wait_ge(sm("qkv_ps"), NT * l + t + 1)
                    if l == 0:
                        if t >= 1:
                            act.wait_ge(sm("qk_ss"), t)
                        act.activation(q_sq[:, 0:512], a, ACT.Square)
                        act.activation(q_sq[:, 512:640], b[:, 0:128], ACT.Square).then_inc(sm("qk_sq"), 1)
                    if l == 1:
                        act.wait_ge(sm("qk_free"), NT * l + t + 1)
                        act.activation(abz[:, 16 * t:16 * t + 16], b[:, 256:272], ACT.Copy)
                    vdst = PROMPT_KEYS if t == NS else t
                    act.activation(vaug[:, :, vdst, 0:HD], b[:, 128:256].rearrange("p (g d) -> p g d", g=2), ACT.Copy).then_inc(sm("v_done"), 1)
                    if l == 0:
                        act.wait_ge(sm("qk_ss"), t + 1)
                        if t >= 1:
                            act.wait_ge(sm("qk_free"), t)
                        act.activation(q_st[:, 10:20], q_st[:, 0:10], ACT.Ln, scale=1.0 / HD, bias=eps_col)
                        act.drain()
                        act.activation(q_st[:, 20:30], q_st[:, 10:20], ACT.Exp, scale=-0.5).then_inc(sm("qk_rs"), 1)
                if t >= 1:
                    u = t - 1
                    act.wait_ge(sm("qkT_ps"), NT * l + u + 1)
                    bk = 4 + 2 * (u % 2)
                    src = ps[:, bk, :].rearrange("p (j t) -> p j t", j=4)
                    cols = slice(u * P, (u + 1) * P)
                    act.activation(qA[LOW, 0:4, cols], src[LOW], ACT.Copy)
                    act.activation(qA[LOW, 4:8, cols], src[HIGH], ACT.Copy)
                    act.activation(qA[HIGH, 4:8, cols], src[HIGH], ACT.Copy)
                    keys_high(act, ps[:, bk + 1, 0:P], key_tile(u)).then_inc(sm("qkT_high"), 1)
            phase_end(act)

        def qkv_dve(v, l):
            v.memset(vaug[:, :, :, HD:P], 1.0)
            v.memset(kB[HD:HD + 1, :, :].bitcast(F32), 1.0)

            def low_parts(u):
                v.wait_ge(sm("qkT_high"), NT * l + u + 1)
                bk = 4 + 2 * (u % 2)
                src = ps[:, bk, :].rearrange("p (j t) -> p j t", j=4)
                cols = slice(u * P, (u + 1) * P)
                v.tensor_tensor(qA[HIGH, 0:4, cols], src[LOW], qA[LOW, 0:4, cols].bitcast(F32), ALU.subtract)
                v.tensor_tensor(qA[HIGH, 4:8, cols], src[HIGH], qA[HIGH, 4:8, cols].bitcast(F32), ALU.subtract)
                if u == 0:
                    keys_low(v, ps[:, 7, 128:256], CTX)
                keys_low(v, ps[:, bk + 1, 0:P], key_tile(u)).then_inc(sm("qkT_done"), 1)

            v.wait_ge(sm("qkv_in"), qkv_in_count(l))
            for t in range(NT):
                a, b = ps[:, 2 * (t % 2), :], ps[:, 2 * (t % 2) + 1, 0:128]
                n, r = q_n[t % 2], q_r[t % 2]
                if l == 0:
                    v.wait_ge(sm("qk_sq"), t + 1)
                    if t >= 1:
                        v.wait_ge(sm("qk_rs"), t)
                    v.tensor_reduce(q_st[:, 0:10], q_sq.rearrange("p (h d) -> p h d", d=HD), AX.X, ALU.add).then_inc(sm("qk_ss"), 1)
                    v.wait_ge(sm("qk_rs"), t + 1)
                    rsb = q_st[:, 20:30].unsqueeze(2).to_broadcast([P, 10, HD])
                    v.tensor_tensor(q_t1[:, 0:512].rearrange("p (h d) -> p h d", d=HD), a.rearrange("p (h d) -> p h d", d=HD), rsb[:, 0:8, :], ALU.mult)
                    v.tensor_tensor(q_t1[:, 512:640].rearrange("p (h d) -> p h d", d=HD), b.rearrange("p (h d) -> p h d", d=HD), rsb[:, 8:10, :], ALU.mult).then_inc(sm("qk_free"), 1)
                    v.drain()
                    for o, m, w in ((0, 8, wqk[:, 0:HD]), (512, 2, wqk[:, HD:2 * HD])):
                        v.tensor_tensor(n[:, o:o + m * HD].rearrange("p (h d) -> p h d", d=HD),
                                        q_t1[:, o:o + m * HD].rearrange("p (h d) -> p h d", d=HD),
                                        w.unsqueeze(1).to_broadcast([P, m, HD]), ALU.mult)
                    v.drain()
                else:
                    v.wait_ge(sm("qkv_ps"), NT * l + t + 1)
                    v.tensor_copy(n[:, 0:512], a)
                    v.tensor_copy(n[:, 512:640], b).then_inc(sm("qk_free"), 1)
                    v.drain()
                if t >= 2:
                    v.wait_ge(sm("qkT_ps"), NT * l + t - 1)
                rq = r[:, 0:512].rearrange("p (j g d) -> p g j d", g=2, d=HD)
                if t == NS:
                    for g in range(2):
                        v.tensor_copy(rq[:, g], heads(n[:, 0:512])[:, g])
                    v.tensor_copy(k_out, n[:, 512:640])
                    v.tensor_copy(r[:, 512:640], n[:, 512:640]).then_inc(sm("qkr_done"), 1)
                else:
                    cosb = cst("cos", t, HD).unsqueeze(1).to_broadcast([P, 10, HD])
                    sinb = cst("sin", t, HD)
                    v.tensor_tensor(q_t1.rearrange("p (h d) -> p h d", d=HD), n.rearrange("p (h d) -> p h d", d=HD), cosb, ALU.mult)
                    nh = n.rearrange("p (h a s f) -> p h a s f", a=2, s=2, f=16)
                    th = q_t2.rearrange("p (h a s f) -> p h a s f", a=2, s=2, f=16)
                    sh = sinb.rearrange("p (a s f) -> p a s f", a=2, s=2)
                    for s in range(2):
                        v.tensor_tensor(th[:, :, :, s, :], nh[:, :, :, 1 - s, :],
                                        sh[:, :, s, :].unsqueeze(1).to_broadcast([P, 10, 2, 16]), ALU.mult)
                    v.drain()
                    for g in range(2):
                        v.tensor_tensor(rq[:, g], heads(q_t1[:, 0:512])[:, g], heads(q_t2[:, 0:512])[:, g], ALU.add)
                    v.tensor_tensor(r[:, 512:640], q_t1[:, 512:640], q_t2[:, 512:640], ALU.add).then_inc(sm("qkr_done"), 1)
                if t:
                    low_parts(t - 1)
            low_parts(NT - 1)
            phase_end(v)

        def key_tiles(l, b):
            if b == NS:
                return [PROMPT_KEYS]
            if l == 0:
                return list(range(NS + 1))
            return ([b - 1] if b > 0 else []) + [b] + ([b + 1] if b < NS - 1 else []) + [CTX]

        CHUNKS = [(0, 4), (4, 8), (8, 9)]

        def products(l):
            out = []
            for h in range(8):
                for c_, (qa, qb) in enumerate(CHUNKS):
                    if c_ == 2:
                        of = [(PROMPT_KEYS, qa, qb)]
                    elif l == 0:
                        of = [(k, qa, qb) for k in range(NS + 1)]
                    else:
                        of = [(CTX, qa, qb)] + [(k, max(k - 1, qa), min(k + 2, qb)) for k in range(max(qa - 1, 0), min(qb + 1, NS))]
                    out += [(h, k, a, b, c_, i == 0, i == len(of) - 1) for i, (k, a, b) in enumerate(of)]
            return out

        PRODUCTS = [products(l) for l in range(2)]
        AHEAD = 2
        ST_BANKS = (2, 3, 4)
        UNITS = [[(u, tiles) for u in range(NT)
                  for tiles in ([[0, 1, 2, 3], [4, 5, 6, 7], [CTX]] if u < NS else [[PROMPT_KEYS]])],
                 [(u, key_tiles(1, u)) for u in range(NT)]]
        MU = [len(x) for x in UNITS]
        assert all((m + 3) % 2 == 0 for m in MU)

        def att_steps(l):
            items = PRODUCTS[l]
            per = len(items) // 8
            spread = per - (4, 6)[l]
            for m in range(MU[l]):
                yield "max", 0, m
            for r in range(3):
                yield "row", 0, r
            for i in range(len(items) + AHEAD):
                if i < len(items):
                    h, p = i // per, i % per
                    yield "scores", i, 0
                    if h < 7:
                        if p < spread:
                            for m in range(MU[l] * p // spread, MU[l] * (p + 1) // spread):
                                yield "max", h + 1, m
                        elif spread < p <= spread + 3:
                            yield "row", h + 1, p - spread - 1
                if i >= AHEAD:
                    yield "values", i - AHEAD, 0
                    if items[i - AHEAD][6]:
                        yield "out", items[i - AHEAD][0], items[i - AHEAD][4]

        def unit_count(l, h, m):
            return 8 * MU[0] * l + MU[l] * h + m

        def last_product(l, h, c_=2):
            return max(i for i, x in enumerate(PRODUCTS[l]) if x[0] == h and x[4] == c_)

        def masked(l, i):
            h, kt, qa, qb, c_, _, _ = PRODUCTS[l][i]
            return l == 1 and kt not in (CTX, PROMPT_KEYS)

        ROW_TILES = [(0, 4), (4, 8), (8, 9)]

        def att_pe(pe, l):
            base = l * len(PRODUCTS[0])
            if l == 1:
                pe.wait_ge(sm("masks_in"), 1)
            for what, x, y in att_steps(l):
                if what == "max":
                    h, m = x, y
                    g = h // 4
                    if m >= 2:
                        pe.wait_ge(sm("mx_used"), unit_count(l, h, m) - 1)
                    elif h:
                        pe.wait_ge(sm("row_out"), 3 * (8 * l + h) - 1 + m)
                    u, tiles = UNITS[l][m]
                    i = 0
                    while i < len(tiles):
                        n = 1
                        while i + n < len(tiles) and tiles[i + n] == tiles[i] + n and (l == 0 or tiles[i + n] != CTX):
                            n += 1
                        band = l == 1 and tiles[i] < NS
                        mm = pe.matmul(ps[:, m % 2, i * P:(i + n) * P], qA[:, h, u * P:(u + 1) * P],
                                       kA[:, g, tiles[i] * P:(tiles[i] + n) * P], start=True, stop=not band)
                        if band:
                            o = tiles[i] - (u - 1)
                            mm = pe.matmul(ps[:, m % 2, i * P:(i + n) * P], ident_r, window_r[:, o * P:(o + n) * P],
                                           start=False, stop=True)
                        i += n
                    mm.then_inc(sm("mx_ps"), 1)
                elif what == "row":
                    h, r = x, y
                    pe.wait_ge(sm("nm_done"), 8 * l + h + 1)
                    if r == 2:
                        pe.wait_ge(sm("row_out"), 3 * (8 * l + h) + 1)
                    for t in range(*ROW_TILES[r]):
                        mm = pe.matmul(ps[HD:HD + 1, (MU[l] + r) % 2, (t - ROW_TILES[r][0]) * P:(t - ROW_TILES[r][0] + 1) * P],
                                       a_nm[h % 2][:, t:t + 1], ident, start=True, stop=True)
                    mm.then_inc(sm("row_ps"), 1)
                elif what == "scores":
                    i = x
                    h, kt, qa, qb, c_, first, last = PRODUCTS[l][i]
                    nb = len(ST_BANKS)
                    if first and c_ == 0:
                        pe.wait_ge(sm("row_out"), 3 * (8 * l + h) + 3)
                    if i >= nb:
                        pe.wait_ge(sm("p_done"), base + i - nb + 1)
                    s_ = ps[:, ST_BANKS[i % nb], 0:(qb - qa) * P]
                    pe.matmul(s_, kA[:, h // 4, kt * P:(kt + 1) * P], qA[:, h, qa * P:qb * P], start=True, stop=False)
                    mm = pe.matmul(s_, kB[R65, h // 4, kt * P:(kt + 1) * P],
                                   qB[h % 2][R65, qa * P:qb * P], start=False, stop=not masked(l, i))
                    if masked(l, i):
                        o = qa - (kt - 1)
                        mm = pe.matmul(s_, ident_r, window_r[:, o * P:(o + qb - qa) * P], start=False, stop=True)
                    mm.then_inc(sm("s_ps"), 1)
                elif what == "values":
                    i = x
                    h, kt, qa, qb, c_, first, last = PRODUCTS[l][i]
                    q0, q1 = CHUNKS[c_]
                    if first and h:
                        pe.wait_ge(sm("y_done"), 3 * (8 * l + h - 1) + c_ + 1)
                    pe.wait_ge(sm("p_done"), base + i + 1)
                    if first and l == 1:
                        pe.matmul(ps[:, 5 + c_, 0:(q1 - q0) * P], sumrow[ES, :], qB_plain[h % 2][ES, q0 * P:q1 * P],
                                  start=True, stop=False, skip_group_check=True)
                    pe.matmul(ps[:, 5 + c_, (qa - q0) * P:(qb - q0) * P], vaug[:, h // 4, kt, :],
                              pT[i % 3][:, 0:(qb - qa) * P], start=(first and l == 0), stop=last,
                              skip_group_check=True).then_inc(sm("pv_ps"), 1)
            phase_end(pe)

        def att_dve(v, l):
            v.memset(sumrow[ES, 0:HD], 0.0)
            v.memset(sumrow[ES, HD:P], 1.0)
            base = l * len(PRODUCTS[0])
            if l == 1:
                v.tensor_scalar(sinks[:, 8:16], sinks[:, 0:8], -8.0, None, ALU.mult)
                v.tensor_copy(ident_r, ident)
                v.tensor_copy(window_r, cst("window")).then_inc(sm("masks_in"), 1)
            v.drain()
            for what, x, y in att_steps(l):
                if what == "max":
                    h, m = x, y
                    u, tiles = UNITS[l][m]
                    v.wait_ge(sm("mx_ps"), unit_count(l, h, m) + 1)
                    n = len(tiles) * P
                    src = ps[:, m % 2, 0:n]
                    dst = a_mx[:, u:u + 1]
                    if l == 0 and u < NS:
                        dst = a_part[:, m:m + 1]
                    v.tensor_reduce(dst, src, AX.X, ALU.max).then_inc(sm("mx_used"), 1)
                    if m == MU[l] - 1:
                        if h >= 2:
                            v.wait_ge(sm("s_ps"), base + last_product(l, h - 2) + 1)
                        v.tensor_copy(qB[h % 2][LOW, :], qA[LOW, h, :])
                        v.drain()
                        if h >= 2:
                            v.wait_ge(sm("row_ps"), 3 * (8 * l + h - 1))
                        if l == 0:
                            v.tensor_reduce(a_mx[:, 0:NS], a_part.rearrange("p (u n) -> p u n", n=3), AX.X, ALU.max)
                            v.drain()
                            v.tensor_scalar(a_nm[h % 2], a_mx, -1.0, None, ALU.mult).then_inc(sm("nm_done"), 1)
                        else:
                            v.tensor_scalar(a_nm[h % 2], a_mx, -1.0, sinks[:, 8 + h:9 + h], ALU.mult, ALU.min).then_inc(sm("nm_done"), 1)
                elif what == "out":
                    h, c_ = x, y
                    q0, q1 = CHUNKS[c_]
                    v.wait_ge(sm("ri_done"), 3 * (8 * l + h) + c_ + 1)
                    v.tensor_tensor(yA[HD * (h % 2):HD * (h % 2) + HD, h // 2, q0 * P:q1 * P], ps[0:HD, 5 + c_, 0:(q1 - q0) * P],
                                    a_ri[(3 * h + c_) % 2][0:HD, 0:(q1 - q0) * P], ALU.mult).then_inc(sm("y_done"), 1)
            phase_end(v)

        def att_act(act, l):
            base = l * len(PRODUCTS[0])
            for what, x, y in att_steps(l):
                if what == "row":
                    h, r = x, y
                    if r == 0:
                        if h >= 2:
                            act.wait_ge(sm("pv_ps"), base + last_product(l, h - 2) + 1)
                    t0, t1 = ROW_TILES[r]
                    cols = slice(t0 * P, t1 * P)
                    act.wait_ge(sm("row_ps"), 3 * (8 * l + h) + r + 1)
                    maxima = qB[h % 2][HD:HD + 1, cols]
                    mm = act.activation(maxima, ps[HD:HD + 1, (MU[l] + r) % 2, 0:(t1 - t0) * P], ACT.Copy)
                    if l == 1:
                        act.drain()
                        mm = act.activation(qB_plain[h % 2][ES, cols], maxima.bitcast(F32), ACT.Exp, scale=0.125, bias=sinks[HD:HD + 1, h:h + 1])
                    mm.then_inc(sm("row_out"), 1)
                elif what == "scores":
                    i = x
                    _, kt, qa, qb, _, _, _ = PRODUCTS[l][i]
                    act.wait_ge(sm("s_ps"), base + i + 1)
                    if i >= 3:
                        act.wait_ge(sm("pv_ps"), base + i - 2)
                    n = (qb - qa) * P
                    act.activation(pT[i % 3][:, 0:n], ps[:, ST_BANKS[i % len(ST_BANKS)], 0:n], ACT.Exp, scale=0.125).then_inc(sm("p_done"), 1)
                elif what == "out":
                    h, c_ = x, y
                    n = 3 * (8 * l + h) + c_
                    m = (CHUNKS[c_][1] - CHUNKS[c_][0]) * P
                    act.wait_ge(sm("pv_ps"), base + last_product(l, h, c_) + 1)
                    if n >= 2:
                        act.wait_ge(sm("y_done"), n - 1)
                    act.drain()
                    act.activation(a_ri[(3 * h + c_) % 2][HD:P, 0:m], ps[HD:P, 5 + c_, 0:m], ACT.Ln)
                    act.drain()
                    act.activation(a_ri[(3 * h + c_) % 2][0:HD, 0:m], a_ri[(3 * h + c_) % 2][HD:P, 0:m], ACT.Exp, scale=-1.0).then_inc(sm("ri_done"), 1)
            phase_end(act)

        GATE_AT = WORK - 3240
        gr_ = Region(GATE_AT)
        g_sl = [gr_.take(QW) for _ in range(2)]
        g_y = [gr_.take(QW) for _ in range(2)]
        g_e = gr_.take(QW)
        g_sq = gr_.take(QW)
        g_on = gr_.take(P)
        g_st = gr_.take(12)
        TOKENS = [(0, 512), (512, 512), (T_S, T_P)]

        def gateA_pe(pe, l):
            w = weights(pe, f"ga{l}")
            for n in range(12):
                b, (o, m) = n // 3, TOKENS[n % 3]
                if l == 1 and n == 1:
                    ab_pe(pe)
                if l == 1 and n == 6:
                    ab_sums_pe(pe)
                if n >= 2:
                    pe.wait_ge(sm("gA_silu"), 12 * l + n - 1)
                for k in range(KD):
                    mm = pe.matmul(ps[:, n % 2, 0:m], w[:, k, b * P:(b + 1) * P], hT[:, k, o:o + m], start=(k == 0), stop=(k == KD - 1))
                mm.then_inc(sm("gA_mm"), 1)
            pe.drain().then_inc(sm("w_used"), 1)
            if l == 1:
                pe.wait_ge(sm("c_ex"), 1)
            gates_pe(pe, l)
            phase_end(pe)

        def gateA_act(act, l):
            if l == 1:
                ab_act(act)
            mod_load(act, f"gateA{l}")
            for n in range(12):
                m = TOKENS[n % 3][1]
                act.wait_ge(sm("gA_mm"), 12 * l + n + 1)
                if n >= 2:
                    act.wait_ge(sm("gA_done"), 12 * l + n - 1)
                act.activation(g_sl[n % 2][:, 0:m], ps[:, n % 2, 0:m], ACT.Silu).then_inc(sm("gA_silu"), 1)
            if l == 1:
                ab_sums_act(act)
            phase_end(act)

        def gateA_dve(v, l):
            if l == 1:
                ab_dve(v)
            for n in range(12):
                b, (o, m) = n // 3, TOKENS[n % 3]
                v.wait_ge(sm("gA_silu"), 12 * l + n + 1)
                y = yA[:, b, o:o + m]
                v.tensor_tensor(y, g_sl[n % 2][:, 0:m], y, ALU.mult).then_inc(sm("gA_done"), 1)
            if l == 1:
                ab_sums_dve(v)
            gates_dve(v, l)
            phase_end(v)

        def gateA_sp(sp, l, n):
            phase_seen(sp, n)
            if l == 1:
                ab_sp(sp)
            gates_sp(sp, l)
            for b in range(4):
                sp.wait_ge(sm("gA_done"), 12 * l + 3 * b + 3)
                sp.dma_start(yA_dram[b], yA[:, b, :]).then_inc(sm("yA_stored"), 16)
            sp.wait_ge(sm("yA_stored"), 64 * (l + 1))
            sp.sem_inc(sm("phase_sp"), 1)

        def gate_pe(pe, l):
            w = weights(pe, f"gb{l}")
            for t in range(NT):
                if t >= 2:
                    pe.wait_ge(sm("gate_free"), NT * l + t - 1)
                for k in range(KD):
                    mm = pe.matmul(ps[:, t % 2, :], hT[:, k, t * P:(t + 1) * P], w[:, k, :], start=(k == 0), stop=(k == KD - 1))
                mm.then_inc(sm("gate_mm"), 1)
            pe.drain().then_inc(sm("w_used"), 1)
            if l == 0:
                pe.wait_ge(sm("vec_loaded"), 96)
                pe.transpose(ps[:, 2, 0:32], vecs[0:32, :], ident[0:32, 0:32]).then_inc(sm("vecT_ps"), 1)
                columns_pe(pe, "gateB0", 3, mod_weights(pe, "gateB0"), 3)
            phase_end(pe)

        def gate_act(act, l):
            if l == 0:
                mod_load(act, "gateB0")
            out_load(act, l)
            for t in range(NT):
                n = NT * l + t
                if t:
                    act.wait_ge(sm("on_ss"), n)
                act.activation(g_sq, ob[:, t, :], ACT.Square).then_inc(sm("on_sq"), 1)
                act.wait_ge(sm("on_ss"), n + 1)
                act.activation(g_st[:, 4:8], g_st[:, 0:4], ACT.Ln, scale=1.0 / DV, bias=eps_col)
                act.drain()
                if t:
                    act.wait_ge(sm("on_scaled"), n)
                act.activation(g_st[:, 8:12], g_st[:, 4:8], ACT.Exp, scale=-0.5).then_inc(sm("on_rs"), 1)
                act.wait_ge(sm("gate_mm"), n + 1)
                act.activation(g_e, ps[:, t % 2, :], ACT.Exp, scale=-1.0)
                act.drain()
                act.activation(g_e, g_e, ACT.Ln, bias=1.0)
                act.drain()
                if t >= 2:
                    act.wait_ge(sm("gated"), n - 1)
                act.activation(g_sl[t % 2], g_e, ACT.Exp, scale=-1.0).then_inc(sm("gate_sig"), 1)
            phase_end(act)

        def gate_dve(v, l):
            v.wait_ge(sm("on_in"), 16 * (l + 1))
            for t in range(NT):
                n = NT * l + t
                o4 = ob[:, t, :].rearrange("p (h n) -> p h n", n=DV)
                v.wait_ge(sm("on_sq"), n + 1)
                v.tensor_reduce(g_st[:, 0:4], g_sq.rearrange("p (h n) -> p h n", n=DV), AX.X, ALU.add).then_inc(sm("on_ss"), 1)
                v.wait_ge(sm("on_rs"), n + 1)
                v.tensor_tensor(o4, o4, g_st[:, 8:12].unsqueeze(2).to_broadcast([P, 4, DV]), ALU.mult).then_inc(sm("on_scaled"), 1)
                v.drain()
                v.tensor_tensor(o4, o4, g_on.unsqueeze(1).to_broadcast([P, 4, DV]), ALU.mult)
                v.drain()
                v.wait_ge(sm("gate_sig"), n + 1)
                v.tensor_tensor(ob[:, t, :], ps[:, t % 2, :], ob[:, t, :], ALU.mult).then_inc(sm("gate_free"), 1)
                v.drain()
                if t >= 2:
                    v.wait_ge(sm(f"ym_stored{t % 2}"), ym_count(l, t - 2))
                v.tensor_tensor(g_y[t % 2], g_sl[t % 2], ob[:, t, :], ALU.mult).then_inc(sm("gated"), 1)
            if l == 0:
                v.wait_ge(sm("vecT_ps"), 2)
                v.tensor_copy(vecsT[:, 0:32], ps[:, 2, 0:32])
                v.drain()
                columns_dve(v, "gateB0", 0, 3, 3)
            phase_end(v)

        def ym_count(l, t):
            per = [(NT + 1) // 2, NT // 2][t % 2]
            return 16 * (per * l + t // 2 + 1)

        def gate_sp(sp, l, n):
            phase_seen(sp, n)
            sp.dma_start(g_on, (gla_onorm, delta_onorm)[l][0].partition_broadcast(P)).then_inc(sm("on_in"), 16)
            if l == 0:
                bias_sp(sp, 1)
            for t in range(NF):
                fin_load(sp, l, t)
            for t in range(NT):
                if 2 <= t < 2 + NF:
                    u = t - 2
                    sp.wait_ge(sm(f"ym_stored{u % 2}"), ym_count(l, u))
                    sp.dma_start(f_y[u], yB_dram[u * P:(u + 1) * P, :]).then_inc(sm(f"f_loaded{u}"), 16)
                sp.wait_ge(sm("gated"), NT * l + t + 1)
                sp.dma_start(yB_dram[t * P:(t + 1) * P, :], g_y[t % 2]).then_inc(sm(f"ym_stored{t % 2}"), 16)
            sp.wait_ge(sm("ym_stored0"), ym_count(l, NT - 1))
            sp.wait_ge(sm("ym_stored1"), ym_count(l, NT - 2))
            sp.sem_inc(sm("phase_sp"), 1)

        fr = Region()
        f_y = [fr.take(QW) for _ in range(NF)]
        f_o = [fr.take(D) for _ in range(2)]
        assert fr.at <= MOD_AT["fin0"]
        f_z = Region(OUT_AT - D).take(D)
        assert MOD_AT["fin0"] + KD * 1024 + D <= OUT_AT - D
        fr2 = Region(FIN_AT)
        f_x = [fr2.take(D) for _ in range(NF)]
        f_yT = [fr2.take(QW) for _ in range(NF)]
        assert fr2.at <= GATE_AT
        f_yh = [take_rounded(fr2, f"f_yh{i}", D) for i in range(2)]
        f_yl = [take_rounded(fr2, f"f_yl{i}", D) for i in range(2)]
        f_st = fr2.take(8)
        f_junk = hT[:, :, :].rearrange("p k t -> p (k t)")[:, KD * 1024:KD * 1024 + D]
        w_out_br = rounded("w_out_br", OUT_AT, KD * 512)[:, :].rearrange("p (k n) -> p k n", n=512)
        w_high = [hT_r[:, j * KD * 512:(j + 1) * KD * 512].rearrange("p (k n) -> p k n", n=512) for j in range(2)]

        def w_raw_low(l):
            i = chunk_no[f"out{l}.0"]
            o = (i % RING) * KD * SLOT
            ring = wring_r[:, o:o + KD * 512].rearrange("p (k n) -> p k n", n=512)
            return (wslot(i, 512), w_out_b), (ring, w_out_br)

        def fin_load(sp, l, t):
            d = sm(f"f_loaded{t % NF}")
            sp.dma_start(f_yT[t % NF][:, 0:QW].rearrange("p (b n) -> p b n", b=4),
                         yA_dram[:, :, t * P:(t + 1) * P].rearrange("b p n -> p b n")).then_inc(d, 16)
            sp.dma_start(f_x[t % NF], x_rows(l, t)).then_inc(d, 16)

        def fin_sp(sp, l, n):
            phase_seen(sp, n)
            for t in range(NT + 2):
                if t < NT:
                    if t >= NF:
                        sp.wait_ge(sm("z_ps"), NT * l + t - NF + 1)
                        sp.wait_ge(sm("res_done"), NT * l + t - NF + 1)
                    if t >= NF:
                        sp.dma_start(f_y[t % NF], yB_dram[t * P:(t + 1) * P, :]).then_inc(sm(f"f_loaded{t % NF}"), 16)
                        fin_load(sp, l, t)
                if t >= 2:
                    u = t - 2
                    sp.wait_ge(sm("res_done"), NT * l + u + 1)
                    sp.dma_start(x_rows(1, u), f_o[u % 2]).then_inc(sm(f"y_stored{u % 2}"), 16)
            for u in (NT - 1, NT - 2):
                sp.wait_ge(sm(f"y_stored{u % 2}"), ym_count(l, u))

        def f_count(l, t):
            return 48 * (NT // NF * l + t // NF + 1)

        def fin_pe(pe, l):
            _, w_low = w_raw_low(l)

            def turn(t):
                pe.wait_ge(sm(f"f_loaded{t % NF}"), f_count(l, t))
                if t >= 2:
                    pe.wait_ge(sm("yT_done"), NT * l + t - 1)
                for k in range(4):
                    mm = pe.transpose(ps[:, t % 2, k * P:(k + 1) * P], f_y[t % NF][:, k * P:(k + 1) * P], ident)
                mm.then_inc(sm("yT_ps"), 1)

            turn(0)
            for t in range(NT):
                if t < NT - 1:
                    turn(t + 1)
                pe.wait_ge(sm("yT_done"), NT * l + t + 1)
                if t >= 3:
                    pe.wait_ge(sm("z_free"), NT * l + t - 2)
                for j in range(2):
                    for k in range(KD):
                        if t == 0:
                            pe.wait_ge(sm("w_split"), 2 * KD * l + KD * j + k + 1)
                        z = ps[:, 2 + 2 * (t % 3) + j, :]
                        yh, yl = (y[t % 2][:, k * P:(k + 1) * P] for y in (f_yh, f_yl))
                        pe.matmul(z, yh, w_high[j][:, k, :], start=(k == 0), stop=False)
                        pe.matmul(z, yh, w_low[j][:, k, :], start=False, stop=False)
                        mm = pe.matmul(z, yl, w_high[j][:, k, :], start=False, stop=(k == KD - 1))
                mm.then_inc(sm("z_ps"), 1)
            pe.drain().then_inc(sm("w_used"), 1)
            if l == 0:
                pe.wait_ge(sm("z_free"), NT - 1)
                columns_pe(pe, "fin0", 4, mod_weights(pe, "fin0"), 2)
            phase_end(pe)

        def fin_act(act, l):
            raw, _ = w_raw_low(l)
            for t in range(NT + 1):
                if l == 0 and t in (2, 5):
                    mod_load(act, "fin0", (t // 5,))
                if t < NT:
                    act.wait_ge(sm(f"f_loaded{t % NF}"), f_count(l, t))
                    if t >= 2:
                        act.wait_ge(sm("z_ps"), NT * l + t - 1)
                    act.activation(f_yh[t % 2][:, 0:QW], f_yT[t % NF], ACT.Copy)
                    act.wait_ge(sm("yT_ps"), NT * l + t + 1)
                    act.activation(f_yh[t % 2][:, QW:D], ps[:, t % 2, :], ACT.Copy).then_inc(sm("yT_high"), 1)
                if t == 0:
                    weights(act, f"out{l}.0")
                    for j in range(2):
                        if j:
                            act.wait_ge(sm("wo_loaded"), 16 * (l + 1))
                        for k in range(KD):
                            act.activation(w_high[j][:, k, :], raw[j][:, k, :], ACT.Copy).then_inc(sm("w_high"), 1)
                if t >= 1:
                    u = t - 1
                    b = 2 + 2 * (u % 3)
                    act.wait_ge(sm("z_ps"), NT * l + u + 1)
                    if u >= 1:
                        act.wait_ge(sm("z_free"), NT * l + u)
                    act.drain()
                    act.activation(f_junk.rearrange("p (a n) -> p a n", a=2), ps[:, b:b + 2, :], ACT.Square, accum_out=f_st[:, 0:1])
                    act.drain()
                    act.activation(f_st[:, 1:2], f_st[:, 0:1], ACT.Ln, scale=1.0 / D, bias=eps_col)
                    act.drain()
                    act.activation(f_st[:, 2:3], f_st[:, 1:2], ACT.Exp, scale=-0.5).then_inc(sm("z_rs"), 1)
            phase_end(act)

        def fin_dve(v, l):
            raw, low = w_raw_low(l)

            def y_low(t):
                v.wait_ge(sm("yT_high"), NT * l + t + 1)
                v.tensor_tensor(f_yl[t % 2][:, 0:QW], f_yT[t % NF], f_yh[t % 2][:, 0:QW].bitcast(F32), ALU.subtract)
                v.tensor_tensor(f_yl[t % 2][:, QW:D], ps[:, t % 2, :], f_yh[t % 2][:, QW:D].bitcast(F32),
                                ALU.subtract).then_inc(sm("yT_done"), 1)

            y_low(0)
            for j in range(2):
                for k in range(KD):
                    v.wait_ge(sm("w_high"), 2 * KD * l + KD * j + k + 1)
                    v.tensor_tensor(low[j][:, k, :], raw[j][:, k, :], w_high[j][:, k, :].bitcast(F32),
                                    ALU.subtract).then_inc(sm("w_split"), 1)
            for t in range(NT):
                cnd = int(t == NS)
                b = 2 + 2 * (t % 3)
                if t + 1 < NT:
                    y_low(t + 1)
                v.wait_ge(sm("z_rs"), NT * l + t + 1)
                v.drain()
                v.scalar_tensor_tensor(f_z.rearrange("p (a n) -> p a n", a=2), ps[:, b:b + 2, :], f_st[:, 2:3],
                                       gg[:, cnd, :].rearrange("p (a n) -> p a n", a=2), ALU.mult, ALU.mult).then_inc(sm("z_free"), 1)
                v.drain()
                if t >= 2:
                    v.wait_ge(sm(f"y_stored{t % 2}"), ym_count(l, t - 2))
                v.tensor_tensor(f_o[t % 2], f_z, f_x[t % NF], ALU.add).then_inc(sm("res_done"), 1)
            if l == 0:
                columns_dve(v, "fin0", 1, 2, 4)
            phase_end(v)

        GN = 512
        lr = Region()
        ob = lr.take(NT * QW).rearrange("p (t n) -> p t n", n=QW)
        l_v = lr.take(NT * QW).rearrange("p (t n) -> p t n", n=QW)
        l_qb = lr.take(NT * 256).rearrange("p (t n) -> p t n", n=256)
        l_kb = lr.take(NT * 256).rearrange("p (t n) -> p t n", n=256)
        l_dec = lr.take(NT * 8).rearrange("p (t n) -> p t n", n=8)
        l_up = lr.take(GN)
        l_rT = lr.take(P)
        l_abs = lr.take(GN)
        l_g = lr.take(GN)
        l_ex = [lr.take(GN) for _ in range(3)]
        l_q = lr.take(GN)
        l_k = lr.take(GN)
        l_kf = [lr.take(256) for _ in range(2)]
        l_qz = lr.take(2 * GN).rearrange("p (i r e n) -> p i r e n", i=2, r=2, e=2)
        l_qT = lr.take(256)
        l_kT = lr.take(GN)
        l_at = [lr.take(GN) for _ in range(2)]
        l_att = lr.take(GN)
        NSTATE = 4
        l_S = [[lr.take(GN).rearrange("p (r n) -> p r n", r=2) for _ in range(NSTATE)] for _ in range(2)]

        def gla_tiles(direction):
            return list(range(NS)) + [NS] if direction == 0 else list(range(NS))[::-1] + [NS]

        def state_view(ap, i):
            return ap[0, 0, i].rearrange("(r two) k v -> two k r v", two=2)

        def diag_blocks(state, e):
            return state[64 * e:64 * e + 64, :, DV * e:DV * e + DV]

        def gla_sp(sp, n):
            phase_seen(sp, n)
            d = sm("gla_in")
            for i in range(2):
                sp.dma_start(l_up[16 * i:16 * i + 16, 256 * i:256 * i + 256], gla_gk_up[0, i]).then_inc(d, 16)
                sp.dma_start(l_up[16 * i:16 * i + 16, 256 * (1 - i):256 * (2 - i)], zeros_dram(16, 256)).then_inc(d, 16)
            sp.dma_start(l_up[32:33, :], gla_gk_bias.rearrange("a i n -> a (i n)")).then_inc(d, 16)
            sp.wait_ge(sm("l_zeros"), 1)
            for i in range(2):
                sv = state_view(state_gla, i)
                for two in range(2):
                    sp.dma_start(diag_blocks(l_S[i][0], two), sv[two]).then_inc(d, 16)
            gla_state_out(sp, 0)

        def gla_state_out(sp, i):
            sp.wait_ge(sm(("l_S", "m_S")[i]), 2 * NT)
            sv = state_view(new_gla_state, i)
            for two in range(2):
                sp.dma_start(sv[two], diag_blocks(l_S[i][2 * NT % NSTATE], two)).then_inc(sm("S_stored"), 16)
            sp.wait_ge(sm("S_stored"), 32 * (i + 1))

        def zeros_dram(a, b):
            o, _ = CONST_AT["sel"]
            return consts[2:2 + a, o:o + b]

        GLA_IN = 16 * 9

        def gla_pe(pe):
            wqk = weights(pe, "bqk")
            pe.wait_ge(sm("l_zeros"), 1)

            def tokens(t):
                return slice(t * P, (t + 1) * P)

            def q_and_k(t):
                for k in range(KD):
                    pe.matmul(ps[:, 1, :], hT[:, k, tokens(t)], wqk[:, k, :], start=(k == 0), stop=(k == KD - 1))

            def rank_and_qk(t):
                if t:
                    pe.wait_ge(sm("l_ex"), 2 * t)
                for k in range(KD):
                    mm = pe.matmul(ps[0:32, 0, 0:P], wv[:, k, 512:544], hT[:, k, tokens(t)], start=(k == 0), stop=(k == KD - 1))
                mm.then_inc(sm("l_r_ps"), 1)
                if t:
                    pe.wait_ge(sm("l_kf"), t)
                    q_and_k(t)

            def gates(t):
                pe.wait_ge(sm("l_rT"), t + 1)
                if t >= 2:
                    pe.wait_ge(sm("l_o_out"), t - 1)
                pe.matmul(ps[:, 3, :], l_rT[0:33, :], l_up[0:33, :], start=True, stop=True).then_inc(sm("l_gk_ps"), 1)

            def values(t):
                if t:
                    pe.wait_ge(sm("l_v"), t)
                for k in range(KD):
                    mm = pe.matmul(ps[:, 2, :], hT[:, k, tokens(t)], wv[:, k, 0:512], start=(k == 0), stop=(k == KD - 1))
                mm.then_inc(sm("l_v_ps"), 1)
                if t == NT - 1:
                    pe.drain().then_inc(sm("w_used"), 2)

            def gate_sums(t):
                pe.wait_ge(sm("l_g"), t + 1)
                if t:
                    pe.wait_ge(sm("l_S"), 2 * t)
                for i in range(2):
                    g = l_g[:, 256 * i:256 * i + 256]
                    pe.matmul(ps[:, 4, 256 * i:256 * i + 256], cst("upto", i, P), g, start=True, stop=True)
                    pe.matmul(ps[:, 5, 256 * i:256 * i + 256], cst("beyond", i, P), g, start=True, stop=True)
                for i in range(2):
                    for r in range(2):
                        mm = pe.matmul(ps[:, 0, 4 * i + 2 * r:4 * i + 2 * r + 2], l_g[:, 256 * i + P * r:256 * i + P * r + P],
                                       cst("chunkcol"), start=True, stop=True)
                mm.then_inc(sm("l_B_ps"), 1)

            def turn(t):
                pe.wait_ge(sm("l_qk"), t + 1)
                for j in range(4):
                    pe.transpose(ps[:, 6, j * P:(j + 1) * P], l_q[:, j * P:(j + 1) * P], ident)
                for j in range(4):
                    mm = pe.transpose(ps[:, 7, j * P:(j + 1) * P], l_k[:, j * P:(j + 1) * P], ident)
                mm.then_inc(sm("l_T_ps"), 1)

            def scores(t):
                pe.wait_ge(sm("l_qT"), t + 1)
                pe.wait_ge(sm("l_kT"), t + 1)
                for i in range(2):
                    for r in range(2):
                        mm = pe.matmul(ps[:, 6 + i, 256 * r:256 * r + 256], l_kT[:, (2 * i + r) * P:(2 * i + r + 1) * P],
                                       l_qz[:, i, r], start=True, stop=True)
                mm.then_inc(sm("l_A_ps"), 1)

            def output(t):
                if t == NT - 1:
                    pe.wait_ge(sm("l_o_out"), t)
                pe.wait_ge(sm("l_att"), t + 1)
                for h in range(4):
                    pe.matmul(ps[:, 3, h * P:(h + 1) * P], l_att[:, h * P:(h + 1) * P],
                              l_v[:, t, h * P:(h + 1) * P], start=(h == 0), stop=False, skip_group_check=True)
                for cc in range(2):
                    if cc:
                        pe.wait_ge(sm("l_S"), 2 * t + 1)
                    elif t == NS:
                        pe.wait_ge(sm("S_zero"), 1)
                    gla_inter(pe, cc, l_qT, l_S[0][(2 * t + cc) % NSTATE], 3)
                pe.drain().then_inc(sm("l_o_ps"), 1)

            q_and_k(0)
            wv = weights(pe, "bvr")
            pe.wait_ge(sm("gla_in"), GLA_IN)
            rank_and_qk(0)
            gates(0)
            values(0)
            gate_sums(0)
            turn(0)
            for t in range(NT):
                if t + 1 < NT:
                    rank_and_qk(t + 1)
                scores(t)
                if t + 1 < NT:
                    gates(t + 1)
                pe.wait_ge(sm("l_v"), t + 1)
                pe.wait_ge(sm("l_kf"), t + 1)
                for cc in range(2):
                    for r in range(2):
                        mm = gla_u(pe, t, r, l_kf[cc], 4 + cc)
                    mm.then_inc(sm("l_u_ps"), 1)
                if t + 1 < NT:
                    values(t + 1)
                    gate_sums(t + 1)
                output(t)
                if t + 1 < NT:
                    turn(t + 1)
            pe.wait_ge(sm("l_S"), 2 * NT)

        def gla_u(pe, t, r, k_end, bank):
            return pe.matmul(ps[:, bank, r * 256:(r + 1) * 256], k_end[:, r * P:(r + 1) * P],
                             l_v[:, t, r * 256:(r + 1) * 256], start=True, stop=True)

        def gla_inter(pe, cc, qT_pairs, state, bank, first=False):
            for r in range(2):
                mm = pe.matmul(ps[64 * cc:64 * cc + 64, bank, r * 256:(r + 1) * 256],
                               qT_pairs[:, r * P + 64 * cc:r * P + 64 * cc + 64],
                               state[:, r], start=first and r == 0, stop=True, skip_group_check=True)
            return mm

        def gla_act(act):
            def gates(t):
                act.wait_ge(sm("l_r_ps"), t + 1)
                act.activation(l_rT[0:32, :], ps[0:32, 0, 0:P], ACT.Copy).then_inc(sm("l_rT"), 1)
                act.wait_ge(sm("l_gk_ps"), t + 1)
                act.activation(l_abs, ps[:, 3, :], ACT.Abs)
                act.drain()
                act.activation(l_abs, l_abs, ACT.Exp, scale=-1.0)
                act.drain()
                act.activation(l_abs, l_abs, ACT.Ln, bias=1.0).then_inc(sm("l_ln"), 1)
                act.wait_ge(sm("l_v_ps"), t + 1)
                act.activation(l_v[:, t, :], ps[:, 2, :], ACT.Copy).then_inc(sm("l_v"), 1)
                act.wait_ge(sm("l_B_ps"), t + 1)
                act.activation(l_ex[0], ps[:, 4, :], ACT.Exp, scale=1 / 16.0)
                act.activation(l_ex[1], ps[:, 4, :], ACT.Exp, scale=-1 / 16.0).then_inc(sm("l_ex"), 1)
                act.activation(l_ex[2], ps[:, 5, :], ACT.Exp, scale=1 / 16.0)
                act.activation(l_dec[:, t, :], ps[:, 0, 0:8], ACT.Exp, scale=1 / 16.0).then_inc(sm("l_ex"), 1)

            act.wait_ge(sm("l_zeros"), 1)
            gates(0)
            for t in range(NT):
                act.wait_ge(sm("l_T_ps"), t + 1)
                for e in range(2):
                    half = slice(64 * e, 64 * e + 64)
                    act.activation(l_qz[half, :, :, e, :], ps[half, 6, :].rearrange("p (i r n) -> p i r n", i=2, r=2), ACT.Copy)
                act.activation(l_qT, ps[:, 6, 0:256], ACT.Copy)
                act.activation(l_qb[:, t, :], ps[:, 6, 256:512], ACT.Copy).then_inc(sm("l_qT"), 1)
                if t + 1 < NT:
                    gates(t + 1)
                act.wait_ge(sm("l_o_ps"), t + 1)
                act.activation(ob[:, t, :], ps[:, 3, :], ACT.Copy).then_inc(sm("l_o_out"), 1)

        def state_step(v, i, n, t, cc, bank):
            for r in range(2):
                for e in range(2):
                    half, cols = slice(64 * e, 64 * e + 64), slice(DV * e, DV * e + DV)
                    v.scalar_tensor_tensor(l_S[i][(n + 1) % NSTATE][half, r, cols], l_S[i][n % NSTATE][half, r, cols],
                                           l_dec[half, t, 4 * i + 2 * r + cc:4 * i + 2 * r + cc + 1],
                                           ps[half, bank, 256 * r + DV * e:256 * r + DV * e + DV], ALU.mult, ALU.add)

        def state_zero(v, i):
            for e in range(2):
                v.memset(diag_blocks(l_S[i][2 * NS % NSTATE], e), 0.0)
            v.drain().then_inc(sm("S_zero"), 1)

        def gla_dve(v):
            v.memset(l_rT[32:33, :], 1.0)
            for i in range(2):
                for state in l_S[i]:
                    v.memset(state, 0.0)
            v.memset(l_qz, 0.0)
            for cc in range(2):
                v.memset(l_kf[cc], 0.0)
            v.drain().then_inc(sm("l_zeros"), 1)
            v.wait_ge(sm("gla_in"), GLA_IN)

            def gates(t):
                v.wait_ge(sm("l_ln"), t + 1)
                v.scalar_tensor_tensor(l_g, ps[:, 3, :], 0.0, l_abs, ALU.min, ALU.subtract).then_inc(sm("l_g"), 1)
                v.wait_ge(sm("l_ex"), 2 * t + 1)
                two = lambda ap: ap.rearrange("p (i n) -> p i n", i=2)
                qps = ps[:, 1, 0:256].unsqueeze(1).to_broadcast([P, 2, 256])
                kps = ps[:, 1, 256:512].unsqueeze(1).to_broadcast([P, 2, 256])
                v.scalar_tensor_tensor(two(l_q), qps, 0.125, two(l_ex[0]), ALU.mult, ALU.mult)
                v.tensor_tensor(two(l_k), kps, two(l_ex[1]), ALU.mult).then_inc(sm("l_qk"), 1)
                v.wait_ge(sm("l_ex"), 2 * t + 2)
                for cc in range(2):
                    half = slice(64 * cc, 64 * cc + 64)
                    v.tensor_tensor(l_kf[cc][half], ps[half, 1, 256:512], l_ex[2][half, 0:256], ALU.mult)
                v.tensor_tensor(l_kb[:, t, :], ps[:, 1, 256:512], l_ex[2][:, 256:512], ALU.mult).then_inc(sm("l_kf"), 1)

            gates(0)
            for t in range(NT):
                v.wait_ge(sm("l_T_ps"), t + 1)
                v.tensor_copy(l_kT, ps[:, 7, :]).then_inc(sm("l_kT"), 1)
                v.wait_ge(sm("l_A_ps"), t + 1)
                for i in range(2):
                    v.tensor_tensor(l_at[i].rearrange("p (h n) -> p h n", n=P), ps[:, 6 + i, :].rearrange("p (h n) -> p h n", n=P),
                                    cst("upto", i, P).unsqueeze(1).to_broadcast([P, 4, P]), ALU.mult)
                v.drain()
                v.tensor_tensor(l_att, l_at[0], l_at[1], ALU.add).then_inc(sm("l_att"), 1)
                if t == NS:
                    v.wait_ge(sm("l_o_ps"), t)
                    state_zero(v, 0)
                for cc in range(2):
                    v.wait_ge(sm("l_u_ps"), 2 * t + cc + 1)
                    if cc and t:
                        v.wait_ge(sm("l_o_ps"), t)
                    state_step(v, 0, 2 * t + cc, t, cc, 4 + cc)
                    v.drain().then_inc(sm("l_S"), 1)
                if t + 1 < NT:
                    gates(t + 1)

        def glab_sp(sp):
            gla_state_out(sp, 1)
            sp.sem_inc(sm("phase_sp"), 1)

        m_kz = [l_kf, [l_ex[0][:, 256 * cc:256 * cc + 256] for cc in range(2)]]

        def glab_pe(pe):
            tiles = gla_tiles(1)

            def u(m):
                if m >= 2:
                    pe.wait_ge(sm("m_S"), 2 * (m - 1))
                pe.wait_ge(sm("m_kz"), m + 1)
                for cc in (1, 0):
                    for r in range(2):
                        mm = gla_u(pe, tiles[m], r, m_kz[m % 2][cc], 4 * (m % 2) + cc)
                    mm.then_inc(sm("l_u_ps"), 1)

            u(0)
            for m, t in enumerate(tiles):
                if m + 1 < NT:
                    u(m + 1)
                if m >= 2:
                    pe.wait_ge(sm("m_o_used"), m - 1)
                for n, cc in enumerate((1, 0)):
                    if n:
                        pe.wait_ge(sm("m_S"), 2 * m + 1)
                    elif t == NS:
                        pe.wait_ge(sm("S_zero"), 2)
                    elif m:
                        pe.wait_ge(sm("m_S"), 2 * m)
                    mm = gla_inter(pe, cc, l_qb[:, t, :], l_S[1][(2 * m + n) % NSTATE], 4 * (m % 2) + 2, first=True)
                mm.then_inc(sm("m_o_ps"), 1)
            phase_end(pe)

        def glab_dve(v):
            def add(m, t):
                v.wait_ge(sm("m_o_ps"), m + 1)
                v.tensor_tensor(ob[:, t, :], ps[:, 4 * (m % 2) + 2, :], ob[:, t, :], ALU.add).then_inc(sm("m_o_used"), 1)

            tiles = gla_tiles(1)
            for cc in range(2):
                v.memset(m_kz[1][cc][64 * (1 - cc):64 * (1 - cc) + 64, :], 0.0)
            v.drain().then_inc(sm("l_zeros"), 1)
            v.wait_ge(sm("l_o_out"), NT)
            for m, t in enumerate(tiles):
                if t == NS:
                    v.wait_ge(sm("m_o_ps"), m)
                    state_zero(v, 1)
                for n, cc in enumerate((1, 0)):
                    v.wait_ge(sm("l_u_ps"), 2 * NT + 2 * m + n + 1)
                    if n and m:
                        v.wait_ge(sm("m_o_ps"), m)
                    state_step(v, 1, 2 * m + n, t, cc, 4 * (m % 2) + cc)
                    v.drain().then_inc(sm("m_S"), 1)
                if m:
                    add(m - 1, tiles[m - 1])
            add(NT - 1, tiles[-1])
            phase_end(v)

        def glab_act(act):
            for m, t in enumerate(gla_tiles(1)):
                if m == 1:
                    act.wait_ge(sm("l_zeros"), 2)
                else:
                    act.wait_ge(sm("l_u_ps"), 2 * NT + 2 * max(m - 1, 0))
                for cc in range(2):
                    half = slice(64 * cc, 64 * cc + 64)
                    mm = act.activation(m_kz[m % 2][cc][half, :], l_kb[half, t, :], ACT.Copy)
                mm.then_inc(sm("m_kz"), 1)
            phase_end(act)

        NZ = T + 6
        NC2 = T + 2
        N72 = 2 * NT * 4
        er_ = Region(NT * QW)
        c_z = er_.take(NT * 16)
        c_in = er_.take(32)
        c_rows = er_.take(P)
        c_w = er_.take(60)
        c_sp = er_.take(NT * 8)
        c_t = er_.take(NT * 8)
        c_g, c_gc, c_beta, c_eg, c_er, c_nb = (er_.take(N72) for _ in range(6))
        c_dec = er_.take(2 * N72)
        d_qT, d_kT = er_.take(T), er_.take(T)
        d_k = er_.take(T).rearrange("p (t n) -> p t n", n=P)
        d_v = er_.take(T).rearrange("p (t n) -> p t n", n=P)
        r1 = er_.at
        zp = er_.take(3 * NZ).rearrange("p (b n) -> p b n", b=3)
        zc = er_.take(3 * NC2)
        zcb = zc.rearrange("p (b n) -> p b n", b=3)
        z_sq = er_.take(2 * NC2)
        z_rn = er_.take(2 * NC2)
        z_e = er_.take(NC2)
        er2 = Region(r1)
        d_Z, d_A, d_W, d_Q, d_K, d_V = (er2.take(2 * T).rearrange("p (i t n) -> p i t n", i=2, n=P) for _ in range(6))
        r3 = er2.at
        d_D, d_Y, d_T, d_X = ([er2.take(3 * P) for _ in range(2)] for _ in range(4))
        er3 = Region(r3)
        d_S = [[er3.take(P) for _ in range(3)] for _ in range(2)]
        d_vn = [[er3.take(P) for _ in range(2)] for _ in range(2)]

        def col(ap, i, t, h):
            n = (i * NT + t) * 4 + h
            return ap[:, n:n + 1]

        def ab_sp(sp):
            d = sm("gate_in")
            sp.dma_start(c_in[:, 0:8], dt_bias_d[0].rearrange("i h -> (i h)").partition_broadcast(P)).then_inc(d, 16)
            sp.dma_start(c_in[:, 8:16], a_log_d[0].rearrange("i h -> (i h)").partition_broadcast(P)).then_inc(d, 16)
            sp.dma_start(c_rows[0:60, :], conv_d[0].rearrange("k (b p) -> (k b) p", p=P)).then_inc(d, 16)

        def ab_pe(pe):
            pe.wait_ge(sm("gate_in"), 112)
            pe.transpose(ps[:, 3, 0:60], c_rows[0:60, :], ident[0:60, 0:60]).then_inc(sm("ab_ps"), 1)

        def ab_sums_pe(pe):
            pe.wait_ge(sm("c_g"), 1)
            for i in range(2):
                g = c_g[:, 36 * i:36 * i + 36]
                pe.matmul(ps[:, 4, 36 * i:36 * i + 36], cst("upto", i, P), g, start=True, stop=True)
                pe.matmul(ps[:, 5, 36 * i:36 * i + 36], cst("beyond", i, P), g, start=True, stop=True)
            for cc in range(2):
                mm = pe.matmul(ps[:, 6, N72 * cc:N72 * cc + N72], cst("inchunk", cc, P), c_g, start=True, stop=True)
            mm.then_inc(sm("c_ps"), 1)

        def ab_act(act):
            act.wait_ge(sm("ab_ps"), 1)
            act.activation(c_w, ps[:, 3, 0:60], ACT.Copy)
            act.activation(c_in[:, 16:24], c_in[:, 8:16], ACT.Exp)
            act.wait_ge(sm("c_a"), 1)
            act.activation(c_z.rearrange("p (t n) -> p t n", n=16)[:, :, 8:16], abz.rearrange("p (t n) -> p t n", n=16)[:, :, 8:16],
                           ACT.Exp, scale=-1.0)
            act.activation(c_t, c_sp, ACT.Abs)
            act.drain()
            act.activation(c_t, c_t, ACT.Exp, scale=-1.0)
            act.drain()
            act.activation(c_t, c_t, ACT.Ln, bias=1.0).then_inc(sm("c_ln"), 1)

        def ab_sums_act(act):
            act.wait_ge(sm("c_ps"), 1)
            act.activation(c_gc, ps[:, 4, 0:N72], ACT.Copy)
            act.activation(c_eg, ps[:, 4, 0:N72], ACT.Exp)
            act.activation(c_er, ps[:, 5, 0:N72], ACT.Exp)
            act.activation(c_dec, ps[:, 6, 0:2 * N72], ACT.Exp).then_inc(sm("c_ex"), 1)

        def ab_dve(v):
            v.wait_ge(sm("gate_in"), 112)
            v.wait_ge(sm("ab_ps"), 1)
            tih = lambda ap, n: ap.rearrange("p (t n) -> p t n", n=n)
            v.tensor_tensor(tih(c_sp, 8), tih(abz, 16)[:, :, 0:8], c_in[:, 0:8].unsqueeze(1).to_broadcast([P, NT, 8]), ALU.add)
            v.drain().then_inc(sm("c_a"), 1)
            v.wait_ge(sm("c_ln"), 1)
            v.scalar_tensor_tensor(c_sp, c_sp, 0.0, c_t, ALU.max, ALU.add)
            v.drain()
            v.scalar_tensor_tensor(tih(c_sp, 8), tih(c_sp, 8), -1.0, c_in[:, 16:24].unsqueeze(1).to_broadcast([P, NT, 8]), ALU.mult, ALU.mult)
            z8 = c_z.rearrange("p (t n) -> p t n", n=16)[:, :, 8:16]
            v.tensor_scalar(z8, z8, 1.0, None, ALU.add)
            v.drain()
            for i in range(2):
                v.tensor_copy(c_g[:, 36 * i:36 * i + 36].rearrange("p (t h) -> p t h", h=4), tih(c_sp, 8)[:, :, 4 * i:4 * i + 4])
            v.drain().then_inc(sm("c_g"), 1)
            for i in range(2):
                v.reciprocal(c_beta[:, 36 * i:36 * i + 36].rearrange("p (t h) -> p t h", h=4), z8[:, :, 4 * i:4 * i + 4])

        def ab_sums_dve(v):
            v.drain()
            v.wait_ge(sm("c_ex"), 1)
            v.scalar_tensor_tensor(c_nb, c_beta, -1.0, c_eg, ALU.mult, ALU.mult)

        TOK = [(0, 512, 2), (512, 512, 514), (T_S, T_P, T_S + 4)]
        NORM = [(a, min(512, NC2 - a)) for a in range(0, NC2, 512)]
        PROJ_BANK = (0, 1, 2, 3, 4, 5, 0, 1, 2)
        SS_BANKS = ((3, 4, 5), (6, 7, 0))
        TURN_BANKS = ((6, 7, 5), (3, 4, 2))
        TURNS = [(0, 4), (4, 8), (8, 9)]

        def zblock(ap, b):
            return ap[:, b * NC2:(b + 1) * NC2]

        def pre_pe(pe, h):
            w = weights(pe, f"dh{h}")
            for n in range(9):
                b, (o, m, _) = n // 3, TOK[n % 3]
                if n >= 6:
                    pe.wait_ge(sm("zp"), 9 * h + n - 5)
                for k in range(KD):
                    mm = pe.matmul(ps[:, PROJ_BANK[n], 0:m], w[:, k, b * P:(b + 1) * P], hT[:, k, o:o + m], start=(k == 0), stop=(k == KD - 1))
                mm.then_inc(sm("zp_ps"), 1)
            pe.drain().then_inc(sm("w_used"), 1)
            for b in range(2):
                pe.wait_ge(sm("zp"), 9 * h + (6, 7)[b])
                pe.wait_ge(sm("z_sq"), 2 * h + b + 1)
                for n, (o, m) in enumerate(NORM):
                    mm = pe.matmul(ps[:, SS_BANKS[b][n], 0:m], ones, zblock(z_sq, b)[:, o:o + m], start=True, stop=True)
                mm.then_inc(sm("z_ss"), 1)
            for b in range(2):
                if b == 0:
                    pe.wait_ge(sm("d_qkT"), h + 1)
                else:
                    pe.wait_ge(sm("z_silu"), 3 * h + 3)
                    pe.wait_ge(sm("zp"), 9 * h + 9)
                for n, (t0, t1) in enumerate(TURNS):
                    for t in range(t0, t1):
                        vo = t * P + (2 if t == NS else 0)
                        src = d_kT[:, t * P:(t + 1) * P] if b == 0 else zcb[:, 2, vo:vo + P]
                        mm = pe.transpose(ps[:, TURN_BANKS[b][n], (t - t0) * P:(t - t0 + 1) * P], src, ident)
                    mm.then_inc(sm("d_kv_ps"), 1)
            phase_end(pe)

        def pre_act(act, h):
            def project(n):
                b, (_, m, o) = n // 3, TOK[n % 3]
                act.wait_ge(sm("zp_ps"), 9 * h + n + 1)
                act.activation(zp[:, b, o:o + m], ps[:, PROJ_BANK[n], 0:m], ACT.Copy).then_inc(sm("zp"), 1)

            def logistic(b):
                act.wait_ge(sm("zc"), 3 * h + b + 1)
                if b:
                    act.wait_ge(sm("z_silu"), 3 * h + b)
                act.activation(z_e, zblock(zc, b), ACT.Exp, scale=-1.0)
                act.drain()
                act.activation(z_e, z_e, ACT.Ln, bias=1.0)
                act.drain()
                act.activation(z_e, z_e, ACT.Exp, scale=-1.0).then_inc(sm("z_sig"), 1)

            def square(b):
                act.wait_ge(sm("z_silu"), 3 * h + b + 1)
                act.activation(zblock(z_sq, b), zblock(zc, b), ACT.Square).then_inc(sm("z_sq"), 1)

            def rnorm(b):
                act.wait_ge(sm("z_ss"), 2 * h + b + 1)
                for n, (o, m) in enumerate(NORM):
                    act.activation(zblock(z_rn, b)[:, o:o + m], ps[:, SS_BANKS[b][n], 0:m], ACT.Ln, bias=eps_col)
                act.drain()
                act.activation(zblock(z_rn, b), zblock(z_rn, b), ACT.Exp, scale=-0.5).then_inc(sm("z_rn"), 1)

            for n in range(4):
                project(n)
            logistic(0)
            project(4)
            square(0)
            for n in (5, 6):
                project(n)
            logistic(1)
            project(7)
            square(1)
            project(8)
            rnorm(0)
            rnorm(1)
            logistic(2)
            for n, (t0, t1) in enumerate(TURNS):
                act.wait_ge(sm("d_kv_ps"), 6 * h + n + 1)
                act.activation(d_k[:, t0:t1, :], ps[:, TURN_BANKS[0][n], 0:(t1 - t0) * P].rearrange("p (t n) -> p t n", n=P), ACT.Copy)
            phase_end(act)

        def pre_dve(v, h):
            if h == 0:
                v.memset(ob.rearrange("p t n -> p (t n)"), 0.0)
            for a in (0, 2 + T_S, 4 + T):
                v.memset(zp[:, :, a:a + 2], 0.0)
            v.drain()

            def convolve(b):
                v.wait_ge(sm("zp"), 9 * h + 3 * b + 3)
                for k in range(5):
                    tap = c_w[:, 12 * k + 4 * b + h:12 * k + 4 * b + h + 1]
                    if k == 0:
                        mm = v.tensor_scalar(zcb[:, b, :], zp[:, b, k:k + NC2], tap, None, ALU.mult)
                    else:
                        v.drain()
                        mm = v.scalar_tensor_tensor(zcb[:, b, :], zp[:, b, k:k + NC2], tap, zcb[:, b, :], ALU.mult, ALU.add)
                mm.then_inc(sm("zc"), 1)

            def silu(b):
                v.wait_ge(sm("z_sig"), 3 * h + b + 1)
                v.tensor_tensor(zblock(zc, b), zblock(zc, b), z_e, ALU.mult).then_inc(sm("z_silu"), 1)

            for b in range(2):
                convolve(b)
                silu(b)
            convolve(2)
            for dst, b, s in ((d_qT, 0, P ** -0.5), (d_kT, 1, 1.0)):
                v.wait_ge(sm("z_rn"), 2 * h + b + 1)
                for o, n, x in ((0, T_S, 0), (T_S, T_P, 2)):
                    a = b * NC2 + o + x
                    mm = v.scalar_tensor_tensor(dst[:, o:o + n], z_rn[:, a:a + n], s, zc[:, a:a + n], ALU.mult, ALU.mult)
            mm.then_inc(sm("d_qkT"), 1)
            silu(2)
            for n, (t0, t1) in enumerate(TURNS):
                v.wait_ge(sm("d_kv_ps"), 6 * h + 3 + n + 1)
                v.tensor_copy(d_v[:, t0:t1, :], ps[:, TURN_BANKS[1][n], 0:(t1 - t0) * P].rearrange("p (t n) -> p t n", n=P))
            phase_end(v)

        GROUPS = [(i, 3 * a) for a in range(3) for i in range(2)]
        ROWS, KK, KQ, Z1 = range(4)
        LY, LZ, LX, LW = 1, 0, 2, 3

        def sbank(n, b):
            return 4 * (n % 2) + b

        def tiles3(ap):
            return ap.rearrange("p (a n) -> p a n", n=P)

        def sys_steps():
            for n in range(0, len(GROUPS), 2):
                for m in (n, n + 1):
                    yield "start", m, 0
                for m in (n, n + 1):
                    yield "first", m, 0
                for k in range(1, NLEV):
                    for m in (n, n + 1):
                        yield "y", m, k
                    for m in (n, n + 1):
                        yield "zx", m, k
                for m in (n, n + 1):
                    yield "w", m, 0

        def sys_pe(pe, h):
            for what, n, k in sys_steps():
                i, t0 = GROUPS[n]
                N = 6 * h + n
                p = n % 2
                cols = [slice(a * P, (a + 1) * P) for a in range(3)]
                if what == "start":
                    if n >= 2:
                        pe.wait_ge(sm("s_Z"), N - 1)
                    for a in range(3):
                        t = t0 + a
                        ks = d_kT[:, t * P:(t + 1) * P]
                        pe.matmul(ps[:, sbank(n, ROWS), cols[a]], col(c_g, i, t, h).to_broadcast([P, P]), cst("upto", i, P), start=True, stop=True)
                        pe.matmul(ps[:, sbank(n, KK), cols[a]], ks, ks, start=True, stop=True)
                        mm = pe.matmul(ps[:, sbank(n, KQ), cols[a]], ks, d_qT[:, t * P:(t + 1) * P], start=True, stop=True)
                    mm.then_inc(sm("s_G_ps"), 1)
                elif what == "first":
                    pe.wait_ge(sm("s_X1"), N + 1)
                    if n >= 2:
                        pe.wait_ge(sm("s_W"), N - 1)
                    for a in range(3):
                        mm = pe.transpose(ps[:, sbank(n, Z1), cols[a]], d_X[p][:, cols[a]], ident)
                    mm.then_inc(sm("s_Z1_ps"), 1)
                elif what == "y":
                    pe.wait_ge(sm(f"s_ZX{p}"), 5 * (N // 2) + k)
                    for a in range(3):
                        mm = pe.matmul(ps[:, sbank(n, LY), cols[a]], d_T[p][:, cols[a]], d_Z[:, i, t0 + a, :], start=True, stop=True)
                    mm.then_inc(sm(f"s_Y_ps{p}"), 1)
                elif what == "zx":
                    pe.wait_ge(sm(f"s_Y{p}"), 5 * (N // 2) + k)
                    if k == 1:
                        pe.wait_ge(sm("s_Q"), N + 1)
                    for a in range(3):
                        mm = pe.matmul(ps[:, sbank(n, LZ), cols[a]], d_X[p][:, cols[a]], d_Y[p][:, cols[a]], start=True, stop=True)
                        if k < NLEV - 1:
                            mm = pe.matmul(ps[:, sbank(n, LX), cols[a]], d_Y[p][:, cols[a]], d_X[p][:, cols[a]], start=True, stop=True)
                    mm.then_inc(sm(f"s_ZY_ps{p}"), 1)
                else:
                    pe.wait_ge(sm("s_Z"), N + 1)
                    pe.wait_ge(sm("s_kb"), N + 1)
                    for a in range(3):
                        mm = pe.matmul(ps[:, sbank(n, LW), cols[a]], d_D[p][:, cols[a]], d_Z[:, i, t0 + a, :], start=True, stop=True)
                    mm.then_inc(sm("s_W_ps"), 1)
            phase_end(pe)

        def sys_act(act, h):
            for what, n, k in sys_steps():
                i, t0 = GROUPS[n]
                N = 6 * h + n
                p = n % 2
                if what == "start":
                    act.wait_ge(sm("s_D"), 2 * N + 1)
                    act.activation(d_D[p], d_D[p], ACT.Exp, scale=-1.0).then_inc(sm("s_ex"), 1)
                    act.wait_ge(sm("s_D"), 2 * N + 2)
                    act.activation(d_Y[p], d_Y[p], ACT.Exp)
                    act.activation(ps[:, sbank(n, ROWS), 0:384], ps[:, sbank(n, ROWS), 0:384], ACT.Exp).then_inc(sm("s_ex"), 1)
                    for a in range(3):
                        t = t0 + a
                        act.activation(d_V[:, i, t, :], d_v[:, t, :], ACT.Copy, scale=col(c_beta, i, t, h))
                        act.activation(d_K[:, i, t, :], d_k[:, t, :], ACT.Copy, scale=col(c_er, i, t, h))
                elif what == "first":
                    act.wait_ge(sm("s_X1"), N + 1)
                    for a in range(3):
                        mm = act.activation(d_D[p][:, a * P:(a + 1) * P], d_k[:, t0 + a, :], ACT.Copy, scale=col(c_nb, i, t0 + a, h))
                    mm.then_inc(sm("s_kb"), 1)
                elif what == "w":
                    act.wait_ge(sm("s_W_ps"), N + 1)
                    act.activation(d_W[:, i, t0:t0 + 3, :], tiles3(ps[:, sbank(n, LW), 0:384]), ACT.Copy).then_inc(sm("s_W"), 1)
            phase_end(act)

        def sys_dve(v, h):
            for what, n, k in sys_steps():
                i, t0 = GROUPS[n]
                N = 6 * h + n
                p = n % 2
                Z = d_Z[:, i, t0:t0 + 3, :]
                if what == "start":
                    v.wait_ge(sm("s_G_ps"), N + 1)
                    if n >= 2:
                        v.wait_ge(sm("s_W_ps"), N - 1)
                    for a in range(3):
                        t, s = t0 + a, slice(a * P, (a + 1) * P)
                        row = ps[:, sbank(n, ROWS), s]
                        mm = v.scalar_tensor_tensor(d_D[p][:, s], row, col(c_gc, i, t, h), cst("strict", i, P), ALU.subtract, ALU.max)
                    mm.then_inc(sm("s_D"), 1)
                    for a in range(3):
                        t, s = t0 + a, slice(a * P, (a + 1) * P)
                        row = ps[:, sbank(n, ROWS), s]
                        mm = v.scalar_tensor_tensor(d_Y[p][:, s], row, col(c_gc, i, t, h), cst("incl", i, P), ALU.subtract, ALU.min)
                    mm.then_inc(sm("s_D"), 1)
                elif what == "first":
                    v.wait_ge(sm("s_ex"), 2 * N + 1)
                    for a in range(3):
                        t, s = t0 + a, slice(a * P, (a + 1) * P)
                        v.scalar_tensor_tensor(d_T[p][:, s], ps[:, sbank(n, KK), s], col(c_beta, i, t, h), d_D[p][:, s], ALU.mult, ALU.mult)
                    v.drain()
                    lv = cst("level0", 1 - i, P).unsqueeze(1).to_broadcast([P, 3, P])
                    v.scalar_tensor_tensor(tiles3(d_X[p]), tiles3(d_T[p]), -1.0, lv, ALU.mult, ALU.mult)
                    v.drain()
                    v.tensor_tensor(tiles3(d_X[p]), tiles3(d_X[p]), ident.unsqueeze(1).to_broadcast([P, 3, P]), ALU.add).then_inc(sm("s_X1"), 1)
                    v.wait_ge(sm("s_ex"), 2 * N + 2)
                    v.tensor_tensor(d_A[:, i, t0:t0 + 3, :], tiles3(ps[:, sbank(n, KQ), 0:384]), tiles3(d_Y[p]), ALU.mult)
                    v.wait_ge(sm("s_Z1_ps"), N + 1)
                    v.tensor_copy(Z, tiles3(ps[:, sbank(n, Z1), 0:384])).then_inc(sm(f"s_ZX{p}"), 1)
                    v.tensor_tensor(d_Q[:, i, t0:t0 + 3, :], tiles3(d_qT[:, t0 * P:t0 * P + 384]), tiles3(ps[:, sbank(n, ROWS), 0:384]), ALU.mult).then_inc(sm("s_Q"), 1)
                elif what == "y":
                    v.wait_ge(sm(f"s_Y_ps{p}"), 5 * (N // 2) + k)
                    lv = cst(f"level{k}", i, P).unsqueeze(1).to_broadcast([P, 3, P])
                    v.tensor_tensor(tiles3(d_Y[p]), tiles3(ps[:, sbank(n, LY), 0:384]), lv, ALU.mult).then_inc(sm(f"s_Y{p}"), 1)
                elif what == "zx":
                    v.wait_ge(sm(f"s_ZY_ps{p}"), 5 * (N // 2) + k)
                    z = v.scalar_tensor_tensor(Z, tiles3(ps[:, sbank(n, LZ), 0:384]), -1.0, Z, ALU.mult, ALU.add)
                    if k < NLEV - 1:
                        z.then_inc(sm(f"s_ZX{p}"), 1)
                        v.scalar_tensor_tensor(d_X[p], ps[:, sbank(n, LX), 0:384], -1.0, d_X[p], ALU.mult, ALU.add)
                    else:
                        z.then_inc(sm("s_Z"), 1)
            phase_end(v)

        STEPS = [(s, False) for s in range(2 * NS)] + [(s, True) for s in range(2)]

        def step_of(i, n):
            s, prompt = STEPS[n]
            if prompt:
                cc = s if i == 0 else 1 - s
                return NS, cc, (2, 1)[s], (1, 0)[s]
            g = s if i == 0 else 2 * NS - 1 - s
            return g // 2, g % 2, n % 2, (n + 1) % 2

        NST = len(STEPS)

        def scan_sp(sp, h, n):
            phase_seen(sp, n)
            for i in range(2):
                sp.dma_start(d_S[i][0], state_delta[0, 0, i, h]).then_inc(sm("d_S_in"), 16)
            for i in range(2):
                sp.wait_ge(sm(f"d_S{i}"), NST * (h + 1))
                sp.dma_start(new_delta_state[0, 0, i, h], d_S[i][0]).then_inc(sm("d_S_stored"), 16)
            sp.wait_ge(sm("d_S_stored"), 32 * (h + 1))
            sp.sem_inc(sm("phase_sp"), 1)

        def scan_pe(pe, h):
            pe.wait_ge(sm("d_S_in"), 32 * (h + 1))
            pe.wait_ge(sm("d_S_zero"), h + 1)
            for n in range(NST):
                N = NST * h + n
                for i in range(2):
                    t, cc, a, _ = step_of(i, n)
                    rows = slice(64 * cc, 64 * cc + 64)
                    pe.matmul(ps[rows, 3 * i, 0:P], d_Z[:, i, t, rows], d_V[:, i, t, :], start=True, stop=False)
                    if n:
                        pe.wait_ge(sm(f"d_S{i}"), N)
                    pe.matmul(ps[rows, 3 * i, 0:P], d_W[:, i, t, rows], d_S[i][a], start=False, stop=True).then_inc(sm(f"d_vn_ps{i}"), 1)
                    if n:
                        pe.wait_ge(sm(f"d_o{i}"), N)
                    pe.matmul(ps[rows, 3 * i + 1, 0:P], d_Q[:, i, t, rows], d_S[i][a], start=True, stop=False)
                for i in range(2):
                    t, cc, a, _ = step_of(i, n)
                    rows = slice(64 * cc, 64 * cc + 64)
                    pe.wait_ge(sm(f"d_vn{i}"), N + 1)
                    pe.matmul(ps[:, 3 * i + 2, 0:P], d_K[:, i, t, :], d_vn[i][cc], start=True, stop=True).then_inc(sm(f"d_kS_ps{i}"), 1)
                    pe.matmul(ps[rows, 3 * i + 1, 0:P], d_A[:, i, t, rows], d_vn[i][cc], start=False, stop=True).then_inc(sm(f"d_o_ps{i}"), 1)
            phase_end(pe)

        def scan_act(act, h):
            for n in range(NST):
                for i in range(2):
                    t, cc, a, _ = step_of(i, n)
                    rows = slice(64 * cc, 64 * cc + 64)
                    act.wait_ge(sm(f"d_vn_ps{i}"), NST * h + n + 1)
                    if n:
                        act.wait_ge(sm(f"d_o_ps{i}"), NST * h + n)
                    act.activation(d_vn[i][cc][rows, :], ps[rows, 3 * i, 0:P], ACT.Copy).then_inc(sm(f"d_vn{i}"), 1)
            phase_end(act)

        def scan_dve(v, h):
            for i in range(2):
                v.memset(d_S[i][2], 0.0)
                for cc in range(2):
                    v.memset(d_vn[i][cc][64 * (1 - cc):64 * (1 - cc) + 64, :], 0.0)
            v.drain().then_inc(sm("d_S_zero"), 1)
            v.wait_ge(sm("d_S_in"), 32 * (h + 1))
            for n in range(NST):
                N = NST * h + n
                for i in range(2):
                    t, cc, a, b = step_of(i, n)
                    m = cc * N72 + (i * NT + t) * 4 + h
                    v.wait_ge(sm(f"d_kS_ps{i}"), N + 1)
                    v.scalar_tensor_tensor(d_S[i][b], d_S[i][a], c_dec[:, m:m + 1], ps[:, 3 * i + 2, 0:P], ALU.mult, ALU.add).then_inc(sm(f"d_S{i}"), 1)
                for i in range(2):
                    t, cc, a, b = step_of(i, n)
                    rows = slice(64 * cc, 64 * cc + 64)
                    v.wait_ge(sm(f"d_o_ps{i}"), N + 1)
                    o = ob[rows, t, h * P:(h + 1) * P]
                    v.tensor_tensor(o, ps[rows, 3 * i + 1, 0:P], o, ALU.add).then_inc(sm(f"d_o{i}"), 1)
            phase_end(v)

        eps_col = cst("eps")
        STAGES = ["mod0", "ada0", "qkv0", "att0", "gateA0", "gla", "gateB0", "fin0",
                  "ada1", "qkv1", "att1", "gateA1"]
        STAGES += [f"{s}{h}" for h in range(4) for s in ("dpre", "dsys", "dscan")]
        STAGES += ["gateB1", "fin1"]
        no = STAGES.index
        STORING = [s for s in STAGES if s.startswith(("qkv", "gate", "gla", "dscan"))]

        def stores_done(eng, stage):
            eng.wait_ge(sm("phase_sp"), STORING.index(stage) + 1)

        block = ctx.enter_context(nc.Block())

        @block.gpsimd
        def _(pool):
            for i, (name, parts, n) in enumerate(chunks):
                if i >= RING:
                    pool.wait_ge(sm("w_used"), i - RING + 1)
                o = 0
                for src in parts:
                    m = src.shape[2]
                    pool.dma_start(wslot(i, n)[:, :, o:o + m], src).then_inc(sm(f"w_loaded{i % RING}"), 16)
                    o += m

        @block.sync
        def _(sp):
            sp.dma_start(con[:, 0:FIRST], consts[:, 0:FIRST]).then_inc(sm("const_in"), 16)
            sp.dma_start(sinks[:, 0:8], sink_c[0].partition_broadcast(P)).then_inc(sm("const_in"), 16)
            for l in range(2):
                if l == 0:
                    mod_sp(sp)
                ada_sp(sp, l, no("ada1") if l else 0)
                qkv_sp(sp, l, no(f"qkv{l}"))
                gateA_sp(sp, l, no(f"gateA{l}"))
                if l == 0:
                    gla_sp(sp, no("gla"))
                    glab_sp(sp)
                else:
                    for h in range(4):
                        scan_sp(sp, h, no(f"dscan{h}"))
                gate_sp(sp, l, no(f"gateB{l}"))
                fin_sp(sp, l, no(f"fin{l}"))

        @block.tensor
        def _(pe):
            pe.wait_ge(sm("const_in"), 32)
            for l in range(2):
                if l == 0:
                    mod_pe(pe)
                ada_pe(pe, l)
                pe.wait_ge(sm("rest_in"), 16)
                qkv_pe(pe, l)
                att_pe(pe, l)
                stores_done(pe, f"qkv{l}")
                gateA_pe(pe, l)
                stores_done(pe, f"gateA{l}")
                if l == 0:
                    gla_pe(pe)
                    glab_pe(pe)
                    stores_done(pe, "gla")
                else:
                    for h in range(4):
                        pre_pe(pe, h)
                        sys_pe(pe, h)
                        scan_pe(pe, h)
                        stores_done(pe, f"dscan{h}")
                gate_pe(pe, l)
                fin_pe(pe, l)

        @block.scalar
        def _(act):
            act.wait_ge(sm("const_in"), 32)
            for l in range(2):
                if l == 0:
                    mod_act(act)
                act.preload_act_table_set(EXP_LN)
                ada_act(act, l)
                act.wait_ge(sm("rest_in"), 16)
                qkv_act(act, l)
                att_act(act, l)
                stores_done(act, f"qkv{l}")
                gateA_act(act, l)
                stores_done(act, f"gateA{l}")
                act.preload_act_table_set(EXP_LN)
                if l == 0:
                    gla_act(act)
                    glab_act(act)
                    stores_done(act, "gla")
                else:
                    for h in range(4):
                        pre_act(act, h)
                        sys_act(act, h)
                        scan_act(act, h)
                        stores_done(act, f"dscan{h}")
                gate_act(act, l)
                fin_act(act, l)

        @block.vector
        def _(v):
            v.wait_ge(sm("const_in"), 32)
            for l in range(2):
                if l == 0:
                    mod_dve(v)
                ada_dve(v, l)
                v.wait_ge(sm("rest_in"), 16)
                qkv_dve(v, l)
                att_dve(v, l)
                stores_done(v, f"qkv{l}")
                gateA_dve(v, l)
                stores_done(v, f"gateA{l}")
                if l == 0:
                    gla_dve(v)
                    glab_dve(v)
                    stores_done(v, "gla")
                else:
                    for h in range(4):
                        pre_dve(v, h)
                        sys_dve(v, h)
                        scan_dve(v, h)
                        stores_done(v, f"dscan{h}")
                gate_dve(v, l)
                stores_done(v, f"gateB{l}")
                fin_dve(v, l)


_OUTS = [("y_prompt", (1, T_P, D)), ("y_sample", (1, T_S, D)), ("new_attn_k", (1, 1, T_P, 2, HD)),
         ("new_attn_v", (1, 1, T_P, 2, HD)), ("new_gla_state", (1, 1, 2, 4, 64, 128)),
         ("new_swa_k", (1, 1, T_P, 2, HD)), ("new_swa_v", (1, 1, T_P, 2, HD)),
         ("new_delta_state", (1, 1, 2, 4, 128, 128))]
_INS = ["x_prompt", "x_sample", "c", "cache_attn_k", "cache_attn_v", "state_gla", "cache_swa_k", "cache_swa_v",
        "state_delta", "c_ctx", "w_mod", "b_mod", "g_pre", "g_post", "w_in_even", "w_out_even", "qnorm_a", "knorm_a",
        "gla_gk_up", "gla_gk_bias", "gla_onorm", "w_in_odd", "w_out_odd", "sink_c", "conv_d", "a_log_d", "dt_bias_d",
        "delta_onorm"]


def kernel(**inputs):
    import numpy as _np
    import concourse.bacc as _bacc
    from concourse import mybir as _mybir
    from concourse.bass_utils import run_bass_kernel_spmd as _run

    nc = _bacc.Bacc("TRN2", target_bir_lowering=False, num_devices=1)
    arrays, args = {}, {}
    for name in _INS:
        a = _np.ascontiguousarray(inputs[name])
        arrays[f"in_{name}"] = a
        args[name] = nc.dram_tensor(f"in_{name}", a.shape, _mybir.dt.from_np(a.dtype), kind="ExternalInput").ap()
    arrays["in_consts"] = CONSTS
    args["consts"] = nc.dram_tensor("in_consts", CONSTS.shape, _mybir.dt.float32, kind="ExternalInput").ap()
    for name, shape in _OUTS:
        args[name] = nc.dram_tensor(f"out_{name}", shape, _mybir.dt.float32, kind="ExternalOutput").ap()
    backbone(nc, **args)
    r = _run(nc, [arrays], core_ids=[0])
    return tuple(r.results[0][f"out_{name}"] for name, _ in _OUTS)
```
